# Optimizing a Trainium2 kernel written in Bass

```python
import math
import jax, jax.numpy as jnp
from jax import lax
import numpy as np

D_MODEL = 1024
BATCH = 1
SEQ = 512
DEPTH = 2

HEAD_DIM = 64
D_MIX = D_MODEL
RWKV_HEADS = (3 * D_MIX) // (8 * HEAD_DIM)
D_RWKV = RWKV_HEADS * HEAD_DIM
ATTN_HEADS = (3 * D_MIX) // (8 * HEAD_DIM)
D_ATTN = ATTN_HEADS * HEAD_DIM
D_CONV = D_MIX - D_RWKV - D_ATTN
DECAY_LORA = 32
ICLR_LORA = 32
GATE_LORA = 64
CONV_WIDTH = 31
DILATED_PATTERNS = ((128, 1), (512, 4), (2048, 16))
ATTN_BLOCK = 128
D_FF = 2816
NORM_EPS = 1e-6
RWKV_GN_EPS = 64e-5
CONV_LN_EPS = 1e-5
D_SHIFT = 3 * D_RWKV + DECAY_LORA + ICLR_LORA + GATE_LORA
D_IN = D_SHIFT + 3 * D_ATTN + 2 * D_CONV


def _alibi_slopes(n):
    def pow2(m):
        start = 2.0 ** (-8.0 / m)
        return [start ** (i + 1) for i in range(m)]
    if math.log2(n).is_integer():
        return pow2(n)
    c = 2 ** int(math.floor(math.log2(n)))
    return pow2(c) + pow2(2 * c)[0::2][: n - c]

def _rms_norm(x, g):
    xf = x.astype(jnp.float32)
    y = xf * lax.rsqrt(jnp.mean(xf * xf, axis=-1, keepdims=True) + NORM_EPS)
    return y.astype(x.dtype) * g

def _head_rms(t, g):
    return t * lax.rsqrt(jnp.mean(t * t, axis=-1, keepdims=True) + NORM_EPS) * g.astype(jnp.float32)

def _swiglu(x, w_gate, w_up, w_down):
    return (jax.nn.silu(x @ w_gate) * (x @ w_up)) @ w_down

def _token_shift(p, mu):
    prev = jnp.pad(p, ((0, 0), (1, 0), (0, 0)))[:, :-1]
    return p + (prev - p) * mu.astype(p.dtype)

def _rwkv7_scan(r, w, k, v, kk, a):
    B, S, H, N = r.shape
    xs = tuple(jnp.moveaxis(t, 1, 0) for t in (r, w, k, v, -kk, kk * a))

    def step(state, inp):
        r_t, w_t, k_t, v_t, a_t, b_t = inp
        sa = jnp.einsum('bhij,bhj->bhi', state, a_t)
        state = (state * w_t[:, :, None, :]
                 + sa[..., None] * b_t[:, :, None, :]
                 + v_t[..., None] * k_t[:, :, None, :])
        y_t = jnp.einsum('bhij,bhj->bhi', state, r_t)
        return state, y_t

    state0 = jnp.zeros((B, H, N, N), jnp.float32)
    _, y = lax.scan(step, state0, xs)
    return jnp.moveaxis(y, 0, 1)

def _rwkv7_mixer(p, w0, w2, a0, a2, g2, k_k, k_a, r_k, ln_w, ln_b):
    B, S, _ = p.shape
    o = 0
    r = p[..., o:o + D_RWKV]; o += D_RWKV
    k = p[..., o:o + D_RWKV]; o += D_RWKV
    v = p[..., o:o + D_RWKV]; o += D_RWKV
    xw = p[..., o:o + DECAY_LORA]; o += DECAY_LORA
    xa = p[..., o:o + ICLR_LORA]; o += ICLR_LORA
    xg = p[..., o:o + GATE_LORA]
    f32 = jnp.float32
    w_log = -jax.nn.softplus(-(w0.astype(f32) + jnp.tanh(xw) @ w2.astype(f32))) - 0.5
    decay = jnp.exp(-jnp.exp(w_log))
    a = jax.nn.sigmoid(a0.astype(f32) + xa @ a2.astype(f32))
    g = jax.nn.sigmoid(xg) @ g2.astype(f32)
    heads = lambda t: t.reshape(B, S, RWKV_HEADS, HEAD_DIM)
    kk = heads(k * k_k.astype(f32))
    kk = kk * lax.rsqrt(jnp.sum(kk * kk, axis=-1, keepdims=True) + 1e-12)
    k = k * (1.0 + (a - 1.0) * k_a.astype(f32))
    rh, kh, vh = heads(r), heads(k), heads(v)
    y = _rwkv7_scan(rh, heads(decay), kh, vh, kk, heads(a))
    mu = jnp.mean(y, axis=-1, keepdims=True)
    var = jnp.mean(jnp.square(y - mu), axis=-1, keepdims=True)
    y = ((y - mu) * lax.rsqrt(var + RWKV_GN_EPS)).reshape(B, S, D_RWKV)
    y = y * ln_w.astype(f32) + ln_b.astype(f32)
    bonus = jnp.sum(rh * kh * r_k.astype(f32), axis=-1, keepdims=True) * vh
    return (y + bonus.reshape(B, S, D_RWKV)) * g

def _dilated_attention(q, k, v, slopes, window, dilation):
    B, S, H, N = q.shape
    n_keys = window // dilation
    L = S // dilation
    nb = -(-L // ATTN_BLOCK)
    Lp = nb * ATTN_BLOCK

    def blocks(t):
        t = t.reshape(B, L, dilation, H, N)
        t = jnp.pad(t, ((0, 0), (0, Lp - L), (0, 0), (0, 0), (0, 0)))
        return t.reshape(B, nb, ATTN_BLOCK, dilation, H, N)

    def band(t):
        prev = jnp.pad(t, ((0, 0), (1, 0), (0, 0), (0, 0), (0, 0), (0, 0)))[:, :-1]
        return jnp.concatenate([prev, t], axis=2)

    qb = blocks(q)
    kb = band(blocks(k))
    vb = band(blocks(v))
    s = jnp.einsum('bnqchd,bnkchd->bnqchk', qb, kb)
    qi = jnp.arange(ATTN_BLOCK)
    ki = jnp.arange(2 * ATTN_BLOCK)
    dist = qi[:, None] + ATTN_BLOCK - ki[None, :]
    key_idx = jnp.arange(nb)[:, None] * ATTN_BLOCK + ki[None, :] - ATTN_BLOCK
    valid = ((dist >= 0) & (dist <= n_keys))[None] & (key_idx >= 0)[:, None, :]
    bias = -slopes[:, None] * (dist * dilation).astype(jnp.float32)[:, None, None, :]
    s = jnp.where(valid[None, :, :, None, None, :], s + bias, -jnp.inf)
    lse = jax.nn.logsumexp(s, axis=-1)
    p = jnp.exp(s - lse[..., None])
    o = jnp.einsum('bnqchk,bnkchd->bnqchd', p, vb)
    o = o.reshape(B, Lp, dilation, H, N)[:, :L].reshape(B, S, H, N)
    lse = lse.reshape(B, Lp, dilation, H)[:, :L].reshape(B, S, H)
    return o, lse

def _attention_mixer(qkv, q_norm, k_norm):
    B, S, _ = qkv.shape
    q = qkv[..., :D_ATTN].reshape(B, S, ATTN_HEADS, HEAD_DIM)
    k = qkv[..., D_ATTN:2 * D_ATTN].reshape(B, S, ATTN_HEADS, HEAD_DIM)
    v = qkv[..., 2 * D_ATTN:].reshape(B, S, ATTN_HEADS, HEAD_DIM)
    q = _head_rms(q, q_norm) * (HEAD_DIM ** -0.5)
    k = _head_rms(k, k_norm)
    slopes = jnp.asarray(_alibi_slopes(ATTN_HEADS), jnp.float32)
    res = [_dilated_attention(q, k, v, slopes, w, d) for (w, d) in DILATED_PATTERNS]
    outs = jnp.stack([r_[0] for r_ in res], axis=0)
    lses = jnp.stack([r_[1] for r_ in res], axis=0)
    alpha = jax.nn.softmax(lses, axis=0)
    out = jnp.sum(alpha[..., None] * outs, axis=0)
    return out.reshape(B, S, D_ATTN)

def _conv_mixer(u, dw_w, dw_b, ln_w, ln_b):
    f32 = jnp.float32
    z = u[..., :D_CONV] * jax.nn.sigmoid(u[..., D_CONV:])
    z = lax.conv_general_dilated(z, dw_w.astype(f32)[:, None, :], window_strides=(1,),
                                 padding=[(CONV_WIDTH - 1, 0)],
                                 dimension_numbers=('NWC', 'WIO', 'NWC'),
                                 feature_group_count=D_CONV) + dw_b.astype(f32)
    mu = jnp.mean(z, axis=-1, keepdims=True)
    var = jnp.mean(jnp.square(z - mu), axis=-1, keepdims=True)
    z = (z - mu) * lax.rsqrt(var + CONV_LN_EPS) * ln_w.astype(f32) + ln_b.astype(f32)
    return jax.nn.silu(z)

def first_inputs(seed: int = 0) -> dict:
    key = jax.random.key(seed)
    ks = iter(jax.random.split(key, 40))
    f32 = jnp.float32
    L = DEPTH

    def normal(shape, scale):
        return jax.random.normal(next(ks), shape, f32) * scale

    def gain(shape):
        return 1.0 + 0.05 * jax.random.normal(next(ks), shape, f32)

    def unif(shape, lo, hi):
        return jax.random.uniform(next(ks), shape, f32, lo, hi)

    return {
        'x': normal((BATCH, SEQ, D_MODEL), 1.0),
        'norm_ffn1': gain((L, D_MODEL)),
        'ffn1_w_gate': normal((L, D_MODEL, D_FF), D_MODEL ** -0.5),
        'ffn1_w_up': normal((L, D_MODEL, D_FF), D_MODEL ** -0.5),
        'ffn1_w_down': normal((L, D_FF, D_MODEL), D_FF ** -0.5),
        'norm_mix': gain((L, D_MODEL)),
        'w_in': normal((L, D_MODEL, D_IN), D_MODEL ** -0.5),
        'shift_mu': unif((L, D_SHIFT), 0.0, 1.0),
        'rwkv_w0': unif((L, D_RWKV), -6.0, 1.0),
        'rwkv_w2': normal((L, DECAY_LORA, D_RWKV), 0.1),
        'rwkv_a0': normal((L, D_RWKV), 0.5),
        'rwkv_a2': normal((L, ICLR_LORA, D_RWKV), 0.1),
        'rwkv_g2': normal((L, GATE_LORA, D_RWKV), GATE_LORA ** -0.5),
        'rwkv_k_k': 0.85 + normal((L, D_RWKV), 0.05),
        'rwkv_k_a': gain((L, D_RWKV)),
        'rwkv_r_k': 0.5 + normal((L, RWKV_HEADS, HEAD_DIM), 0.1),
        'rwkv_ln_w': gain((L, D_RWKV)),
        'rwkv_ln_b': normal((L, D_RWKV), 0.02),
        'attn_q_norm': gain((L, HEAD_DIM)),
        'attn_k_norm': gain((L, HEAD_DIM)),
        'conv_dw_w': normal((L, CONV_WIDTH, D_CONV), CONV_WIDTH ** -0.5),
        'conv_dw_b': normal((L, D_CONV), 0.02),
        'conv_ln_w': gain((L, D_CONV)),
        'conv_ln_b': normal((L, D_CONV), 0.02),
        'w_out': normal((L, D_MIX, D_MODEL), D_MIX ** -0.5),
        'norm_ffn2': gain((L, D_MODEL)),
        'ffn2_w_gate': normal((L, D_MODEL, D_FF), D_MODEL ** -0.5),
        'ffn2_w_up': normal((L, D_MODEL, D_FF), D_MODEL ** -0.5),
        'ffn2_w_down': normal((L, D_FF, D_MODEL), D_FF ** -0.5),
    }

def first_block(x, norm_ffn1, ffn1_w_gate, ffn1_w_up, ffn1_w_down, norm_mix, w_in, shift_mu,
              rwkv_w0, rwkv_w2, rwkv_a0, rwkv_a2, rwkv_g2, rwkv_k_k, rwkv_k_a, rwkv_r_k,
              rwkv_ln_w, rwkv_ln_b, attn_q_norm, attn_k_norm, conv_dw_w, conv_dw_b,
              conv_ln_w, conv_ln_b, w_out, norm_ffn2, ffn2_w_gate, ffn2_w_up, ffn2_w_down):
    for l in range(DEPTH):
        x = x + 0.5 * _swiglu(_rms_norm(x, norm_ffn1[l]), ffn1_w_gate[l], ffn1_w_up[l], ffn1_w_down[l])
        h = _rms_norm(x, norm_mix[l])
        proj = (h @ w_in[l]).astype(jnp.float32)
        p_rwkv = _token_shift(proj[..., :D_SHIFT], shift_mu[l])
        y_rwkv = _rwkv7_mixer(p_rwkv, rwkv_w0[l], rwkv_w2[l], rwkv_a0[l], rwkv_a2[l], rwkv_g2[l],
                              rwkv_k_k[l], rwkv_k_a[l], rwkv_r_k[l], rwkv_ln_w[l], rwkv_ln_b[l])
        y_attn = _attention_mixer(proj[..., D_SHIFT:D_SHIFT + 3 * D_ATTN], attn_q_norm[l], attn_k_norm[l])
        y_conv = _conv_mixer(proj[..., D_SHIFT + 3 * D_ATTN:], conv_dw_w[l], conv_dw_b[l],
                             conv_ln_w[l], conv_ln_b[l])
        mix = jnp.concatenate([y_rwkv, y_attn, y_conv], axis=-1).astype(x.dtype)
        x = x + mix @ w_out[l]
        x = x + 0.5 * _swiglu(_rms_norm(x, norm_ffn2[l]), ffn2_w_gate[l], ffn2_w_up[l], ffn2_w_down[l])
    return x


N_A = DEPTH // 2
N_B = DEPTH - N_A
MEM_LEN = 256
MEM_HEADS = 4
MEM_DH = D_MODEL // (2 * MEM_HEADS)
MEM_WIDTH = MEM_HEADS * MEM_DH
GLA_HEADS = 4
GLA_DV = D_MODEL // (2 * GLA_HEADS)
GLA_DK = GLA_DV // 2
GLA_QK = GLA_HEADS * GLA_DK
GLA_V = GLA_HEADS * GLA_DV
GLA_RANK = 16
GLA_TAU = 16.0
GLA_CHUNK = 64
NSA_HEADS = 8
NSA_GROUPS = 2
NSA_HPG = NSA_HEADS // NSA_GROUPS
NSA_DH = D_MODEL // (2 * NSA_HEADS)
NSA_WIDTH = NSA_HEADS * NSA_DH
KV_WIDTH = NSA_GROUPS * NSA_DH
CMP_BLOCK = 32
CMP_STRIDE = 16
CMP_HIDDEN = 256
SEL_BLOCK = 64
SEL_TOPN = 16
WINDOW = 512
Q_BLOCK = 128
FFN_DIM = ((8 * D_MODEL // 3 + 127) // 128) * 128
CONV_WIDTH_2 = 3
EPS = 1e-6
A_PROJ = 2 * GLA_QK + 2 * GLA_V + GLA_RANK + MEM_WIDTH
B_PROJ = NSA_WIDTH + 3 * NSA_HEADS + MEM_WIDTH
SHARED_KV_PROJ = 6 * KV_WIDTH


F32 = jnp.float32

def rmsnorm(x, g):
    xf = x.astype(F32)
    y = xf * lax.rsqrt(jnp.mean(xf * xf, axis=-1, keepdims=True) + EPS)
    return y.astype(x.dtype) * g

def split_cols(z, widths):
    idx = [int(i) for i in np.cumsum(widths)[:-1]]
    return jnp.split(z, idx, axis=-1)

def masked_softmax(s, mask):
    s = jnp.where(mask, s.astype(F32), -jnp.inf)
    m = jnp.max(s, axis=-1, keepdims=True)
    m = jnp.where(jnp.isfinite(m), m, 0.0)
    e = jnp.exp(s - m)
    return e / jnp.maximum(jnp.sum(e, axis=-1, keepdims=True), 1e-30)

def alibi_slopes(n):
    return jnp.exp2(-8.0 * jnp.arange(1, n + 1, dtype=F32) / n)

def mem_attend(mq, mem_k, mem_v):
    B, T, _ = mq.shape
    qh = mq.reshape(B, T, MEM_HEADS, MEM_DH) * (MEM_DH ** -0.5)
    s = jnp.einsum('bthd,bmhd->bhtm', qh, mem_k)
    p = jax.nn.softmax(s.astype(F32), axis=-1).astype(mem_v.dtype)
    return jnp.einsum('bhtm,bmhd->bthd', p, mem_v).reshape(B, T, MEM_WIDTH)

def gla_chunked(q, k, v, log_a):
    B, T, H, DK = q.shape
    DV = v.shape[-1]
    C = GLA_CHUNK
    NC = T // C

    def chunks(a):
        return a.astype(F32).reshape(B, NC, C, H, a.shape[-1]).transpose(1, 0, 3, 2, 4)

    causal = jnp.tril(jnp.ones((C, C), dtype=bool))[:, :, None]

    def step(S, inp):
        qc, kc, vc, gc = inp
        b = jnp.cumsum(gc, axis=2)
        b_last = b[:, :, -1:, :]
        o_inter = jnp.einsum('bhtd,bhde->bhte', qc * jnp.exp(b), S)
        decay = jnp.exp(jnp.where(causal, b[:, :, :, None, :] - b[:, :, None, :, :], -jnp.inf))
        attn = jnp.einsum('bhtd,bhsd,bhtsd->bhts', qc, kc, decay)
        o = o_inter + jnp.einsum('bhts,bhse->bhte', attn, vc)
        S = jnp.exp(b_last[:, :, 0, :])[..., None] * S + jnp.einsum('bhsd,bhse->bhde', kc * jnp.exp(b_last - b), vc)
        return S, o

    S0 = jnp.zeros((B, H, DK, DV), F32)
    _, o = lax.scan(step, S0, (chunks(q), chunks(k), chunks(v), chunks(log_a)))
    return o.transpose(1, 0, 3, 2, 4).reshape(B, T, H, DV)

def gla_layer_mix(h, mem_k, mem_v, w_in, w_alpha, b_alpha, g_head, w_out):
    B, T, _ = h.shape
    q, k, v, r, alr, mq = split_cols(h @ w_in, [GLA_QK, GLA_QK, GLA_V, GLA_V, GLA_RANK, MEM_WIDTH])
    q = q.reshape(B, T, GLA_HEADS, GLA_DK) * (GLA_DK ** -0.5)
    k = k.reshape(B, T, GLA_HEADS, GLA_DK)
    v = v.reshape(B, T, GLA_HEADS, GLA_DV)
    log_a = jax.nn.log_sigmoid((alr @ w_alpha + b_alpha).astype(F32)) / GLA_TAU
    log_a = log_a.reshape(B, T, GLA_HEADS, GLA_DK)
    o = gla_chunked(q, k, v, log_a).astype(h.dtype)
    o = rmsnorm(o, g_head).reshape(B, T, GLA_V) * jax.nn.silu(r)
    m = mem_attend(mq, mem_k, mem_v)
    return jnp.concatenate([o, m], axis=-1) @ w_out

def compress_blocks(a, pe, w1, w2):
    B, T, G, DH = a.shape
    n_sub = CMP_BLOCK // CMP_STRIDE
    sub = a.reshape(B, T // CMP_STRIDE, CMP_STRIDE, G, DH)
    ncmp = T // CMP_STRIDE - n_sub + 1
    blocks = jnp.concatenate([sub[:, i:i + ncmp] for i in range(n_sub)], axis=2)
    blocks = blocks + pe[:, None, :]
    flat = blocks.transpose(0, 1, 3, 2, 4).reshape(B, ncmp, G, CMP_BLOCK * DH)
    return jax.nn.gelu(flat @ w1) @ w2

def nsa_shared_kv(x, g_kv, w_kv, pe_k, pe_v, w_ck1, w_ck2, w_cv1, w_cv2):
    B, T, _ = x.shape
    kv = (rmsnorm(x, g_kv) @ w_kv).reshape(B, T, 6, NSA_GROUPS, NSA_DH)
    k_c, v_c, k_s, v_s, k_w, v_w = [kv[:, :, i] for i in range(6)]
    return (compress_blocks(k_c, pe_k, w_ck1, w_ck2), compress_blocks(v_c, pe_v, w_cv1, w_cv2),
            k_s, v_s, k_w, v_w)

def selection_overlap(ncmp, ns):
    cs = jnp.arange(ncmp) * CMP_STRIDE
    ss = jnp.arange(ns) * SEL_BLOCK
    ov = jnp.minimum(cs[:, None] + CMP_BLOCK, ss[None, :] + SEL_BLOCK) - jnp.maximum(cs[:, None], ss[None, :])
    return jnp.clip(ov, 0, None).astype(F32) / CMP_BLOCK

def nsa_attend(q, gates, k_cmp, v_cmp, k_slc, v_slc, k_win, v_win):
    B, T, H, DH = q.shape
    G, HPG = NSA_GROUPS, NSA_HPG
    nqb = T // Q_BLOCK
    ncmp = k_cmp.shape[1]
    ns = T // SEL_BLOCK
    n_sel = min(SEL_TOPN, ns)
    slope = alibi_slopes(H).reshape(G, HPG)[None, None, :, :, None]
    cmp_end = jnp.arange(ncmp) * CMP_STRIDE + CMP_BLOCK - 1
    overlap = selection_overlap(ncmp, ns)

    def to_blocks(a):
        return a.reshape(B, ns, SEL_BLOCK, G, DH).transpose(0, 3, 1, 2, 4)

    ks_b, vs_b = to_blocks(k_slc), to_blocks(v_slc)
    pad = ((0, 0), (WINDOW, 0), (0, 0), (0, 0))
    kw_pad, vw_pad = jnp.pad(k_win, pad), jnp.pad(v_win, pad)
    gather = jax.vmap(jax.vmap(lambda blocks, ix: blocks[ix]))
    sel_off = jnp.arange(SEL_BLOCK)
    win_off = jnp.arange(Q_BLOCK + WINDOW)
    blk = jnp.arange(ns)

    def one_block(inp):
        qi, gi, bi = inp
        t = bi * Q_BLOCK + jnp.arange(Q_BLOCK)
        dist_c = (t[:, None] - cmp_end[None, :])
        s = jnp.einsum('bqghd,bngd->bqghn', qi, k_cmp).astype(F32) - slope * dist_c.astype(F32)[None, :, None, None, :]
        p_c = masked_softmax(s, (dist_c >= 0)[None, :, None, None, :])
        o_c = jnp.einsum('bqghn,bngd->bqghd', p_c.astype(v_cmp.dtype), v_cmp)
        cur = t // SEL_BLOCK
        imp = jnp.einsum('bqghn,nj->bqgj', p_c, overlap)
        valid = (blk[None, :] <= cur[:, None])[None, :, None, :]
        forced = ((blk[None, :] == 0) | (blk[None, :] == cur[:, None]) | (blk[None, :] == cur[:, None] - 1))[None, :, None, :]
        imp = jnp.where(forced, jnp.inf, jnp.where(valid, imp, -jnp.inf))
        _, idx = lax.top_k(imp, n_sel)
        idx = idx.transpose(0, 2, 1, 3)
        kg = gather(ks_b, idx).reshape(B, G, Q_BLOCK, n_sel * SEL_BLOCK, DH)
        vg = gather(vs_b, idx).reshape(B, G, Q_BLOCK, n_sel * SEL_BLOCK, DH)
        pos = (idx[..., None] * SEL_BLOCK + sel_off).reshape(B, G, Q_BLOCK, n_sel * SEL_BLOCK)
        dist_s = (t[None, None, :, None] - pos).transpose(0, 2, 1, 3)[:, :, :, None, :]
        s = jnp.einsum('bqghd,bgqsd->bqghs', qi, kg).astype(F32) - slope * dist_s.astype(F32)
        p_s = masked_softmax(s, dist_s >= 0)
        o_s = jnp.einsum('bqghs,bgqsd->bqghd', p_s.astype(vg.dtype), vg)
        start = bi * Q_BLOCK
        kw = lax.dynamic_slice_in_dim(kw_pad, start, Q_BLOCK + WINDOW, axis=1)
        vw = lax.dynamic_slice_in_dim(vw_pad, start, Q_BLOCK + WINDOW, axis=1)
        kpos = start - WINDOW + win_off
        dist_w = t[:, None] - kpos[None, :]
        mask_w = ((dist_w >= 0) & (dist_w < WINDOW) & (kpos >= 0)[None, :])[None, :, None, None, :]
        s = jnp.einsum('bqghd,bkgd->bqghk', qi, kw).astype(F32) - slope * dist_w.astype(F32)[None, :, None, None, :]
        p_w = masked_softmax(s, mask_w)
        o_w = jnp.einsum('bqghk,bkgd->bqghd', p_w.astype(vw.dtype), vw)
        return gi[..., 0:1] * o_c + gi[..., 1:2] * o_s + gi[..., 2:3] * o_w

    qb = q.reshape(B, nqb, Q_BLOCK, G, HPG, DH).transpose(1, 0, 2, 3, 4, 5)
    gb = gates.reshape(B, nqb, Q_BLOCK, G, HPG, 3).transpose(1, 0, 2, 3, 4, 5).astype(q.dtype)
    out = lax.map(one_block, (qb, gb, jnp.arange(nqb)))
    return out.transpose(1, 0, 2, 3, 4, 5).reshape(B, T, H * DH)

def nsa_layer_mix(h, shared, mem_k, mem_v, w_in, w_out):
    B, T, _ = h.shape
    q, gl, mq = split_cols(h @ w_in, [NSA_WIDTH, 3 * NSA_HEADS, MEM_WIDTH])
    q = q.reshape(B, T, NSA_HEADS, NSA_DH) * (NSA_DH ** -0.5)
    gates = jax.nn.sigmoid(gl.reshape(B, T, NSA_HEADS, 3))
    o = nsa_attend(q, gates, *shared)
    m = mem_attend(mq, mem_k, mem_v)
    return jnp.concatenate([o, m], axis=-1) @ w_out

def conv_ffn(h, w_up, conv_w, conv_b, w_down):
    T = h.shape[1]
    a, b = jnp.split(h @ w_up, 2, axis=-1)
    a_pad = jnp.pad(a, ((0, 0), (CONV_WIDTH_2 - 1, 0), (0, 0)))
    a = sum(a_pad[:, j:j + T] * conv_w[j] for j in range(CONV_WIDTH_2)) + conv_b
    return (jax.nn.silu(a) * b) @ w_down

def second_inputs(seed: int = 0) -> dict:
    key = jax.random.key(seed)
    ks = jax.random.split(key, 26)

    def nrm(k, shape, scale):
        return jax.random.normal(k, shape, F32) * scale

    def gain(k, shape):
        return 1.0 + 0.02 * jax.random.normal(k, shape, F32)

    D = D_MODEL
    return {
        'x': nrm(ks[0], (BATCH, SEQ, D), 1.0),
        'mem': nrm(ks[1], (BATCH, MEM_LEN, D), 1.0),
        'g_mix': gain(ks[2], (DEPTH, D)),
        'g_ffn': gain(ks[3], (DEPTH, D)),
        'g_mem': gain(ks[4], (DEPTH, D)),
        'w_mem_kv': nrm(ks[5], (DEPTH, D, 2 * MEM_WIDTH), D ** -0.5),
        'w_up': nrm(ks[6], (DEPTH, D, 2 * FFN_DIM), D ** -0.5),
        'conv_w': nrm(ks[7], (DEPTH, CONV_WIDTH_2, FFN_DIM), CONV_WIDTH_2 ** -0.5),
        'conv_b': nrm(ks[8], (DEPTH, FFN_DIM), 0.01),
        'w_down': nrm(ks[9], (DEPTH, FFN_DIM, D), FFN_DIM ** -0.5),
        'a_w_in': nrm(ks[10], (N_A, D, A_PROJ), D ** -0.5),
        'a_w_alpha': nrm(ks[11], (N_A, GLA_RANK, GLA_QK), GLA_RANK ** -0.5),
        'a_b_alpha': nrm(ks[12], (N_A, GLA_QK), 0.01),
        'a_g_head': gain(ks[13], (N_A, GLA_DV)),
        'a_w_out': nrm(ks[14], (N_A, GLA_V + MEM_WIDTH, D), (GLA_V + MEM_WIDTH) ** -0.5),
        'g_kv': gain(ks[15], (D,)),
        'w_kv': nrm(ks[16], (D, SHARED_KV_PROJ), D ** -0.5),
        'pe_k': nrm(ks[17], (CMP_BLOCK, NSA_DH), 0.1),
        'pe_v': nrm(ks[18], (CMP_BLOCK, NSA_DH), 0.1),
        'w_ck1': nrm(ks[19], (CMP_BLOCK * NSA_DH, CMP_HIDDEN), (CMP_BLOCK * NSA_DH) ** -0.5),
        'w_ck2': nrm(ks[20], (CMP_HIDDEN, NSA_DH), CMP_HIDDEN ** -0.5),
        'w_cv1': nrm(ks[21], (CMP_BLOCK * NSA_DH, CMP_HIDDEN), (CMP_BLOCK * NSA_DH) ** -0.5),
        'w_cv2': nrm(ks[22], (CMP_HIDDEN, NSA_DH), CMP_HIDDEN ** -0.5),
        'b_w_in': nrm(ks[23], (N_B, D, B_PROJ), D ** -0.5),
        'b_w_out': nrm(ks[24], (N_B, NSA_WIDTH + MEM_WIDTH, D), (NSA_WIDTH + MEM_WIDTH) ** -0.5),
        'g_final': gain(ks[25], (D,)),
    }

def second_block(x, mem, g_mix, g_ffn, g_mem, w_mem_kv, w_up, conv_w, conv_b, w_down,
              a_w_in, a_w_alpha, a_b_alpha, a_g_head, a_w_out,
              g_kv, w_kv, pe_k, pe_v, w_ck1, w_ck2, w_cv1, w_cv2,
              b_w_in, b_w_out, g_final):
    B, M, _ = mem.shape
    shared = None
    for l in range(DEPTH):
        if l == N_A:
            shared = nsa_shared_kv(x, g_kv, w_kv, pe_k, pe_v, w_ck1, w_ck2, w_cv1, w_cv2)
        mkv = (rmsnorm(mem, g_mem[l]) @ w_mem_kv[l]).reshape(B, M, 2, MEM_HEADS, MEM_DH)
        mem_k, mem_v = mkv[:, :, 0], mkv[:, :, 1]
        h = rmsnorm(x, g_mix[l])
        if l < N_A:
            x = x + gla_layer_mix(h, mem_k, mem_v, a_w_in[l], a_w_alpha[l], a_b_alpha[l], a_g_head[l], a_w_out[l])
        else:
            j = l - N_A
            x = x + nsa_layer_mix(h, shared, mem_k, mem_v, b_w_in[j], b_w_out[j])
        x = x + conv_ffn(rmsnorm(x, g_ffn[l]), w_up[l], conv_w[l], conv_b[l], w_down[l])
    return rmsnorm(x, g_final)


def setup_inputs(seed=0):
    out = dict(first_inputs(seed))
    for name, value in second_inputs(seed + 1).items():
        if name != "x":
            out[name + "_2"] = value
    return out


def reference(
    x, norm_ffn1, ffn1_w_gate, ffn1_w_up, ffn1_w_down, norm_mix, w_in, shift_mu, rwkv_w0,
    rwkv_w2, rwkv_a0, rwkv_a2, rwkv_g2, rwkv_k_k, rwkv_k_a, rwkv_r_k, rwkv_ln_w, rwkv_ln_b,
    attn_q_norm, attn_k_norm, conv_dw_w, conv_dw_b, conv_ln_w, conv_ln_b, w_out, norm_ffn2,
    ffn2_w_gate, ffn2_w_up, ffn2_w_down, mem_2, g_mix_2, g_ffn_2, g_mem_2, w_mem_kv_2, w_up_2,
    conv_w_2, conv_b_2, w_down_2, a_w_in_2, a_w_alpha_2, a_b_alpha_2, a_g_head_2, a_w_out_2,
    g_kv_2, w_kv_2, pe_k_2, pe_v_2, w_ck1_2, w_ck2_2, w_cv1_2, w_cv2_2, b_w_in_2, b_w_out_2,
    g_final_2,
):
    x = first_block(
        x, norm_ffn1, ffn1_w_gate, ffn1_w_up, ffn1_w_down, norm_mix, w_in, shift_mu, rwkv_w0,
        rwkv_w2, rwkv_a0, rwkv_a2, rwkv_g2, rwkv_k_k, rwkv_k_a, rwkv_r_k, rwkv_ln_w, rwkv_ln_b,
        attn_q_norm, attn_k_norm, conv_dw_w, conv_dw_b, conv_ln_w, conv_ln_b, w_out, norm_ffn2,
        ffn2_w_gate, ffn2_w_up, ffn2_w_down,
    )
    return second_block(
        x, mem_2, g_mix_2, g_ffn_2, g_mem_2, w_mem_kv_2, w_up_2, conv_w_2, conv_b_2, w_down_2,
        a_w_in_2, a_w_alpha_2, a_b_alpha_2, a_g_head_2, a_w_out_2, g_kv_2, w_kv_2, pe_k_2,
        pe_v_2, w_ck1_2, w_ck2_2, w_cv1_2, w_cv2_2, b_w_in_2, b_w_out_2, g_final_2,
    )


_drawn_inputs = setup_inputs


def setup_inputs(seed=0):
    import zlib

    import numpy as np

    out = dict(_drawn_inputs(seed))
    spreads = {}
    factors = {'rwkv_w2': 3.643,
     'rwkv_ln_b': 5.383,
     'attn_q_norm': 4.761,
     'attn_k_norm': 4.672,
     'conv_dw_b': 2.773,
     'conv_ln_b': 5.671,
     'g_mix_2': 4.487,
     'g_ffn_2': 3.788,
     'g_mem_2': 8.0,
     'conv_b_2': 8.0,
     'a_b_alpha_2': 8.0,
     'a_g_head_2': 8.0,
     'g_kv_2': 8.0,
     'pe_k_2': 8.0,
     'pe_v_2': 34.752,
     'g_final_2': 7.939}
    for name, (base, spread) in spreads.items():
        noise = np.random.default_rng([zlib.crc32(name.encode()), seed]).standard_normal(out[name].shape)
        drawn = base * np.exp(spread * noise) if base else spread * noise
        out[name] = __import__('jax').numpy.asarray(drawn.astype(out[name].dtype))
    for name, factor in factors.items():
        out[name] = (out[name] * factor).astype(out[name].dtype)
    return out
```

```python
import math
from contextlib import ExitStack, contextmanager

import numpy as np

import concourse.bass as bass
from concourse import mybir

F32 = mybir.dt.float32
ALU = mybir.AluOpType
ACT = mybir.ActivationFunctionType
AX = mybir.AxisListType

P = 128
D = 1024
T = 512
NT = T // P
KD = D // P
FF = 2816
KF = FF // P
HD = 64
MEM_T = 256
D_IN = 2944
M_IN = D_IN // P
RW = 3
AT = 3
CV = 2
TAPS = 31
CH = 64
NCH = T // CH
GC = 32
NGC = T // GC
NCMP = 31
NEG = -1e30

def columns(widths):
    at, out = 0, {}
    for name, n in widths:
        out[name] = at
        at += n
    return out, at


PC1, NP1 = columns([
    ("norm_ffn1", KD), ("norm_mix", KD), ("norm_ffn2", KD), ("mu", 10), ("w0", RW), ("a0", RW),
    ("k_k", RW), ("k_a", RW), ("r_k", RW), ("ln_w", RW), ("ln_b", RW), ("q_norm", 1), ("k_norm", 1),
    ("dw", TAPS * CV), ("dw_b", CV), ("cln_w", CV), ("cln_b", CV), ("lora", 3 * P)])
PC2, NP2 = columns([
    ("g_mix", 2 * KD), ("g_ffn", 2 * KD), ("g_mem", 2 * KD), ("cw", 2 * 3 * KF), ("cb", 2 * KF),
    ("b_alpha", 2), ("g_head", 1), ("g_kv", KD), ("g_final", KD), ("pe_k", 32), ("pe_v", 32)])
CC, NCC = columns([
    ("ident", P), ("ones", P), ("head", P), ("m16", P), ("m32", P), ("m64", P), ("m16T", P),
    ("strictT", P), ("inclT", P), ("incl32T", P), ("dist", T), ("log_count", T), ("causal", T),
    ("start64", T), ("start32", T), ("cmp_dist", NT * NCMP), ("cmp_mask", NT * NCMP), ("zero", T),
    ("eps6", 1), ("eps12", 1), ("eps_gn", 1), ("eps5", 1), ("one", 1)])


def constants():
    i = np.arange(P)
    same = lambda n: (i[:, None] // n == i[None, :] // n).astype(np.float32)
    below = (i[:, None] > i[None, :]).astype(np.float32)
    upto = (i[:, None] <= i[None, :]).astype(np.float32)
    dist = (i[:, None] + (T - P) - np.arange(T)[None, :]).astype(np.int64)
    count = (dist <= 128).astype(int) + (dist % 4 == 0) + (dist % 16 == 0)
    count = np.where(dist >= 0, count, 0)
    t = np.arange(T)
    cmp_dist = np.concatenate([(P * b + i)[:, None] - (16 * np.arange(NCMP) + 31)[None, :] for b in range(NT)], axis=1)
    row = lambda v: np.broadcast_to(np.asarray(v, np.float32)[None, :], (P, len(v)))
    col = lambda v: np.full((P, 1), v, np.float32)
    parts = [
        np.eye(P), np.ones((P, P)), same(HD), below * same(16), below * (same(32) - same(16)),
        below * (same(64) - same(32)), (below * same(16)).T, (below * same(64)).T, upto * same(64),
        upto * same(32), dist, np.where(count > 0, 8.0 * np.log(np.maximum(count, 1)), NEG),
        np.where(dist >= 0, 0.0, NEG), row(t % CH != 0), row(t % GC != 0), cmp_dist,
        np.where(cmp_dist >= 0, 0.0, NEG), np.zeros((P, T)), col(1e-6), col(1e-12), col(64e-5), col(1e-5), col(1.0)]
    return np.concatenate([np.asarray(p, np.float32) for p in parts], axis=1)


def dilated_slopes():
    pow2 = lambda m: [(2.0 ** (-8.0 / m)) ** (i + 1) for i in range(m)]
    return pow2(4) + pow2(8)[0::2][:2]


NSA_SLOPES = [2.0 ** (-(h + 1)) for h in range(8)]


class Phases:

    FIRST, SIZE = 100, 40

    def __init__(self, nc):
        self.nc, self.n = nc, 0

    @contextmanager
    def phase(self, *names):
        nc = self.nc
        own = self.FIRST + self.SIZE * (self.n % 2)
        other = self.FIRST + self.SIZE * ((self.n + 1) % 2)
        self.n += 1
        assert len(names) <= self.SIZE
        with ExitStack() as ctx:
            sems = [ctx.enter_context(nc.semaphore(f"{n}_{self.n}", num=own + i)) for i, n in enumerate(names)]
            block = ctx.enter_context(nc.Block())

            @block.gpsimd
            def _(pool):
                pool.sem_clear(range(other, other + self.SIZE))

            yield (block, *sems)


def repeat(eng, total, unroll, body):
    whole = total // unroll
    if whole >= 2:
        with eng.Fori(0, whole) as n:
            for u in range(unroll):
                body(n * unroll + u, n, u)
    else:
        whole = 0
    for i in range(whole * unroll, total):
        body(i, i // unroll, i % unroll)


def uses(n, per, k, slots):
    assert per % slots == 0
    return n * (per // slots) + k // slots + 1


def chunk(ap, i):
    if isinstance(i, int):
        return ap[:, i, :]
    return ap[:, bass.ds(i, 1), :].rearrange("p a t -> p (a t)")


def column(ap, i):
    return ap[:, i:i + 1] if isinstance(i, int) else ap[:, bass.ds(i, 1)]


class Core:

    def __init__(self, nc, ctx, dram):
        self.nc, self.dram, self.phases = nc, dram, Phases(nc)
        sb = lambda name, shape: ctx.enter_context(nc.sbuf_tensor(name, shape, F32))
        self.x = sb("x_res", [P, KD, T])
        self.h = sb("h_norm", [P, KD, T])
        self.mix = sb("mix", [P, KD, T])
        self.big = sb("big", [P, M_IN * (T + 1)])
        self.ring = sb("ring", [P, 4, 11 * P])
        self.arena = sb("arena", [P, 34 * T])
        self.const = sb("const", [P, NCC])
        self.par1 = sb("par1", [P, NP1])
        self.par2 = sb("par2", [P, NP2])
        self.small = sb("small", [P, 400 + NT * 24])
        self.banks = [ctx.enter_context(nc.psum_tensor(f"bank{i}", [P, T], F32)) for i in range(8)]
        self.proj = self.big[:, :].rearrange("p (m t) -> p m t", t=T + 1)
        self.hid = self.big[:, 0:KF * T].rearrange("p (m t) -> p m t", t=T)

    def c(self, name, n=1, rows=P, at=0):
        a = CC[name] + at
        return self.const[0:rows, a:a + n]

    def units(self, *where):
        mem, first, n = where
        flat = {"arena": self.arena[:, :], "big": self.big[:, :],
                "ring": self.ring[:, :, :].rearrange("p s c -> p (s c)"),
                "h": self.h[:, :, :].rearrange("p s c -> p (s c)")}[mem]
        return flat[:, first * T:(first + n) * T].rearrange("p (n t) -> p n t", t=T)

    def load_start(self):
        dram = self.dram
        with self.phases.phase("loaded") as (block, loaded):
            @block.sync
            def _(sp):
                sp.dma_start(self.const[:, :], dram["consts"]).then_inc(loaded, 16)
                sp.dma_start(self.par2[:, :], dram["par2"]).then_inc(loaded, 16)
                sp.dma_start(self.x[:, :, :], dram["x"]).then_inc(loaded, 16)
                sp.wait_ge(loaded, 48)

    def load_layer(self, layer):
        with self.phases.phase("loaded") as (block, loaded):
            @block.sync
            def _(sp):
                src = self.dram["par1"][bass.ds(layer, 1), :, :].rearrange("a p c -> p (a c)")
                sp.dma_start(self.par1[:, :], src).then_inc(loaded, 16)
                sp.wait_ge(loaded, 16)

    def norm(self, x, h, gain, n=T, scratch=0):
        nc, banks = self.nc, self.banks
        sq = self.units("arena", scratch, 2)
        logm, rstd = (self.units("arena", scratch + i, 1)[:, 0, 0:n] for i in (2, 3))
        names = ("squared", "summed", "logged", "rstd_ready", "normed")
        with self.phases.phase(*names) as (block, squared, summed, logged, rstd_ready, normed):
            @block.scalar
            def _(act):
                for k in range(KD):
                    if k >= 2:
                        act.wait_ge(summed, k - 1)
                    nc.scalar.activation(sq[:, k % 2, 0:n], x[:, k, 0:n], ACT.Square).then_inc(squared, 1)
                act.wait_ge(summed, KD)
                nc.scalar.activation(logm, banks[0][:, 0:n], ACT.Ln, bias=self.c("eps6"), scale=1.0 / D).then_inc(logged, 1)
                act.wait_ge(logged, 1)
                nc.scalar.activation(rstd, logm, ACT.Exp, scale=-0.5).then_inc(rstd_ready, 1)

            @block.tensor
            def _(pe):
                for k in range(KD):
                    pe.wait_ge(squared, k + 1)
                    nc.tensor.matmul(banks[0][:, 0:n], self.c("ones", P), sq[:, k % 2, 0:n],
                                     start=(k == 0), stop=(k == KD - 1)).then_inc(summed, 1)

            @block.vector
            def _(dve):
                dve.wait_ge(rstd_ready, 1)
                for k in range(KD):
                    nc.vector.scalar_tensor_tensor(h[:, k, 0:n], x[:, k, 0:n], gain[:, k:k + 1], rstd,
                                                   ALU.mult, ALU.mult).then_inc(normed, 1)

    def weight_tile(self, name, first, i, kc):
        at = i + first
        src = self.dram[name][at:at + 1, :, :] if isinstance(at, int) else self.dram[name][bass.ds(at, 1), :, :]
        return src.rearrange("a p c -> p (a c)")

    def linear(self, name, first, kc, m, src, finish, n=T, halves=1, gather=None):
        nc, banks, ring = self.nc, self.banks, self.ring
        R = 4
        names = [f"tile_in_slot{r}" for r in range(R)]
        with self.phases.phase("tile_used", "product", "bank_free", *names) as (
                block, tile_used, product, bank_free, *tile_in_slot):
            @block.sync
            def _(sp):
                def body(i, n_, u):
                    for s in range(halves):
                        sp.wait_ge(tile_used, i * halves + s + 1)
                        sp.dma_start(ring[:, (u * halves + s) % R, 0:kc * P],
                                     self.weight_tile(name, first, i * halves + s, kc)
                                     ).then_inc(tile_in_slot[(u * halves + s) % R], 16)
                repeat(sp, m, 4, body)

            @block.tensor
            def _(pe):
                pe.sem_inc(tile_used, R)

                def body(i, n_, u):
                    pe.wait_ge(bank_free, i + 1)
                    for s in range(halves):
                        pe.wait_ge(tile_in_slot[(u * halves + s) % R], uses(n_, 4 * halves, u * halves + s, R) * 16)
                        for k in range(kc):
                            mm = nc.tensor.matmul(banks[u % 2][:, 0:n], ring[:, (u * halves + s) % R, k * P:(k + 1) * P],
                                                  src[:, s * kc + k, 0:n], start=(s == 0 and k == 0),
                                                  stop=(s == halves - 1 and k == kc - 1))
                        if s < halves - 1:
                            mm.then_inc(tile_used, 1)
                    mm.then_inc(product, 1)
                    pe.wait_ge(product, i + 1)
                    pe.sem_inc(tile_used, 1)
                repeat(pe, m, 4, body)

            @block.vector
            def _(dve):
                dve.sem_inc(bank_free, 2)

                def body(i, n_, u):
                    dve.wait_ge(product, i + 1)
                    finish(banks[u % 2][:, 0:n], i).then_inc(bank_free, 1)
                repeat(dve, m, 4, body)

    def project(self, name, first, kc, m, src, dst, n=T):
        self.linear(name, first, kc, m, src,
                    lambda bank, i: self.nc.vector.tensor_copy(chunk(dst[:, :, 0:n], i), bank), n)

    def add_to_residual(self, name, first, kc, src, factor, halves=1):
        self.linear(name, first, kc, KD, src,
                    lambda bank, i: self.nc.vector.scalar_tensor_tensor(
                        chunk(self.x, i), bank, float(factor), chunk(self.x, i), ALU.mult, ALU.add), T, halves)

    def gated(self, name, first, taps=None, tap_bias=None):
        nc, banks, ring, hid = self.nc, self.banks, self.ring, self.hid
        R = 4
        act_out = self.arena[:, 0:2 * T].rearrange("p (s t) -> p s t", s=2)
        conv = self.arena[:, 2 * T:4 * T].rearrange("p (s t) -> p s t", s=2)
        raw = self.arena[:, 4 * T:6 * T + 4].rearrange("p (s t) -> p s t", s=2)
        names = ["tile_used", "products", "banks_free", "activated", "convolved", "chain"]
        names += [f"tile_in_slot{r}" for r in range(R)]
        with self.phases.phase(*names) as (block, tile_used, products, banks_free, activated, convolved, chain, *tile_in_slot):
            @block.sync
            def _(sp):
                def body(i, n_, u):
                    for s in range(2):
                        sp.wait_ge(tile_used, i + 1)
                        sp.dma_start(ring[:, (2 * u + s) % R, 0:KD * P],
                                     self.weight_tile(name, first, 2 * i + s, KD)
                                     ).then_inc(tile_in_slot[2 * u + s], 16)
                repeat(sp, KF, 2, body)

            @block.tensor
            def _(pe):
                pe.sem_inc(tile_used, 2)

                def body(i, n_, u):
                    pe.wait_ge(banks_free, i + 1)
                    for s in range(2):
                        pe.wait_ge(tile_in_slot[2 * u + s], uses(n_, 4, 2 * u + s, R) * 16)
                        for k in range(KD):
                            mm = nc.tensor.matmul(banks[2 * u + s][:, :], ring[:, (2 * u + s) % R, k * P:(k + 1) * P],
                                                  self.h[:, k, :], start=(k == 0), stop=(k == KD - 1))
                    mm.then_inc(products, 1)
                    pe.wait_ge(products, i + 1)
                    pe.sem_inc(tile_used, 1)
                repeat(pe, KF, 2, body)

            @block.scalar
            def _(act):
                def body(i, n_, u):
                    if taps is None:
                        act.wait_ge(products, i + 1)
                        nc.scalar.activation(act_out[:, u, :], banks[2 * u][:, :], ACT.Silu).then_inc(activated, 1)
                    else:
                        act.wait_ge(convolved, i + 1)
                        nc.scalar.activation(act_out[:, u, :], conv[:, u, :], ACT.Silu,
                                             bias=column(tap_bias, i)).then_inc(activated, 1)
                repeat(act, KF, 2, body)

            @block.vector
            def _(dve):
                dve.sem_inc(banks_free, 2)
                if taps is not None:
                    nc.vector.memset(raw[:, :, 0:2], 0.0).then_inc(chain, 1)

                def body(i, n_, u):
                    if taps is not None:
                        dve.wait_ge(products, i + 1)
                        nc.vector.tensor_copy(raw[:, u, 2:T + 2], banks[2 * u][:, :]).then_inc(chain, 1)
                        dve.wait_ge(chain, 3 * i + 2)
                        nc.vector.tensor_scalar(conv[:, u, :], raw[:, u, 0:T], column(taps[0], i), None,
                                                ALU.mult).then_inc(chain, 1)
                        dve.wait_ge(chain, 3 * i + 3)
                        nc.vector.scalar_tensor_tensor(conv[:, u, :], raw[:, u, 1:T + 1], column(taps[1], i),
                                                       conv[:, u, :], ALU.mult, ALU.add).then_inc(chain, 1)
                        dve.wait_ge(chain, 3 * i + 4)
                        nc.vector.scalar_tensor_tensor(conv[:, u, :], raw[:, u, 2:T + 2], column(taps[2], i),
                                                       conv[:, u, :], ALU.mult, ALU.add).then_inc(convolved, 1)
                    dve.wait_ge(activated, i + 1)
                    nc.vector.tensor_tensor(chunk(hid, i), act_out[:, u, :], banks[2 * u + 1][:, :],
                                            ALU.mult).then_inc(banks_free, 1)
                repeat(dve, KF, 2, body)

    def ffn(self, gain, gate_up, gu_first, down, down_first, factor, taps=None, tap_bias=None):
        self.norm(self.x, self.h, gain)
        self.gated(gate_up, gu_first, taps, tap_bias)
        self.add_to_residual(down, down_first, KF // 2, self.hid, factor, halves=2)

    def transposes(self, groups):
        nc, banks = self.nc, self.banks
        with self.phases.phase("turned", "copied_a", "copied_v") as (block, turned, copied_a, copied_v):
            def shape(g):
                blocks, out = groups[g]
                rows, cols = out.shape[0], out.shape[2]
                return banks[g % 4][0:rows, 0:len(blocks) * cols], rows, cols

            @block.tensor
            def _(pe):
                for g, (blocks, out) in enumerate(groups):
                    if g >= 4:
                        pe.wait_ge(copied_v if g % 2 else copied_a, (g - 4) // 2 + 1)
                    bank, rows, cols = shape(g)
                    for j, b in enumerate(blocks):
                        t = nc.tensor.transpose(bank[:, j * cols:(j + 1) * cols], b, self.c("ident", cols, cols))
                    t.then_inc(turned, 1)

            @block.scalar
            def _(act):
                for g in range(0, len(groups), 2):
                    act.wait_ge(turned, g + 1)
                    bank, rows, cols = shape(g)
                    nc.scalar.activation(groups[g][1], bank.rearrange("p (n c) -> p n c", c=cols),
                                         ACT.Copy).then_inc(copied_a, 1)

            @block.vector
            def _(dve):
                for g in range(1, len(groups), 2):
                    dve.wait_ge(turned, g + 1)
                    bank, rows, cols = shape(g)
                    nc.vector.tensor_copy(groups[g][1], bank.rearrange("p (n c) -> p n c", c=cols)).then_inc(copied_v, 1)

    def to_tokens(self, src_chunks, dst):
        nt = src_chunks[0].shape[1] // P
        return [([s[:, i * P:(i + 1) * P] for i in range(nt)], dst[:, :, c * P:(c + 1) * P])
                for c, s in enumerate(src_chunks)]

    def to_features(self, src, dst_chunks, first=0):
        return [([src[:, i, (first + c) * P:(first + c + 1) * P] for i in range(NT)],
                 d.rearrange("p (n t) -> p n t", t=P)) for c, d in enumerate(dst_chunks)]

    def head_norm(self, items, div, eps):
        nc, banks = self.nc, self.banks
        n = len(items)
        sq = self.units("ring", 0, 2)
        lg = self.units("ring", 2, 2)
        rs = self.units("ring", 4, 2)
        with self.phases.phase("squared", "summed", "logged", "rstd_ready", "normed") as (
                block, squared, summed, logged, rstd_ready, normed):
            @block.scalar
            def _(act):
                for k in range(n + 1):
                    if k < n:
                        if k >= 2:
                            act.wait_ge(summed, k - 1)
                        nc.scalar.activation(sq[:, k % 2, :], items[k][0], ACT.Square,
                                             scale=items[k][3]).then_inc(squared, 1)
                    if k >= 1:
                        j = k - 1
                        act.wait_ge(summed, j + 1)
                        if j >= 2:
                            act.wait_ge(rstd_ready, j - 1)
                        nc.scalar.activation(lg[:, j % 2, :], banks[j % 2][:, :], ACT.Ln, bias=self.c(eps),
                                             scale=1.0 / div).then_inc(logged, 1)
                        act.wait_ge(logged, j + 1)
                        if j >= 2:
                            act.wait_ge(normed, j - 1)
                        nc.scalar.activation(rs[:, j % 2, :], lg[:, j % 2, :], ACT.Exp, scale=-0.5).then_inc(rstd_ready, 1)

            @block.tensor
            def _(pe):
                for k in range(n):
                    pe.wait_ge(squared, k + 1)
                    if k >= 2:
                        pe.wait_ge(logged, k - 1)
                    nc.tensor.matmul(banks[k % 2][:, :], self.c("head", P), sq[:, k % 2, :],
                                     start=True, stop=True).then_inc(summed, 1)

            @block.vector
            def _(dve):
                for k, (src, gain, dst, _) in enumerate(items):
                    dve.wait_ge(rstd_ready, k + 1)
                    nc.vector.scalar_tensor_tensor(dst, src, gain, rs[:, k % 2, :], ALU.mult, ALU.mult).then_inc(normed, 1)

    def attention(self, tiles, scale):
        nc, banks = self.nc, self.banks
        n = len(tiles)
        S = self.units("ring", 0, 2)
        E = self.units("ring", 2, 2)
        ET = self.units("ring", 4, 2)
        top, ntop, den, rec = (self.small[:, i * 100:i * 100 + 100] for i in range(4))
        NEG_ROW = -1e20
        names = ("scored", "biased", "top_ready", "exped", "turned", "turned_copied", "weighed", "chain", "out_done")
        assert n <= 100
        keys = [t["k"].shape[1] for t in tiles]
        parts = [[(j * P, min(P, m - j * P)) for j in range(-(-m // P))] for m in keys]
        with self.phases.phase(*names) as (block, scored, biased, top_ready, exped, turned, turned_copied, weighed, chain, out_done):
            @block.tensor
            def _(pe):
                for s in range(n + 2):
                    if s < n:
                        if s >= 2:
                            pe.wait_ge(biased, s - 1)
                        nc.tensor.matmul(banks[s % 2][:, 0:keys[s]], tiles[s]["q"], tiles[s]["k"],
                                         start=True, stop=True).then_inc(scored, 1)
                    if 1 <= s <= n:
                        j = s - 1
                        pe.wait_ge(exped, j + 1)
                        if j >= 2:
                            pe.wait_ge(turned_copied, j - 1)
                        for a, w in parts[j]:
                            mm = nc.tensor.transpose(banks[2 + j % 2][0:w, a:a + P], E[:, j % 2, a:a + w], self.c("ident", P))
                        mm.then_inc(turned, 1)
                    if s >= 2:
                        j = s - 2
                        pe.wait_ge(turned_copied, j + 1)
                        if j >= 2:
                            pe.wait_ge(out_done, j - 1)
                        dv = tiles[j]["out"].shape[1]
                        for i, (a, w) in enumerate(parts[j]):
                            mm = nc.tensor.matmul(banks[4 + j % 2][:, 0:dv], ET[0:w, j % 2, a:a + P], tiles[j]["v"][i],
                                                  start=(i == 0), stop=(i == len(parts[j]) - 1))
                        mm.then_inc(weighed, 1)

            @block.scalar
            def _(act):
                for s in range(n + 1):
                    if s < n:
                        act.wait_ge(top_ready, s + 1)
                        if s >= 2:
                            act.wait_ge(turned, s - 1)
                        nc.scalar.activation(E[:, s % 2, 0:keys[s]], S[:, s % 2, 0:keys[s]], ACT.Exp,
                                             bias=ntop[:, s:s + 1], accum_out=den[:, s:s + 1]).then_inc(exped, 1)
                    if s >= 1:
                        j = s - 1
                        act.wait_ge(turned, j + 1)
                        if j >= 2:
                            act.wait_ge(weighed, j - 1)
                        w = min(P, keys[j])
                        m = len(parts[j]) * P
                        nc.scalar.activation(ET[0:w, j % 2, 0:m], banks[2 + j % 2][0:w, 0:m], ACT.Copy).then_inc(turned_copied, 1)

            @block.vector
            def _(dve):
                links = 0
                for s in range(n + 2):
                    if s < n:
                        dve.wait_ge(scored, s + 1)
                        if s >= 2:
                            dve.wait_ge(exped, s - 1)
                        nc.vector.tensor_tensor_reduce(
                            out=S[:, s % 2, 0:keys[s]], in0=banks[s % 2][:, 0:keys[s]], in1=tiles[s]["bias"],
                            scale=scale, scalar=NEG_ROW, op0=ALU.add, op1=ALU.max,
                            accum_out=top[:, s:s + 1]).then_inc(biased, 1)
                        dve.wait_ge(biased, s + 1)
                        nc.vector.tensor_scalar(ntop[:, s:s + 1], top[:, s:s + 1], -1.0, None, ALU.mult).then_inc(top_ready, 1)
                    if s >= 2:
                        j = s - 2
                        t = tiles[j]
                        dve.wait_ge(weighed, j + 1)
                        nc.vector.tensor_scalar(rec[:, j:j + 1], den[:, j:j + 1], 1e-30, None, ALU.max).then_inc(chain, 1)
                        links += 1
                        dve.wait_ge(chain, links)
                        nc.vector.reciprocal(rec[:, j:j + 1], rec[:, j:j + 1]).then_inc(chain, 1)
                        links += 1
                        dve.wait_ge(chain, links)
                        if t.get("gate") is not None:
                            nc.vector.tensor_tensor(rec[:, j:j + 1], rec[:, j:j + 1], t["gate"], ALU.mult).then_inc(chain, 1)
                            links += 1
                            dve.wait_ge(chain, links)
                        dv = t["out"].shape[1]
                        if t.get("add"):
                            if t["after"] is not None:
                                dve.wait_ge(out_done, t["after"] + 1)
                            nc.vector.scalar_tensor_tensor(t["out"], banks[4 + j % 2][:, 0:dv], rec[:, j:j + 1], t["out"],
                                                           ALU.mult, ALU.add).then_inc(out_done, 1)
                        else:
                            nc.vector.tensor_scalar(t["out"], banks[4 + j % 2][:, 0:dv], rec[:, j:j + 1], None,
                                                    ALU.mult).then_inc(out_done, 1)

    def pause(self):
        with self.phases.phase("unused"):
            pass

    def vector_phase(self, work):
        with self.phases.phase("step") as (block, step):
            @block.vector
            def _(dve):
                for n, do in enumerate(work):
                    if n:
                        dve.wait_ge(step, n)
                    do(self.nc.vector).then_inc(step, 1)

    def p1(self, name, at=0, n=1):
        a = PC1[name] + at
        return self.par1[:, a:a + n]

    def pj(self, c):
        return self.proj[:, c, 1:T + 1]

    def token_shift(self):
        nc = self.nc
        diff = self.units("h", 0, 4)
        with self.phases.phase("diff_ready", "shifted") as (block, diff_ready, shifted):
            @block.vector
            def _(dve):
                for c in range(12):
                    if c < 10:
                        if c >= 4:
                            dve.wait_ge(shifted, c - 3)
                        nc.vector.tensor_tensor(diff[:, c % 4, :], self.proj[:, c, 0:T], self.pj(c),
                                                ALU.subtract).then_inc(diff_ready, 1)
                    if c >= 2:
                        dve.wait_ge(diff_ready, c - 1)
                        nc.vector.scalar_tensor_tensor(self.pj(c - 2), diff[:, (c - 2) % 4, :], self.p1("mu", c - 2),
                                                       self.pj(c - 2), ALU.mult, ALU.add).then_inc(shifted, 1)

    def rwkv_gates(self):
        nc, banks = self.nc, self.banks
        x9, low = self.pj(9), self.units("h", 0, 1)[:, 0, :]
        lora = lambda a, b, c: self.par1[a:b, PC1["lora"] + c * P:PC1["lora"] + (c + 1) * P]
        sigw, a, g = self.units("arena", 0, 3), self.units("arena", 3, 3), [self.pj(16 + c) for c in range(RW)]
        with self.phases.phase("low_ready", "gate_product", "gates_read") as (block, low_ready, gate_product, gates_read):
            @block.scalar
            def _(act):
                nc.scalar.activation(low[0:32, :], x9[0:32, :], ACT.Tanh).then_inc(low_ready, 1)
                nc.scalar.activation(low[64:128, :], x9[64:128, :], ACT.Sigmoid).then_inc(low_ready, 1)
                for c in range(RW):
                    b = 3 * (c % 2)
                    act.wait_ge(gate_product, c + 1)
                    nc.scalar.activation(sigw[:, c, :], banks[b][:, :], ACT.Sigmoid, bias=self.p1("w0", c)).then_inc(gates_read, 1)
                    nc.scalar.activation(a[:, c, :], banks[b + 1][:, :], ACT.Sigmoid, bias=self.p1("a0", c)).then_inc(gates_read, 1)

            @block.vector
            def _(dve):
                nc.vector.tensor_copy(low[32:64, :], x9[32:64, :]).then_inc(low_ready, 1)
                for c in range(RW):
                    dve.wait_ge(gate_product, c + 1)
                    nc.vector.tensor_copy(g[c], banks[3 * (c % 2) + 2][:, :]).then_inc(gates_read, 1)

            @block.tensor
            def _(pe):
                pe.wait_ge(low_ready, 3)
                for c in range(RW):
                    b = 3 * (c % 2)
                    if c >= 2:
                        pe.wait_ge(gates_read, 6)
                    nc.tensor.matmul(banks[b][:, :], lora(0, 32, c), low[0:32, :], start=True, stop=True)
                    nc.tensor.matmul(banks[b + 1][:, :], lora(32, 64, c), low[32:64, :], start=True, stop=True)
                    nc.tensor.matmul(banks[b + 2][:, :], lora(64, 128, c), low[64:128, :], start=True, stop=True).then_inc(gate_product, 1)

    def rwkv_scale(self):
        nc, banks = self.nc, self.banks
        sigw, a, bonus = self.units("arena", 0, 3), self.units("arena", 3, 3), self.units("arena", 6, 3)
        cum, before, e_in, e_before, e_out, t1, rk = (self.units("h", i, 1)[:, 0, :] for i in range(1, 8))
        kappa = math.exp(-0.5)
        ends = self.small[:, 0:RW * NCH].rearrange("p (c n) -> p c n", c=RW)
        names = ("chain", "sums_ready", "exps_ready", "bonus_in", "bonus_sum", "chunk_done")
        with self.phases.phase(*names) as (block, chain, sums_ready, exps_ready, bonus_in, bonus_sum, chunk_done):
            @block.scalar
            def _(act):
                for c in range(RW):
                    act.wait_ge(sums_ready, c + 1)
                    if c:
                        act.wait_ge(chunk_done, c)
                    nc.scalar.activation(e_in, cum, ACT.Exp, scale=-kappa)
                    nc.scalar.activation(e_before, before, ACT.Exp, scale=-kappa)
                    nc.scalar.activation(e_out, cum, ACT.Exp, scale=kappa).then_inc(exps_ready, 1)

            @block.tensor
            def _(pe):
                for c in range(RW):
                    pe.wait_ge(bonus_in, c + 1)
                    nc.tensor.matmul(banks[c][:, :], self.c("head", P), rk, start=True, stop=True).then_inc(bonus_sum, 1)

            @block.vector
            def _(dve):
                v = nc.vector
                for c in range(RW):
                    r, k, val, at, bt = self.pj(c), self.pj(3 + c), self.pj(6 + c), self.pj(10 + c), self.pj(13 + c)
                    base = 6 * c
                    if c:
                        dve.wait_ge(chunk_done, c)
                    v.tensor_tensor_scan(cum, self.c("start64", T), sigw[:, c, :], 0.0, ALU.mult, ALU.add).then_inc(chain, 1)
                    v.tensor_scalar(t1, a[:, c, :], -1.0, self.p1("k_a", c), ALU.add, ALU.mult).then_inc(chain, 1)
                    dve.wait_ge(chain, base + 1)
                    v.tensor_tensor(before, cum, sigw[:, c, :], ALU.subtract).then_inc(sums_ready, 1)
                    dve.wait_ge(chain, base + 2)
                    v.scalar_tensor_tensor(k, t1, 1.0, k, ALU.add, ALU.mult).then_inc(chain, 1)
                    v.tensor_tensor(bt, at, a[:, c, :], ALU.mult).then_inc(chain, 1)
                    dve.wait_ge(chain, base + 3)
                    v.scalar_tensor_tensor(rk, r, self.p1("r_k", c), k, ALU.mult, ALU.mult).then_inc(bonus_in, 1)
                    dve.wait_ge(exps_ready, c + 1)
                    dve.wait_ge(chain, base + 4)
                    v.tensor_tensor(bt, bt, e_out, ALU.mult).then_inc(chain, 1)
                    v.scalar_tensor_tensor(at, at, -1.0, e_before, ALU.mult, ALU.mult).then_inc(chain, 1)
                    dve.wait_ge(bonus_in, c + 1)
                    v.tensor_tensor(r, r, e_in, ALU.mult)
                    v.tensor_tensor(k, k, e_out, ALU.mult)
                    v.tensor_copy(ends[:, c, :], e_in[:, CH - 1:T:CH])
                    dve.wait_ge(bonus_sum, c + 1)
                    v.tensor_tensor(bonus[:, c, :], banks[c][:, :], val, ALU.mult).then_inc(chunk_done, 1)

    def rwkv_pair(self, cc):
        nc, banks = self.nc, self.banks
        fa, fb, fr, fk = self.pj(10 + cc), self.pj(13 + cc), self.pj(cc), self.pj(3 + cc)
        At, Kt, Vt = (self.units("ring", i, 1)[:, 0, :] for i in range(3))
        Bt = self.units("arena", cc, 1)[:, 0, :]
        tok = lambda u: u.rearrange("p (n f) -> p n f", f=P)
        self.transposes([g for src, dst in ((fa, At), (fk, Kt), (self.pj(6 + cc), Vt), (fb, Bt))
                         for g in self.to_tokens([src], tok(dst))])
        buffers = [[self.units("h", i, 1)[:, 0, :] for i in range(8)], [self.units("ring", 3 + i, 1)[:, 0, :] for i in range(8)]]
        (L, LT, L2, L2T, I, IT, O32, O64) = zip(*buffers)
        UT, W, MV = (self.units("arena", u, 1)[:, 0, :] for u in (3 + cc, 9 + cc, 33))
        KV = self.units("arena", 12 + 2 * cc, 2)
        G = self.units("arena", 18 + 2 * cc, 2)
        RKV = self.units("arena", 24 + cc, 1)[:, 0, :]
        rows = [slice(0, HD), slice(HD, P)]
        tile = lambda u, i: u[:, i * P:(i + 1) * P]
        wide = lambda name: self.c(name, P).unsqueeze(1).to_broadcast([P, NT, P])
        names = ("scores_a", "scores_b", "masked_a", "masked_b", "values", "values_read",
                 "squares", "squares_copied", "updates", "updated", "corner", "corner_copied", "ends", "ends_read")
        with self.phases.phase(*names) as (block, scores_a, scores_b, masked_a, masked_b, values, values_read,
                                           squares, squares_copied, updates, updated, corner, corner_copied, ends, ends_read):
            @block.tensor
            def _(pe):
                def by_tile(bank, lhs, rhs, r=slice(0, P), out=slice(0, P)):
                    for i in range(NT):
                        mm = nc.tensor.matmul(tile(banks[bank][out, :], i), tile(lhs[r, :], i), tile(rhs[r, :], i), start=True, stop=True)
                    return mm
                for e in range(2):
                    by_tile(0 + e, fb, fa, rows[e])
                    by_tile(2 + e, fa, fb, rows[e])
                    by_tile(4 + e, fk, fa, rows[e])
                    by_tile(6 + e, fb, fr, rows[e]).then_inc(scores_a, 1)
                for e in range(2):
                    pe.wait_ge(masked_a, e + 1)
                    by_tile(0 + e, fk, fr, rows[e]).then_inc(scores_b, 1)
                pe.wait_ge(masked_b, 2)
                for e in range(2):
                    for i in range(NT):
                        nc.tensor.matmul(banks[4][:, i * P + e * HD:i * P + e * HD + HD], tile(L2[e], i),
                                         tile(Vt, i)[:, e * HD:e * HD + HD], start=True, stop=True)
                        mm = nc.tensor.matmul(tile(banks[5][rows[e], :], i), tile(Vt, i)[:, e * HD:e * HD + HD],
                                              tile(L2T[e], i), start=True, stop=True)
                mm.then_inc(values, 1)
                pw = [(L, LT), (L2, L2T)]
                pe.wait_ge(values_read, 2)
                for n in range(3):
                    (p, pt), (q, qt) = pw[n % 2], pw[(n + 1) % 2]
                    if n:
                        pe.wait_ge(squares_copied, 4 * n)
                    for e in range(2):
                        by_tile(0 + 2 * e, pt[e], p[e])
                        by_tile(1 + 2 * e, p[e], pt[e]).then_inc(squares, 1)
                    pe.wait_ge(squares_copied, 4 * n + 4)
                    if n:
                        pe.wait_ge(updated, 2 * n)
                    for e in range(2):
                        by_tile(4 + 2 * e, qt[e], I[e])
                        by_tile(5 + 2 * e, q[e], IT[e]).then_inc(updates, 1)
                pe.wait_ge(updated, 6)
                for e in range(2):
                    by_tile(e, O32[e], IT[e]).then_inc(corner, 1)
                pe.wait_ge(corner_copied, 2)
                for e in range(2):
                    by_tile(4 + 2 * e, L[e], I[e])
                    by_tile(5 + 2 * e, I[e], L[e]).then_inc(updates, 1)
                pe.wait_ge(updated, 8)
                for e in range(2):
                    by_tile(e, O64[e], IT[e]).then_inc(corner, 1)
                pe.wait_ge(corner_copied, 4)
                for e in range(2):
                    by_tile(5 + 2 * e, I[e], L[e]).then_inc(updates, 1)
                pe.wait_ge(updated, 10)
                for i in range(NT):
                    for e in range(2):
                        nc.tensor.matmul(tile(banks[0][rows[e], :], i), tile(At, i)[:, e * HD:e * HD + HD], tile(IT[e], i), start=True, stop=True)
                        nc.tensor.matmul(banks[1][:, i * P + e * HD:i * P + e * HD + HD], tile(IT[e], i),
                                         tile(MV, i)[:, e * HD:e * HD + HD], start=True, stop=True)
                for o in range(2):
                    for i in range(NT):
                        mm = nc.tensor.matmul(tile(banks[2 + o], i), tile(Kt[rows[o], :], i), tile(Vt[rows[o], :], i), start=True, stop=True)
                mm.then_inc(ends, 1)

            @block.scalar
            def _(act):
                act.wait_ge(values, 1)
                nc.scalar.activation(RKV, banks[5][:, :], ACT.Copy).then_inc(values_read, 1)
                pw = [(L, LT), (L2, L2T)]
                for n in range(3):
                    q, qt = pw[(n + 1) % 2]
                    for e in range(2):
                        act.wait_ge(squares, 2 * n + e + 1)
                        nc.scalar.activation(q[e], banks[0 + 2 * e][:, :], ACT.Copy).then_inc(squares_copied, 1)
                for n in range(2):
                    for e in range(2):
                        act.wait_ge(corner, 2 * n + e + 1)
                        nc.scalar.activation(L[e], banks[e][:, :], ACT.Copy).then_inc(corner_copied, 1)
                act.wait_ge(ends, 1)
                nc.scalar.activation(UT, banks[0][:, :], ACT.Copy)
                nc.scalar.activation(W, banks[1][:, :], ACT.Copy).then_inc(ends_read, 1)

            @block.vector
            def _(dve):
                v = nc.vector
                for e in range(2):
                    dve.wait_ge(scores_a, e + 1)
                    v.tensor_tensor(tok(LT[e]), tok(banks[0 + e][:, :]), wide("m16T"), ALU.mult)
                    v.tensor_tensor(tok(L[e]), tok(banks[2 + e][:, :]), wide("m16"), ALU.mult)
                    v.tensor_tensor(tok(O32[e]), tok(banks[2 + e][:, :]), wide("m32"), ALU.mult)
                    v.tensor_tensor(tok(O64[e]), tok(banks[2 + e][:, :]), wide("m64"), ALU.mult)
                    v.tensor_tensor(tok(L2[e]), tok(banks[4 + e][:, :]), wide("strictT"), ALU.mult)
                    v.tensor_tensor(tok(G[:, e, :]), tok(banks[6 + e][:, :]), wide("inclT"), ALU.mult).then_inc(masked_a, 1)
                    dve.wait_ge(masked_a, e + 1)
                    v.tensor_tensor(tok(IT[e]), tok(LT[e]), wide("ident"), ALU.add)
                    v.tensor_tensor(tok(I[e]), tok(L[e]), wide("ident"), ALU.add)
                for e in range(2):
                    dve.wait_ge(scores_b, e + 1)
                    v.tensor_tensor(tok(L2T[e]), tok(banks[0 + e][:, :]), wide("inclT"), ALU.mult).then_inc(masked_b, 1)
                dve.wait_ge(values, 1)
                v.tensor_copy(MV, banks[4][:, :]).then_inc(values_read, 1)
                pw = [(L, LT), (L2, L2T)]
                for n in range(3):
                    q, qt = pw[(n + 1) % 2]
                    for e in range(2):
                        dve.wait_ge(squares, 2 * n + e + 1)
                        v.tensor_copy(qt[e], banks[1 + 2 * e][:, :]).then_inc(squares_copied, 1)
                    for e in range(2):
                        dve.wait_ge(updates, 2 * n + e + 1)
                        v.tensor_tensor(I[e], I[e], banks[4 + 2 * e][:, :], ALU.add)
                        v.tensor_tensor(IT[e], IT[e], banks[5 + 2 * e][:, :], ALU.add).then_inc(updated, 1)
                for e in range(2):
                    dve.wait_ge(updates, 6 + e + 1)
                    v.tensor_tensor(I[e], I[e], banks[4 + 2 * e][:, :], ALU.add)
                    v.tensor_tensor(IT[e], IT[e], banks[5 + 2 * e][:, :], ALU.add).then_inc(updated, 1)
                for e in range(2):
                    dve.wait_ge(updates, 8 + e + 1)
                    v.tensor_tensor(IT[e], IT[e], banks[5 + 2 * e][:, :], ALU.add).then_inc(updated, 1)
                dve.wait_ge(ends, 1)
                for o in range(2):
                    v.tensor_tensor(tok(KV[:, o, :]), tok(banks[2 + o][:, :]), wide("head"), ALU.mult)

    def rwkv_states(self):
        nc, banks = self.nc, self.banks
        Bt, UT, W = self.units("arena", 0, 3), self.units("arena", 3, 3), self.units("arena", 9, 3)
        KV, S, SA = self.units("arena", 12, 6), self.units("arena", 27, 6), self.units("ring", 0, 3)
        ends = self.small[:, 0:RW * NCH].rearrange("p (c n) -> p c n", c=RW)
        ends_mask, kept, kept2, change = (self.units("ring", 3 + i, 1)[:, 0, 0:RW * P].rearrange("p (c f) -> p c f", c=RW) for i in range(4))
        state = lambda c: S.rearrange("p u t -> p (u t)")[:, c * RW * P:(c + 1) * RW * P].rearrange("p (c f) -> p c f", c=RW)
        three = lambda bank: bank[:, 0:RW * P].rearrange("p (c f) -> p c f", c=RW)
        with self.phases.phase("state_ready", "sa_product", "sa_ready", "update", "chain") as (
                block, state_ready, sa_product, sa_ready, update, chain):
            @block.tensor
            def _(pe):
                for c in range(NCH):
                    i, o = c // 2, slice(HD * (c % 2), HD * (c % 2) + HD)
                    pe.wait_ge(state_ready, c + 1)
                    for cc in range(RW):
                        mm = nc.tensor.matmul(three(banks[c % 2])[o, cc, :], UT[:, cc, c * CH:(c + 1) * CH], state(c)[:, cc, :],
                                              start=True, stop=True)
                    mm.then_inc(sa_product, 1)
                    if c < NCH - 1:
                        pe.wait_ge(sa_ready, c + 1)
                        for cc in range(RW):
                            mm = nc.tensor.matmul(three(banks[2 + c % 2])[:, cc, :], Bt[o, cc, i * P:(i + 1) * P],
                                                  SA[o, cc, i * P:(i + 1) * P], start=True, stop=True)
                        mm.then_inc(update, 1)

            @block.vector
            def _(dve):
                v = nc.vector
                v.memset(state(0), 0.0).then_inc(state_ready, 1)
                for c in range(NCH):
                    i, o = c // 2, slice(HD * (c % 2), HD * (c % 2) + HD)
                    dve.wait_ge(sa_product, c + 1)
                    v.tensor_tensor(SA[o, :, i * P:(i + 1) * P], three(banks[c % 2])[o, :, :], W[o, :, i * P:(i + 1) * P],
                                    ALU.add).then_inc(sa_ready, 1)
                    if c < NCH - 1:
                        end = ends[:, :, c:c + 1].to_broadcast([P, RW, P])
                        n = 3 * c
                        v.tensor_tensor(ends_mask, self.c("head", P).unsqueeze(1).to_broadcast([P, RW, P]), end, ALU.mult).then_inc(chain, 1)
                        kv = KV.rearrange("p (c o) t -> p c o t", o=2)[:, :, c % 2, i * P:(i + 1) * P]
                        dve.wait_ge(state_ready, c + 1)
                        v.tensor_tensor(kept, state(c), kv, ALU.add).then_inc(chain, 1)
                        dve.wait_ge(chain, n + 2)
                        v.tensor_tensor(kept2, kept, end, ALU.mult)
                        dve.wait_ge(update, c + 1)
                        v.tensor_tensor(change, three(banks[2 + c % 2]), ends_mask, ALU.mult).then_inc(chain, 1)
                        dve.wait_ge(chain, n + 3)
                        v.tensor_tensor(state(c + 1), change, kept2, ALU.add).then_inc(state_ready, 1)

    def rwkv_output(self):
        nc, banks = self.nc, self.banks
        S, SA, G = self.units("arena", 27, 6), self.units("ring", 0, 3), self.units("arena", 18, 6)
        RKV, bonus = self.units("arena", 24, 3), self.units("arena", 6, 3)
        state = lambda c: S.rearrange("p u t -> p (u t)")[:, c * RW * P:(c + 1) * RW * P].rearrange("p (c f) -> p c f", c=RW)
        y, sq, lg = self.units("h", 0, 3), self.units("h", 3, 2), self.units("h", 5, 2)
        rs = self.units("ring", 3, 3)
        names = ("y_product", "y_ready", "mean_sum", "centred", "squared", "var_sum", "logged", "rstd_ready", "chain")
        with self.phases.phase(*names) as (block, y_product, y_ready, mean_sum, centred, squared, var_sum, logged, rstd_ready, chain):
            @block.tensor
            def _(pe):
                for cc in range(RW):
                    for i in range(NT):
                        for c in (2 * i, 2 * i + 1):
                            nc.tensor.matmul(banks[cc][:, c * CH:(c + 1) * CH], state(c)[:, cc, :], self.pj(cc)[:, c * CH:(c + 1) * CH],
                                             start=(c == 0), stop=False, skip_group_check=True)
                        for e in range(2):
                            mm = nc.tensor.matmul(banks[cc][e * HD:(e + 1) * HD, i * P:(i + 1) * P],
                                                  SA[:, cc, i * P + e * HD:i * P + (e + 1) * HD], G[:, 2 * cc + e, i * P:(i + 1) * P],
                                                  start=False, stop=(i == NT - 1), skip_group_check=True)
                    mm.then_inc(y_product, 1)
                for cc in range(RW):
                    pe.wait_ge(y_ready, cc + 1)
                    nc.tensor.matmul(banks[3 + cc % 2][:, :], self.c("head", P), y[:, cc, :], start=True, stop=True).then_inc(mean_sum, 1)
                    pe.wait_ge(squared, cc + 1)
                    nc.tensor.matmul(banks[5 + cc % 2][:, :], self.c("head", P), sq[:, cc % 2, :], start=True, stop=True).then_inc(var_sum, 1)

            @block.scalar
            def _(act):
                for cc in range(RW):
                    act.wait_ge(centred, cc + 1)
                    nc.scalar.activation(sq[:, cc % 2, :], y[:, cc, :], ACT.Square).then_inc(squared, 1)
                    act.wait_ge(var_sum, cc + 1)
                    nc.scalar.activation(lg[:, cc % 2, :], banks[5 + cc % 2][:, :], ACT.Ln, bias=self.c("eps_gn"), scale=1.0 / HD).then_inc(logged, 1)
                    act.wait_ge(logged, cc + 1)
                    nc.scalar.activation(rs[:, cc, :], lg[:, cc % 2, :], ACT.Exp, scale=-0.5).then_inc(rstd_ready, 1)

            @block.vector
            def _(dve):
                v = nc.vector
                for cc in range(RW):
                    dve.wait_ge(y_product, cc + 1)
                    v.tensor_tensor(y[:, cc, :], banks[cc][:, :], RKV[:, cc, :], ALU.add).then_inc(y_ready, 1)
                for cc in range(RW):
                    dve.wait_ge(mean_sum, cc + 1)
                    v.scalar_tensor_tensor(y[:, cc, :], banks[3 + cc % 2][:, :], -1.0 / HD, y[:, cc, :], ALU.mult, ALU.add).then_inc(centred, 1)
                    dve.wait_ge(rstd_ready, cc + 1)
                    v.scalar_tensor_tensor(y[:, cc, :], y[:, cc, :], self.p1("ln_w", cc), rs[:, cc, :], ALU.mult, ALU.mult).then_inc(chain, 1)
                    dve.wait_ge(chain, 2 * cc + 1)
                    v.scalar_tensor_tensor(y[:, cc, :], y[:, cc, :], self.p1("ln_b", cc), bonus[:, cc, :], ALU.add, ALU.add).then_inc(chain, 1)
                    dve.wait_ge(chain, 2 * cc + 2)
                    v.tensor_tensor(self.mix[:, cc, :], y[:, cc, :], self.pj(16 + cc), ALU.mult)

    def dilated_attention(self):
        nc = self.nc
        self.head_norm([(self.pj(10 + c), self.p1("q_norm"), self.pj(10 + c), 1.0) for c in range(AT)]
                       + [(self.pj(13 + c), self.p1("k_norm"), self.pj(13 + c), 1.0) for c in range(AT)], HD, "eps6")
        vt = self.units("arena", 0, 3).rearrange("p u t -> p (u t)").rearrange("p (n f) -> p n f", f=AT * P)
        out = self.units("arena", 3, 3).rearrange("p u t -> p (u t)").rearrange("p (n f) -> p n f", f=AT * P)
        bias = self.units("arena", 6, 6)
        self.transposes(self.to_tokens([self.pj(16 + c) for c in range(AT)], vt))
        self.vector_phase([lambda v, h=h, s=s: v.scalar_tensor_tensor(bias[:, h, :], self.c("dist", T), -8.0 * s,
                                                                    self.c("log_count", T), ALU.mult, ALU.add)
                           for h, s in enumerate(dilated_slopes())])
        tiles = []
        for h in range(2 * AT):
            r = slice(HD * (h % 2), HD * (h % 2) + HD)
            for i in range(NT):
                tiles.append(dict(q=self.pj(10 + h // 2)[r, i * P:(i + 1) * P], k=self.pj(13 + h // 2)[r, 0:(i + 1) * P],
                                  bias=bias[:, h, T - (i + 1) * P:T], v=[vt[:, j, h * HD:(h + 1) * HD] for j in range(i + 1)],
                                  out=out[:, i, h * HD:(h + 1) * HD]))
        self.attention(tiles, HD ** -0.5)
        self.transposes(self.to_features(out, [self.mix[:, RW + c, :] for c in range(AT)]))

    def conv_mixer(self):
        nc, banks = self.nc, self.banks
        pad = TAPS - 1
        z = self.arena[:, 0:CV * (T + pad)].rearrange("p (c t) -> p c t", c=CV)
        sg, acc = self.units("arena", 3, 2), self.units("arena", 5, 2)
        sq, lg, rs = self.units("arena", 7, 2), self.units("arena", 9, 1)[:, 0, :], self.units("arena", 10, 1)[:, 0, :]
        names = ("opened", "z_ready", "tap", "mean_sum", "centred", "squared", "var_sum", "logged", "rstd_ready", "normed")
        with self.phases.phase(*names) as (block, opened, z_ready, tap, mean_sum, centred, squared, var_sum, logged, rstd_ready, normed):
            @block.scalar
            def _(act):
                for c in range(CV):
                    nc.scalar.activation(sg[:, c, :], self.pj(21 + c), ACT.Sigmoid).then_inc(opened, 1)
                for c in range(CV):
                    act.wait_ge(centred, c + 1)
                    nc.scalar.activation(sq[:, c, :], acc[:, c, :], ACT.Square).then_inc(squared, 1)
                act.wait_ge(var_sum, 1)
                nc.scalar.activation(lg, banks[1][:, :], ACT.Ln, bias=self.c("eps5"), scale=1.0 / (CV * P)).then_inc(logged, 1)
                act.wait_ge(logged, 1)
                nc.scalar.activation(rs, lg, ACT.Exp, scale=-0.5).then_inc(rstd_ready, 1)
                for c in range(CV):
                    act.wait_ge(normed, c + 1)
                    nc.scalar.activation(self.mix[:, RW + AT + c, :], acc[:, c, :], ACT.Silu, bias=self.p1("cln_b", c))

            @block.tensor
            def _(pe):
                pe.wait_ge(tap, CV * TAPS)
                for c in range(CV):
                    mm = nc.tensor.matmul(banks[0][:, :], self.c("ones", P), acc[:, c, :], start=(c == 0), stop=(c == CV - 1))
                mm.then_inc(mean_sum, 1)
                for c in range(CV):
                    pe.wait_ge(squared, c + 1)
                    mm = nc.tensor.matmul(banks[1][:, :], self.c("ones", P), sq[:, c, :], start=(c == 0), stop=(c == CV - 1))
                mm.then_inc(var_sum, 1)

            @block.vector
            def _(dve):
                v = nc.vector
                v.memset(z[:, :, 0:pad], 0.0).then_inc(z_ready, 1)
                for c in range(CV):
                    dve.wait_ge(opened, c + 1)
                    v.tensor_tensor(z[:, c, pad:], self.pj(19 + c), sg[:, c, :], ALU.mult).then_inc(z_ready, 1)
                dve.wait_ge(z_ready, 1 + CV)
                for j in range(TAPS):
                    for c in range(CV):
                        w = self.p1("dw", j * CV + c)
                        if j == 0:
                            v.tensor_scalar(acc[:, c, :], z[:, c, 0:T], w, self.p1("dw_b", c), ALU.mult, ALU.add).then_inc(tap, 1)
                        else:
                            dve.wait_ge(tap, CV * (j - 1) + c + 1)
                            v.scalar_tensor_tensor(acc[:, c, :], z[:, c, j:j + T], w, acc[:, c, :], ALU.mult, ALU.add).then_inc(tap, 1)
                dve.wait_ge(mean_sum, 1)
                for c in range(CV):
                    v.scalar_tensor_tensor(acc[:, c, :], banks[0][:, :], -1.0 / (CV * P), acc[:, c, :], ALU.mult, ALU.add).then_inc(centred, 1)
                dve.wait_ge(rstd_ready, 1)
                for c in range(CV):
                    v.scalar_tensor_tensor(acc[:, c, :], acc[:, c, :], self.p1("cln_w", c), rs, ALU.mult, ALU.mult).then_inc(normed, 1)

    def first_layer(self, layer, stop=None):
        self.load_layer(layer)
        gains = lambda n: self.p1(n, 0, KD)
        self.ffn(gains("norm_ffn1"), "gu1", layer * 2 * KF, "down1", layer * 2 * KD, 0.5)
        self.norm(self.x, self.h, gains("norm_mix"))
        self.vector_phase([lambda v: v.memset(self.proj[:, :, 0:1], 0.0)])
        self.project("w_in", layer * M_IN, KD, M_IN, self.h, self.proj[:, :, 1:T + 1])
        self.dilated_attention()
        self.conv_mixer()
        self.token_shift()
        self.rwkv_gates()
        self.head_norm([(self.pj(3 + c), self.p1("k_k", c), self.pj(10 + c), self.p1("k_k", c)) for c in range(RW)], 1, "eps12")
        self.rwkv_scale()
        for cc in range(RW):
            self.rwkv_pair(cc)
        self.rwkv_states()
        self.rwkv_output()
        self.add_to_residual("w_out", layer * KD, KD, self.mix, 1.0)
        self.ffn(gains("norm_ffn2"), "gu2", layer * 2 * KF, "down2", layer * 2 * KD, 0.5)

    def p2(self, name, at=0, n=1):
        a = PC2[name] + at
        return self.par2[:, a:a + n]

    def memory_kv(self, layer):
        with self.phases.phase("loaded") as (block, loaded):
            @block.sync
            def _(sp):
                sp.dma_start(self.mix[:, :, 0:MEM_T], self.dram["mem"]).then_inc(loaded, 16)
                sp.wait_ge(loaded, 16)
        self.norm(self.mix, self.h, self.p2("g_mem", KD * layer, KD), MEM_T)
        self.project("w_mem", layer * KD, KD, KD, self.h, self.mix, MEM_T)
        self.mk = self.units("arena", 30, 2).rearrange("p u t -> p (u t)").rearrange("p (h t) -> p h t", h=4)
        self.mv = self.units("arena", 32, 2).rearrange("p u t -> p (u t)").rearrange("p (n f) -> p n f", f=T)
        self.vector_phase([lambda v: v.tensor_copy(self.mk, self.mix[:, 0:4, 0:MEM_T])])
        self.transposes(self.to_tokens([self.mix[:, 4 + c, 0:MEM_T] for c in range(4)], self.mv))

    def memory_attention(self, first, out, done):
        tiles = [dict(q=self.pj(first + h)[:, i * P:(i + 1) * P], k=self.mk[:, h, :], bias=self.c("zero", MEM_T),
                      v=[self.mv[:, j, h * P:(h + 1) * P] for j in range(2)], out=out[:, i, h * P:(h + 1) * P])
                 for h in range(4) for i in range(NT)]
        self.attention(tiles, P ** -0.5)
        self.transposes(self.to_features(out, done))

    def gla_decays(self):
        nc, banks = self.nc, self.banks
        small = self.units("ring", 0, 1)[:, 0, 0:3 * P]
        alr, z, low, mag, ex, lg, la, cum, ein, eout = (self.units("arena", i, 1)[:, 0, :] for i in range(10))
        kt = self.units("arena", 10, 2)
        ends = self.small[:, 0:2 * NGC].rearrange("p (c n) -> p c n", c=2)
        names = ("loaded", "alr_product", "alr_ready", "z_product", "z_ready", "chain", "magnitude", "exped", "logged",
                 "summed_up", "decays_ready", "chunk_done")
        with self.phases.phase(*names) as (block, loaded, alr_product, alr_ready, z_product, z_ready, chain, magnitude,
                                           exped, logged, summed_up, decays_ready, chunk_done):
            @block.sync
            def _(sp):
                sp.dma_start(small, self.dram["gla_small"]).then_inc(loaded, 16)

            @block.tensor
            def _(pe):
                pe.wait_ge(loaded, 16)
                for k in range(KD):
                    mm = nc.tensor.matmul(banks[0][0:16, :], small[:, 16 * k:16 * k + 16], self.h[:, k, :], start=(k == 0), stop=(k == KD - 1))
                mm.then_inc(alr_product, 1)
                pe.wait_ge(alr_ready, 1)
                for cc in range(2):
                    nc.tensor.matmul(banks[1 + cc][:, :], small[0:16, P + cc * P:P + (cc + 1) * P], alr[0:16, :], start=True, stop=True).then_inc(z_product, 1)

            @block.scalar
            def _(act):
                for cc in range(2):
                    act.wait_ge(magnitude, cc + 1)
                    nc.scalar.activation(ex, mag, ACT.Exp, scale=-1.0).then_inc(exped, 1)
                    act.wait_ge(exped, cc + 1)
                    nc.scalar.activation(lg, ex, ACT.Ln, bias=self.c("one")).then_inc(logged, 1)
                    act.wait_ge(summed_up, cc + 1)
                    nc.scalar.activation(ein, cum, ACT.Exp, scale=1.0 / 16)
                    nc.scalar.activation(eout, cum, ACT.Exp, scale=-1.0 / 16).then_inc(decays_ready, 1)

            @block.vector
            def _(dve):
                v = nc.vector
                dve.wait_ge(alr_product, 1)
                v.tensor_copy(alr[0:16, :], banks[0][0:16, :]).then_inc(alr_ready, 1)
                for cc in range(2):
                    q, k = self.pj(cc), self.pj(2 + cc)
                    n = 2 * cc
                    dve.wait_ge(z_product, cc + 1)
                    if cc:
                        dve.wait_ge(chunk_done, cc)
                    v.tensor_scalar(z, banks[1 + cc][:, :], self.p2("b_alpha", cc), None, ALU.add).then_inc(z_ready, 1)
                    dve.wait_ge(z_ready, cc + 1)
                    v.tensor_scalar(low, z, 0.0, None, ALU.min)
                    v.scalar_tensor_tensor(mag, z, -1.0, z, ALU.mult, ALU.max).then_inc(magnitude, 1)
                    dve.wait_ge(logged, cc + 1)
                    v.tensor_tensor(la, low, lg, ALU.subtract).then_inc(chain, 1)
                    dve.wait_ge(chain, n + 1)
                    v.tensor_tensor_scan(cum, self.c("start32", T), la, 0.0, ALU.mult, ALU.add).then_inc(summed_up, 1)
                    dve.wait_ge(decays_ready, cc + 1)
                    v.scalar_tensor_tensor(q, q, 0.125, ein, ALU.mult, ALU.mult)
                    v.tensor_tensor(k, k, eout, ALU.mult).then_inc(chain, 1)
                    v.tensor_copy(ends[:, cc, :], ein[:, GC - 1:T:GC])
                    dve.wait_ge(chain, n + 2)
                    v.tensor_tensor(kt[:, cc, :].rearrange("p (c t) -> p c t", t=GC), k.rearrange("p (c t) -> p c t", t=GC),
                                    ein.rearrange("p (c t) -> p c t", t=GC)[:, :, GC - 1:GC].to_broadcast([P, NGC, GC]),
                                    ALU.mult).then_inc(chunk_done, 1)

    def gla_mix(self):
        nc, banks = self.nc, self.banks
        flat = lambda w, f: self.units(*w).rearrange("p u t -> p (u t)").rearrange("p (n f) -> p n f", f=f)
        Vt, Kh = flat(("arena", 0, 4), T), flat(("arena", 4, 2), 2 * P)
        self.transposes(self.to_tokens([self.pj(4 + c) for c in range(4)], Vt)
                        + self.to_tokens([self.units("arena", 10 + c, 1)[:, 0, :] for c in range(2)], Kh))
        S = self.units("arena", 12, 8).rearrange("p u t -> p (u t)").rearrange("p (c n f) -> p c n f", c=2, f=P)
        A = self.units("arena", 20, 4)
        ends = self.small[:, 0:2 * NGC].rearrange("p (c n) -> p c n", c=2)
        rows = [slice(0, HD), slice(HD, P)]
        tile = lambda u, i: u[:, i * P:(i + 1) * P]
        with self.phases.phase("kv_product", "state_ready") as (block, kv_product, state_ready):
            @block.tensor
            def _(pe):
                for cc in range(2):
                    for g in range(4):
                        r = slice(GC * g, GC * g + GC)
                        for i in range(NT):
                            for e in range(2):
                                mm = nc.tensor.matmul(tile(banks[4 * cc + g][rows[e], :], i),
                                                      Kh[r, i, cc * P + e * HD:cc * P + (e + 1) * HD],
                                                      Vt[r, i, (2 * cc + e) * P:(2 * cc + e + 1) * P], start=True, stop=True,
                                                      tile_position=(GC * g, HD * e))
                    mm.then_inc(kv_product, 1)

            @block.vector
            def _(dve):
                v = nc.vector
                v.memset(S[:, :, 0, :], 0.0).then_inc(state_ready, 1)
                dve.wait_ge(kv_product, 2)
                for c in range(NGC - 1):
                    for cc in range(2):
                        dve.wait_ge(state_ready, max(1, 2 * c + cc))
                        v.scalar_tensor_tensor(S[:, cc, c + 1, :], S[:, cc, c, :], ends[:, cc, c:c + 1],
                                               tile(banks[4 * cc + c % 4], c // 4), ALU.mult, ALU.add).then_inc(state_ready, 1)

        o, sr = self.units("arena", 24, 4), self.units("h", 0, 4)
        sq, lg, rs = self.units("ring", 0, 2), self.units("ring", 2, 2), self.units("ring", 4, 2)
        names = ("scores", "masked", "product", "stored", "squared", "summed", "logged", "rstd_ready", "opened", "normed")
        with self.phases.phase(*names) as (block, scores, masked, product, stored, squared, summed, logged, rstd_ready, opened, normed):
            @block.tensor
            def _(pe):
                for h in range(4):
                    cc, r = h // 2, rows[h % 2]
                    for i in range(NT):
                        mm = nc.tensor.matmul(tile(banks[h], i), tile(self.pj(2 + cc)[r, :], i), tile(self.pj(cc)[r, :], i), start=True, stop=True)
                    mm.then_inc(scores, 1)
                for h in range(4):
                    cc, r = h // 2, rows[h % 2]
                    pe.wait_ge(masked, h + 1)
                    for i in range(NT):
                        nc.tensor.matmul(tile(banks[4 + h], i), Vt[:, i, h * P:(h + 1) * P], tile(A[:, h, :], i), start=True, stop=False)
                        for c in range(4 * i, 4 * i + 4):
                            mm = nc.tensor.matmul(banks[4 + h][:, c * GC:(c + 1) * GC], S[r, cc, c, :], self.pj(cc)[r, c * GC:(c + 1) * GC],
                                                  start=False, stop=(c == 4 * i + 3))
                    mm.then_inc(product, 1)
                for h in range(4):
                    pe.wait_ge(squared, h + 1)
                    nc.tensor.matmul(banks[h % 2][:, :], self.c("ones", P), sq[:, h % 2, :], start=True, stop=True).then_inc(summed, 1)

            @block.scalar
            def _(act):
                for h in range(4):
                    nc.scalar.activation(sr[:, h, :], self.pj(8 + h), ACT.Silu).then_inc(opened, 1)
                for h in range(4):
                    act.wait_ge(stored, h + 1)
                    if h >= 2:
                        act.wait_ge(summed, h - 1)
                    nc.scalar.activation(sq[:, h % 2, :], o[:, h, :], ACT.Square).then_inc(squared, 1)
                    act.wait_ge(summed, h + 1)
                    nc.scalar.activation(lg[:, h % 2, :], banks[h % 2][:, :], ACT.Ln, bias=self.c("eps6"), scale=1.0 / P).then_inc(logged, 1)
                    act.wait_ge(logged, h + 1)
                    if h >= 2:
                        act.wait_ge(normed, h - 1)
                    nc.scalar.activation(rs[:, h % 2, :], lg[:, h % 2, :], ACT.Exp, scale=-0.5).then_inc(rstd_ready, 1)

            @block.vector
            def _(dve):
                v = nc.vector
                for h in range(4):
                    dve.wait_ge(scores, h + 1)
                    v.tensor_tensor(A[:, h, :].rearrange("p (n t) -> p n t", t=P), banks[h][:, :].rearrange("p (n t) -> p n t", t=P),
                                    self.c("incl32T", P).unsqueeze(1).to_broadcast([P, NT, P]), ALU.mult).then_inc(masked, 1)
                for h in range(4):
                    dve.wait_ge(product, h + 1)
                    v.tensor_copy(o[:, h, :], banks[4 + h][:, :]).then_inc(stored, 1)
                for h in range(4):
                    dve.wait_ge(rstd_ready, h + 1)
                    v.scalar_tensor_tensor(o[:, h, :], o[:, h, :], self.p2("g_head"), rs[:, h % 2, :], ALU.mult, ALU.mult).then_inc(normed, 1)
                    dve.wait_ge(normed, h + 1)
                    dve.wait_ge(opened, h + 1)
                    v.tensor_tensor(self.mix[:, h, :], o[:, h, :], sr[:, h, :], ALU.mult)

    def gla_layer(self):
        self.memory_kv(0)
        self.norm(self.x, self.h, self.p2("g_mix", 0, KD))
        self.project("a_in", 0, KD, 16, self.h, self.proj[:, :, 1:T + 1])
        self.gla_decays()
        self.gla_mix()
        out = self.units("arena", 0, 4).rearrange("p u t -> p (u t)").rearrange("p (n f) -> p n f", f=T)
        self.memory_attention(12, out, [self.mix[:, 4 + c, :] for c in range(4)])
        self.add_to_residual("a_out", 0, KD, self.mix, 1.0)
        self.conv_ffn(0)

    def conv_ffn(self, layer):
        taps = [self.p2("cw", (3 * layer + j) * KF, KF) for j in range(3)]
        self.ffn(self.p2("g_ffn", layer * KD, KD), "gu3", layer * 2 * KF, "down3", layer * 2 * KD, 1.0,
                 taps, self.p2("cb", layer * KF, KF))

    def compress(self, src, pe_name, weights, w2, out_k, out_v):
        nc, banks = self.nc, self.banks
        GELU = math.sqrt(2.0 / math.pi)
        early, late = self.units("ring", 0, 1)[:, 0, :], self.units("ring", 1, 1)[:, 0, :]
        w = self.arena[:, 8 * T:24 * T].rearrange("p (j f) -> p j f", f=256)
        wb = self.units("ring", 2, 1)[:, 0, 0:P]
        hid, cube, act_in, th, ge = (self.units("ring", 3 + i, 1)[:, 0, 0:4 * 32].rearrange("p (n b) -> p n b", b=32)[:, :, 0:NCMP] for i in range(5))
        names = ("loaded", "shifted", "product", "chain", "argument", "tanh_ready", "gelu_ready", "out_product")
        with self.phases.phase(*names) as (block, loaded, shifted, product, chain, argument, tanh_ready, gelu_ready, out_product):
            @block.sync
            def _(sp):
                for half in range(2):
                    sp.dma_start(w[half * HD:(half + 1) * HD, :, :], self.dram[weights]).then_inc(loaded, 16)
                sp.dma_start(wb, self.dram[w2]).then_inc(loaded, 16)

            @block.tensor
            def _(pe):
                pe.wait_ge(loaded, 48)
                pe.wait_ge(shifted, 2)
                for g in range(2):
                    r = slice(g * HD, (g + 1) * HD)
                    for m in range(2):
                        for j in range(32):
                            tokens = (early if j < 16 else late)[r, j:j + 16 * NCMP - 15:16]
                            mm = nc.tensor.matmul(banks[2 * g + m][:, 0:NCMP], w[r, j, m * P:(m + 1) * P], tokens, start=(j == 0), stop=(j == 31))
                mm.then_inc(product, 1)
                pe.wait_ge(gelu_ready, 1)
                for g in range(2):
                    for m in range(2):
                        if out_k is not None:
                            mm = nc.tensor.matmul(banks[4][g * HD:(g + 1) * HD, 0:NCMP], wb[:, m * HD:(m + 1) * HD], ge[:, 2 * g + m, :],
                                                  start=(m == 0), stop=(m == 1))
                        else:
                            mm = nc.tensor.matmul(banks[4][0:NCMP, g * HD:(g + 1) * HD], ge[:, 2 * g + m, :], wb[:, m * HD:(m + 1) * HD],
                                                  start=(m == 0), stop=(m == 1))
                mm.then_inc(out_product, 1)

            @block.scalar
            def _(act):
                act.wait_ge(argument, 1)
                nc.scalar.activation(th, act_in, ACT.Tanh, scale=GELU).then_inc(tanh_ready, 1)

            @block.vector
            def _(dve):
                v = nc.vector
                both = lambda half: self.p2(pe_name, 16 * half, 16).unsqueeze(1).to_broadcast([P, 32, 16])
                blocks = lambda u: u.rearrange("p (m j) -> p m j", j=16)
                v.tensor_tensor(blocks(early), blocks(src), both(0), ALU.add).then_inc(shifted, 1)
                v.tensor_tensor(blocks(late), blocks(src), both(1), ALU.add).then_inc(shifted, 1)
                dve.wait_ge(product, 1)
                for n in range(4):
                    v.tensor_copy(hid[:, n, :], banks[n][:, 0:NCMP]).then_inc(chain, 1)
                dve.wait_ge(chain, 4)
                v.tensor_tensor(cube, hid, hid, ALU.mult).then_inc(chain, 1)
                dve.wait_ge(chain, 5)
                v.tensor_scalar(cube, cube, 0.044715, 1.0, ALU.mult, ALU.add).then_inc(chain, 1)
                dve.wait_ge(chain, 6)
                v.tensor_tensor(act_in, cube, hid, ALU.mult).then_inc(argument, 1)
                dve.wait_ge(argument, 1)
                v.tensor_scalar(cube, hid, 0.5, None, ALU.mult).then_inc(chain, 1)
                dve.wait_ge(chain, 7)
                dve.wait_ge(tanh_ready, 1)
                v.scalar_tensor_tensor(ge, th, 1.0, cube, ALU.add, ALU.mult).then_inc(gelu_ready, 1)
                dve.wait_ge(out_product, 1)
                if out_k is not None:
                    v.tensor_copy(out_k, banks[4][:, 0:NCMP])
                else:
                    v.tensor_copy(out_v, banks[4][0:NCMP, 0:P])

    def nsa_gates(self, gates):
        nc, banks = self.nc, self.banks
        w = self.units("ring", 0, 1)[:, 0, 0:KD * 24].rearrange("p (k c) -> p k c", c=24)
        with self.phases.phase("loaded", "product") as (block, loaded, product):
            @block.sync
            def _(sp):
                sp.dma_start(w, self.dram["w_gates"]).then_inc(loaded, 16)

            @block.tensor
            def _(pe):
                pe.wait_ge(loaded, 16)
                for i in range(NT):
                    for k in range(KD):
                        mm = nc.tensor.matmul(banks[0][:, i * 24:(i + 1) * 24], self.h[:, k, i * P:(i + 1) * P], w[:, k, :],
                                              start=(k == 0), stop=(k == KD - 1))
                mm.then_inc(product, 1)

            @block.scalar
            def _(act):
                act.wait_ge(product, 1)
                nc.scalar.activation(gates, banks[0][:, 0:NT * 24], ACT.Sigmoid)

    def nsa_layer(self):
        self.memory_kv(1)
        kv = self.units("arena", 0, 6)
        self.norm(self.x, self.h, self.p2("g_kv", 0, KD))
        self.project("w_kv", 0, KD, 6, self.h, kv)
        k_cmp, v_cmp = self.big[:, 8000:8000 + NCMP], self.big[0:NCMP, 8064:8064 + P]
        self.compress(kv[:, 0, :], "pe_k", "w_ck1", "w_ck2", k_cmp, None)
        self.compress(kv[:, 1, :], "pe_v", "w_cv1", "w_cv2", None, v_cmp)
        self.norm_into_h()
        self.project("b_in", 0, KD, 8, self.h, self.proj[:, :, 1:T + 1])
        gates_flat = self.small[:, 400:400 + NT * 24]
        self.nsa_gates(gates_flat)
        gate = lambda i, h, b: gates_flat[:, i * 24 + h * 3 + b:i * 24 + h * 3 + b + 1]
        flat = lambda w, f: self.units(*w).rearrange("p u t -> p (u t)").rearrange("p (n f) -> p n f", f=f)
        vs, vw = flat(("arena", 6, 1), P), flat(("arena", 7, 1), P)
        self.transposes(self.to_tokens([kv[:, 3, :]], vs) + self.to_tokens([kv[:, 5, :]], vw))
        out = flat(("arena", 8, 4), T)
        bias = self.units("arena", 12, 8)
        cmp_bias = self.units("arena", 20, 2).rearrange("p u t -> p (u t)")[:, 0:8 * 124].rearrange("p (h c) -> p h c", h=8)
        self.vector_phase(
            [lambda v, h=h, s=s: v.scalar_tensor_tensor(bias[:, h, :], self.c("dist", T), -8.0 * s, self.c("causal", T), ALU.mult, ALU.add)
             for h, s in enumerate(NSA_SLOPES)]
            + [lambda v, h=h, s=s: v.scalar_tensor_tensor(cmp_bias[:, h, :], self.c("cmp_dist", NT * NCMP), -8.0 * s,
                                                          self.c("cmp_mask", NT * NCMP), ALU.mult, ALU.add)
               for h, s in enumerate(NSA_SLOPES)])
        tiles = []
        for h in range(8):
            g = h // 4
            r = slice(HD * g, HD * (g + 1))
            for i in range(NT):
                q, o = self.pj(h % 4)[r, i * P:(i + 1) * P], out[:, i, h * HD:(h + 1) * HD]
                n = len(tiles)
                tiles.append(dict(q=q, k=k_cmp[r, :], bias=cmp_bias[:, h, i * NCMP:(i + 1) * NCMP], v=[v_cmp[:, r]],
                                  out=o, gate=gate(i, h, 0)))
                for b, kk, vv in ((1, kv[:, 2, :], vs), (2, kv[:, 4, :], vw)):
                    tiles.append(dict(q=q, k=kk[r, 0:(i + 1) * P], bias=bias[:, h, T - (i + 1) * P:T],
                                      v=[vv[:, j, HD * g:HD * (g + 1)] for j in range(i + 1)], out=o, gate=gate(i, h, b),
                                      add=True, after=n + b - 1))
        self.attention(tiles, HD ** -0.5)
        self.transposes(self.to_features(out, [self.mix[:, c, :] for c in range(4)]))
        self.memory_attention(4, out, [self.mix[:, 4 + c, :] for c in range(4)])
        self.add_to_residual("b_out", 0, KD, self.mix, 1.0)
        self.conv_ffn(1)

    def norm_into_h(self):
        self.norm(self.x, self.h, self.p2("g_mix", KD, KD), scratch=24)

    def store(self):
        self.norm(self.x, self.h, self.p2("g_final", 0, KD))
        with self.phases.phase("written") as (block, written):
            @block.sync
            def _(sp):
                sp.dma_start(self.dram["out"], self.h[:, :, :]).then_inc(written, 16)
                sp.wait_ge(written, 16)


def build(nc, dram, parts=3):
    with ExitStack() as ctx:
        core = Core(nc, ctx, dram)
        core.load_start()
        with nc.Fori(0, 2) as layer:
            core.first_layer(layer)
            if core.phases.n % 2 == 0:
                core.pause()
        core.gla_layer()
        core.nsa_layer()
        core.store()


def feature_columns(v):
    return np.ascontiguousarray(v.reshape(-1, P).T)


def tiles_of(w, kc):
    n, k, m = w.shape
    t = w.reshape(n, k // (kc * P), kc, P, m // P, P).transpose(0, 4, 1, 3, 2, 5)
    return t.reshape(-1, P, kc * P)


def in_turn(a, b):
    return np.stack([tiles_of(a, KD), tiles_of(b, KD)], axis=1).reshape(-1, P, KD * P)


def layouts(i):
    two = lambda v: np.concatenate([v, v]).reshape(P, 1)
    par1 = []
    for l in range(2):
        cols = [feature_columns(i[n][l]) for n in ("norm_ffn1", "norm_mix", "norm_ffn2", "shift_mu", "rwkv_w0", "rwkv_a0",
                                                    "rwkv_k_k", "rwkv_k_a", "rwkv_r_k", "rwkv_ln_w", "rwkv_ln_b")]
        cols += [two(i["attn_q_norm"][l]), two(i["attn_k_norm"][l])]
        cols += [feature_columns(i[n][l]) for n in ("conv_dw_w", "conv_dw_b", "conv_ln_w", "conv_ln_b")]
        cols += [np.concatenate([i["rwkv_w2"][l], i["rwkv_a2"][l], i["rwkv_g2"][l]])]
        par1.append(np.concatenate(cols, axis=1))
    cols = [feature_columns(i[n]) for n in ("g_mix_2", "g_ffn_2", "g_mem_2", "conv_w_2", "conv_b_2", "a_b_alpha_2",
                                             "a_g_head_2", "g_kv_2", "g_final_2")]
    cols += [np.concatenate([i[n].T, i[n].T]) for n in ("pe_k_2", "pe_v_2")]
    a = i["a_w_in_2"]
    q, mq = i["b_w_in_2"][:, :, 0:512], i["b_w_in_2"][:, :, 536:1048]
    q = q.reshape(1, D, 2, 4, HD).transpose(0, 1, 3, 2, 4).reshape(1, D, 512)
    alr = a[0, :, 1536:1552].reshape(KD, P, 16).transpose(1, 0, 2).reshape(P, P)
    w_alpha = np.concatenate([i["a_w_alpha_2"][0]] * 8)
    halves = lambda w: w.reshape(2, P, HD).transpose(1, 0, 2).reshape(P, P)
    return {
        "consts": constants(),
        "x": i["x"][0].T.reshape(KD, P, T).transpose(1, 0, 2),
        "mem": i["mem_2"][0].T.reshape(KD, P, MEM_T).transpose(1, 0, 2),
        "par1": np.stack(par1),
        "par2": np.concatenate(cols, axis=1),
        "gu1": in_turn(i["ffn1_w_gate"], i["ffn1_w_up"]),
        "down1": tiles_of(i["ffn1_w_down"], KF // 2),
        "w_in": tiles_of(i["w_in"], KD),
        "w_out": tiles_of(i["w_out"], KD),
        "gu2": in_turn(i["ffn2_w_gate"], i["ffn2_w_up"]),
        "down2": tiles_of(i["ffn2_w_down"], KF // 2),
        "w_mem": tiles_of(i["w_mem_kv_2"], KD),
        "gu3": in_turn(i["w_up_2"][:, :, 0:FF], i["w_up_2"][:, :, FF:]),
        "down3": tiles_of(i["w_down_2"], KF // 2),
        "a_in": tiles_of(np.concatenate([a[:, :, 0:1536], a[:, :, 1552:]], axis=2), KD),
        "a_out": tiles_of(i["a_w_out_2"], KD),
        "gla_small": np.concatenate([alr, w_alpha], axis=1),
        "w_kv": tiles_of(i["w_kv_2"][None], KD),
        "w_ck1": i["w_ck1_2"].reshape(32, HD, 256).transpose(1, 0, 2),
        "w_ck2": halves(i["w_ck2_2"]),
        "w_cv1": i["w_cv1_2"].reshape(32, HD, 256).transpose(1, 0, 2),
        "w_cv2": halves(i["w_cv2_2"]),
        "w_gates": i["b_w_in_2"][0, :, 512:536].reshape(KD, P, 24).transpose(1, 0, 2),
        "b_in": tiles_of(np.concatenate([q, mq], axis=2), KD),
        "b_out": tiles_of(i["b_w_out_2"], KD),
    }


def kernel(**inputs):
    import concourse.bacc as bacc
    from concourse.bass_utils import run_bass_kernel_spmd

    nc = bacc.Bacc("TRN2", target_bir_lowering=False, num_devices=1)
    arrays = {n: np.ascontiguousarray(a) for n, a in layouts({n: np.asarray(v) for n, v in inputs.items()}).items()}
    dram = {n: nc.dram_tensor(f"in_{n}", a.shape, F32, kind="ExternalInput").ap() for n, a in arrays.items()}
    dram["out"] = nc.dram_tensor("out_x", (P, KD, T), F32, kind="ExternalOutput").ap()
    build(nc, dram)
    r = run_bass_kernel_spmd(nc, [{f"in_{n}": a for n, a in arrays.items()}], core_ids=[0])
    out = np.asarray(r.results[0]["out_x"])
    return out.transpose(2, 1, 0).reshape(1, T, D)
```

```python
import math
from contextlib import ExitStack, contextmanager

import numpy as np

import concourse.bass as bass
from concourse import mybir

F32 = mybir.dt.float32
F32R = mybir.dt.float32r
ALU = mybir.AluOpType
ACT = mybir.ActivationFunctionType
AX = mybir.AxisListType

P = 128
D = 1024
T = 512
NT = T // P
KD = D // P
FF = 2816
KF = FF // P
HD = 64
MEM_T = 256
D_IN = 2944
M_IN = D_IN // P
RW = 3
AT = 3
CV = 2
TAPS = 31
CH = 64
NCH = T // CH
GC = 32
NGC = T // GC
NCMP = 31
NEG = -1e30

def columns(widths):
    at, out = 0, {}
    for name, n in widths:
        out[name] = at
        at += n
    return out, at


PC1, NP1 = columns([
    ("norm_ffn1", KD), ("norm_mix", KD), ("norm_ffn2", KD), ("mu", 10), ("w0", RW), ("a0", RW),
    ("k_k", RW), ("k_a", RW), ("r_k", RW), ("ln_w", RW), ("ln_b", RW), ("q_norm", 1), ("k_norm", 1),
    ("dw", TAPS * CV), ("dw_b", CV), ("cln_w", CV), ("cln_b", CV), ("lora", 3 * P)])
PC2, NP2 = columns([
    ("g_mix", 2 * KD), ("g_ffn", 2 * KD), ("g_mem", 2 * KD), ("cw", 2 * 3 * KF), ("cb", 2 * KF),
    ("b_alpha", 2), ("g_head", 1), ("g_kv", KD), ("g_final", KD), ("pe_k", 32), ("pe_v", 32)])
CA, NCA = columns([("ident", P), ("ones", P), ("head", P), ("eps6", 1), ("eps12", 1), ("eps_gn", 1), ("eps5", 1), ("one", 1)])
CB, NCB = columns([
    ("m16", P), ("m32", P), ("m64", P), ("m16T", P), ("strictT", P), ("inclT", P), ("incl32T", P), ("dist", T),
    ("log_count", T), ("causal", T), ("start64", T), ("start32", T), ("cmp_dist", NT * NCMP),
    ("cmp_mask", NT * NCMP), ("zero", T)])


def constants():
    i = np.arange(P)
    same = lambda n: (i[:, None] // n == i[None, :] // n).astype(np.float32)
    below = (i[:, None] > i[None, :]).astype(np.float32)
    upto = (i[:, None] <= i[None, :]).astype(np.float32)
    dist = (i[:, None] + (T - P) - np.arange(T)[None, :]).astype(np.int64)
    count = (dist <= 128).astype(int) + (dist % 4 == 0) + (dist % 16 == 0)
    count = np.where(dist >= 0, count, 0)
    t = np.arange(T)
    cmp_dist = np.concatenate([(P * b + i)[:, None] - (16 * np.arange(NCMP) + 31)[None, :] for b in range(NT)], axis=1)
    row = lambda v: np.broadcast_to(np.asarray(v, np.float32)[None, :], (P, len(v)))
    col = lambda v: np.full((P, 1), v, np.float32)
    always = [np.eye(P), np.ones((P, P)), same(HD), col(1e-6), col(1e-12), col(64e-5), col(1e-5), col(1.0)]
    mixers = [
        below * same(16), below * (same(32) - same(16)), below * (same(64) - same(32)), (below * same(16)).T,
        (below * same(64)).T, upto * same(64), upto * same(32), dist,
        np.where(count > 0, 8.0 * np.log(np.maximum(count, 1)), NEG), np.where(dist >= 0, 0.0, NEG),
        row(t % CH != 0), row(t % GC != 0), cmp_dist, np.where(cmp_dist >= 0, 0.0, NEG), np.zeros((P, T))]
    return [np.concatenate([np.asarray(p, np.float32) for p in parts], axis=1) for parts in (always, mixers)]


def dilated_slopes():
    pow2 = lambda m: [(2.0 ** (-8.0 / m)) ** (i + 1) for i in range(m)]
    return pow2(4) + pow2(8)[0::2][:2]


NSA_SLOPES = [2.0 ** (-(h + 1)) for h in range(8)]


class Phases:

    FIRST, SIZE = 110, 40

    def __init__(self, nc):
        self.nc, self.n = nc, 0

    @contextmanager
    def phase(self, *names):
        nc = self.nc
        own = self.FIRST + self.SIZE * (self.n % 2)
        other = self.FIRST + self.SIZE * ((self.n + 1) % 2)
        self.n += 1
        assert len(names) <= self.SIZE
        with ExitStack() as ctx:
            sems = [ctx.enter_context(nc.semaphore(f"{n}_{self.n}", num=own + i)) for i, n in enumerate(names)]
            block = ctx.enter_context(nc.Block())

            @block.gpsimd
            def _(pool):
                pool.sem_clear(range(other, other + self.SIZE))

            yield (block, *sems)


def repeat(eng, total, unroll, body):
    whole = total // unroll
    if whole >= 2:
        with eng.Fori(0, whole) as n:
            for u in range(unroll):
                body(n * unroll + u, n, u)
    else:
        whole = 0
    for i in range(whole * unroll, total):
        body(i, i // unroll, i % unroll)


def uses(n, per, k, slots):
    assert per % slots == 0
    return n * (per // slots) + k // slots + 1


def chunk(ap, i):
    if isinstance(i, int):
        return ap[:, i, :]
    return ap[:, bass.ds(i, 1), :].rearrange("p a t -> p (a t)")


def column(ap, i):
    return ap[:, i:i + 1] if isinstance(i, int) else ap[:, bass.ds(i, 1)]


class Core:

    SLOTS = 4
    SLOT = 11 * P
    align = lambda n: -(-n // 8) * 8
    SMALL = 400 + NT * 24
    AT_X = 0
    AT_FIXED = AT_X + KD * T
    AT_PAR1 = AT_FIXED + align(NCA)
    AT_PAR2 = AT_PAR1 + align(NP1)
    AT_SMALL = AT_PAR2 + align(NP2)
    AT_TEMPS = AT_SMALL + SMALL
    N_TEMPS = align(NCB)
    AT_WORK = AT_TEMPS + N_TEMPS
    AT_SPLIT = AT_WORK + SLOTS * SLOT
    AT_SRC = AT_SPLIT + 4 * SLOT
    AT_HID = AT_SRC + 2 * KD * T
    AT_BIG = AT_WORK + 53 * T
    AT_MIX = AT_BIG + align(M_IN * (T + 1))

    def __init__(self, nc, ctx, dram):
        self.nc, self.dram, self.phases, self.products = nc, dram, Phases(nc), 0
        base = -(-nc.sbuf_base // 32) * 32
        at = lambda name, shape, offset, dt=F32: nc.alloc_sbuf_tensor_at(name, shape, dt, offset=base + 4 * offset)
        self.x = at("x_res", [P, KD, T], self.AT_X)
        self.const = at("const", [P, NCA], self.AT_FIXED)
        self.par1 = at("par1", [P, NP1], self.AT_PAR1)
        self.par2 = at("par2", [P, NP2], self.AT_PAR2)
        self.small = at("small", [P, self.SMALL], self.AT_SMALL)
        temps = at("temps", [P, self.N_TEMPS], self.AT_TEMPS)
        self.temps = temps[:, 0:8 * T].rearrange("p (n t) -> p n t", t=T)
        self.gate_room = temps[:, 6 * T:6 * T + 2 * (T + 2)].rearrange("p (s t) -> p s t", s=2)
        self.masks = at("masks", [P, NCB], self.AT_TEMPS)
        self.raw = at("raw_tiles", [P, self.SLOTS, self.SLOT], self.AT_WORK)
        self.tile_hi = at("tile_hi", [P, 2, self.SLOT], self.AT_SPLIT, F32R)
        self.tile_lo = at("tile_lo", [P, 2, self.SLOT], self.AT_SPLIT + 2 * self.SLOT, F32R)
        self.src_hi = at("src_hi", [P, KD, T], self.AT_SRC, F32R)
        self.src_lo = at("src_lo", [P, KD, T], self.AT_SRC + KD * T, F32R)
        self.hid_hi = at("hid_hi", [P, KF, T], self.AT_HID, F32R)
        self.hid_lo = at("hid_lo", [P, KF, T], self.AT_HID + KF * T, F32R)
        self.arena = at("arena", [P, 34 * T], self.AT_WORK)
        self.hspace = at("hspace", [P, 8 * T], self.AT_WORK + 34 * T)
        self.ring = at("ring", [P, 11 * T], self.AT_WORK + 42 * T)
        self.big = at("big", [P, M_IN * (T + 1)], self.AT_BIG)
        self.mix = at("mix", [P, KD, T], self.AT_MIX)
        assert 8 * T + 4 <= self.N_TEMPS and self.AT_HID + 2 * KF * T <= self.AT_MIX + KD * T
        assert self.AT_BIG >= self.AT_HID
        assert base + 4 * (self.AT_MIX + KD * T) <= nc.sbuf_usable_end, (base + 4 * (self.AT_MIX + KD * T), nc.sbuf_usable_end)
        self.banks = [ctx.enter_context(nc.psum_tensor(f"bank{i}", [P, T], F32)) for i in range(8)]
        self.slot_sems = [[ctx.enter_context(nc.semaphore(f"raw_slot{r}_{s}", num=100 + 4 * s + r)) for r in range(4)] for s in range(2)]
        self.proj = self.big[:, :].rearrange("p (m t) -> p m t", t=T + 1)
        self.squares = self.temps[:, 7, :]
        self.mem_squares = self.temps[:, 6, :]

    def c(self, name, n=1, rows=P, at=0):
        if name in CA:
            return self.const[0:rows, CA[name] + at:CA[name] + at + n]
        return self.masks[0:rows, CB[name] + at:CB[name] + at + n]

    def units(self, *where):
        mem, first, n = where
        flat = {"arena": self.arena, "big": self.big, "ring": self.ring, "h": self.hspace}[mem]
        return flat[:, first * T:(first + n) * T].rearrange("p (n t) -> p n t", t=T)

    def load_start(self):
        dram = self.dram
        with self.phases.phase("loaded") as (block, loaded):
            @block.sync
            def _(sp):
                sp.dma_start(self.x[:, :, :], dram["x"]).then_inc(loaded, 16)
                sp.dma_start(self.const[:, :], dram["consts"]).then_inc(loaded, 16)
                sp.dma_start(self.par2[:, :], dram["par2"]).then_inc(loaded, 16)
                sp.wait_ge(loaded, 48)
        self.sum_squares()

    def load_layer(self, layer):
        with self.phases.phase("loaded") as (block, loaded):
            @block.sync
            def _(sp):
                src = self.dram["par1"][bass.ds(layer, 1), :, :].rearrange("a p c -> p (a c)")
                sp.dma_start(self.par1[:, :], src).then_inc(loaded, 16)
                sp.wait_ge(loaded, 16)

    def load_masks(self):
        with self.phases.phase("loaded") as (block, loaded):
            @block.sync
            def _(sp):
                sp.dma_start(self.masks[:, :], self.dram["masks"]).then_inc(loaded, 16)
                sp.wait_ge(loaded, 16)

    def sum_squares(self):
        nc = self.nc
        with self.phases.phase("squared", "added") as (block, squared, added):
            @block.scalar
            def _(act):
                for k in range(KD):
                    if k >= 2:
                        act.wait_ge(added, k - 1)
                    nc.scalar.activation(self.temps[:, k % 2, :], self.x[:, k, :], ACT.Square).then_inc(squared, 1)

            @block.vector
            def _(dve):
                for k in range(KD):
                    dve.wait_ge(squared, k + 1)
                    if k == 0:
                        nc.vector.tensor_copy(self.squares, self.temps[:, 0, :]).then_inc(added, 1)
                    else:
                        dve.wait_ge(added, k)
                        nc.vector.tensor_tensor(self.squares, self.squares, self.temps[:, k % 2, :], ALU.add).then_inc(added, 1)

    def weight_part(self, name, first, j):
        at = j + first
        src = self.dram[name][at:at + 1, :, :] if isinstance(at, int) else self.dram[name][bass.ds(at, 1), :, :]
        return src.rearrange("a p c -> p (a c)")

    def product(self, weights, m, h, source, finish_act, finish_dve, norm=None, split=None, n=T,
                prefetched=False, then=None, own=(), begin_dve=None, separate=False, clear=None):
        nc, banks, R = self.nc, self.banks, self.SLOTS
        name, first, kc = weights
        hi, lo = source
        parts = m * h
        landed = self.slot_sems[self.products % 2]
        landed_next = self.slot_sems[(self.products + 1) % 2]
        self.products += 1
        sq, logm, rstd, fresh = self.temps[:, 0:2, 0:n], self.temps[:, 2, 0:n], self.temps[:, 3, 0:n], self.temps[:, 4:6, 0:n]
        squares = self.mem_squares[:, 0:n] if norm is not None and norm[2] else self.squares[:, 0:n]
        tile_banks = lambda u: [banks[2 * (u % 2) + s][:, 0:n] for s in range(h)] if separate else banks[u % 2][:, 0:n]
        names = ("tile_split", "hi_ready", "part_done", "bank_free", "square_ready", "added", "squares_ready", "summed",
                 "logged", "rstd_ready", "fresh_ready", "src_hi_ready", "src_ready", *own)
        with self.phases.phase(*names) as (block, tile_split, hi_ready, part_done, bank_free, square_ready, added,
                                           squares_ready, summed, logged, rstd_ready, fresh_ready, src_hi_ready,
                                           src_ready, *more):
            own = dict(zip(own, more), part_done=part_done, bank_free=bank_free)

            @block.sync
            def _(sp):
                sp.sem_clear(range(landed_next[0].num, landed_next[0].num + R))
                if not prefetched:
                    for j in range(min(R, parts)):
                        sp.dma_start(self.raw[:, j, 0:kc * P], self.weight_part(name, first, j)).then_inc(landed[j], 16)

                def load(j, n_, u):
                    sp.wait_ge(tile_split, j + R + 1)
                    sp.dma_start(self.raw[:, u, 0:kc * P], self.weight_part(name, first, j + R)).then_inc(landed[u], 16)
                if parts > R:
                    repeat(sp, parts - R, R, load)
                if then is not None:
                    name2, first2, kc2 = then
                    assert parts % R == 0
                    for r in range(R):
                        sp.wait_ge(tile_split, parts + r + 1)
                        sp.dma_start(self.raw[:, r, 0:kc2 * P], self.weight_part(name2, first2, r)).then_inc(landed_next[r], 16)

            @block.tensor
            def _(pe):
                pe.sem_inc(part_done, 2)
                if norm is not None:
                    pe.wait_ge(squares_ready, 1)
                    nc.tensor.matmul(banks[7][:, 0:n], self.c("ones", P), squares, start=True, stop=True).then_inc(summed, 1)

                def body(i, n_, u):
                    pe.wait_ge(bank_free, i + 1)
                    for s in range(h):
                        t = (u * h + s) % 2
                        pe.wait_ge(tile_split, i * h + s + 1 + R)
                        bank = tile_banks(u)[s] if separate else tile_banks(u)
                        for k in range(kc):
                            kk = k if separate else s * kc + k
                            if norm is not None or split is not None:
                                pe.wait_ge(src_ready, kk + 1)
                            wh, wl = (w[:, t, k * P:(k + 1) * P] for w in (self.tile_hi, self.tile_lo))
                            nc.tensor.matmul(bank, wh, hi[:, kk, 0:n], start=(kk == 0), stop=False)
                            nc.tensor.matmul(bank, wh, lo[:, kk, 0:n], start=False, stop=False)
                            mm = nc.tensor.matmul(bank, wl, hi[:, kk, 0:n], start=False, stop=(k == kc - 1 and (separate or s == h - 1)))
                        mm.then_inc(part_done, 1)
                repeat(pe, m, 4, body)

            @block.scalar
            def _(act):
                def split_hi(j, t, r, used):
                    act.wait_ge(landed[r], 16 * used)
                    act.wait_ge(part_done, j + 1)
                    nc.scalar.activation(self.tile_hi[:, t, 0:kc * P], self.raw[:, r, 0:kc * P], ACT.Copy).then_inc(hi_ready, 1)

                if norm is not None:
                    x, gain, own_squares = norm
                    if own_squares:
                        for k in range(KD):
                            if k >= 2:
                                act.wait_ge(added, k - 1)
                            nc.scalar.activation(sq[:, k % 2, :], x[:, k, 0:n], ACT.Square).then_inc(square_ready, 1)
                    act.wait_ge(summed, 1)
                    nc.scalar.activation(logm, banks[7][:, 0:n], ACT.Ln, bias=self.c("eps6"), scale=1.0 / D).then_inc(logged, 1)
                    act.wait_ge(logged, 1)
                    nc.scalar.activation(rstd, logm, ACT.Exp, scale=-0.5).then_inc(rstd_ready, 1)
                if norm is not None or split is not None:
                    for k in range(KD):
                        if norm is not None:
                            act.wait_ge(fresh_ready, k + 1)
                        one = fresh[:, k % 2, :] if norm is not None else split[:, k, 0:n]
                        nc.scalar.activation(hi[:, k, 0:n], one, ACT.Copy).then_inc(src_hi_ready, 1)
                        if k == 0:
                            for s in range(h):
                                split_hi(s, s % 2, s % R, 1)
                else:
                    for s in range(h):
                        split_hi(s, s % 2, s % R, 1)

                def body(i, n_, u):
                    for s in range(h):
                        k = (u + 1) * h + s
                        split_hi((i + 1) * h + s, k % 2, k % R, uses(n_, 4 * h, k, R))
                    finish_act(act, i, u, tile_banks(u), own)
                repeat(act, m - 1, 4, body)
                finish_act(act, m - 1, (m - 1) % 4, tile_banks((m - 1) % 4), own)

            @block.vector
            def _(dve):
                v = nc.vector

                def split_lo(j, t, r):
                    dve.wait_ge(hi_ready, j + 1)
                    v.tensor_tensor(self.tile_lo[:, t, 0:kc * P], self.raw[:, r, 0:kc * P],
                                    self.tile_hi[:, t, 0:kc * P].bitcast(F32), ALU.subtract).then_inc(tile_split, 1)

                dve.sem_inc(tile_split, R)
                dve.sem_inc(bank_free, 2)
                if begin_dve is not None:
                    begin_dve(dve, own)
                if norm is not None:
                    x, gain, own_squares = norm
                    if own_squares:
                        for k in range(KD):
                            dve.wait_ge(square_ready, k + 1)
                            if k == 0:
                                v.tensor_copy(squares, sq[:, 0, :]).then_inc(added, 1)
                            else:
                                dve.wait_ge(added, k)
                                v.tensor_tensor(squares, squares, sq[:, k % 2, :], ALU.add).then_inc(added, 1)
                        dve.wait_ge(added, KD)
                    dve.sem_inc(squares_ready, 1)
                    dve.wait_ge(rstd_ready, 1)
                    if clear is not None:
                        v.memset(clear, 0.0).then_inc(own["chain"], 1)
                if norm is not None or split is not None:
                    def fresh_chunk(k):
                        if k >= 2:
                            dve.wait_ge(src_ready, k - 1)
                        v.scalar_tensor_tensor(fresh[:, k % 2, :], x[:, k, 0:n], gain[:, k:k + 1], rstd, ALU.mult, ALU.mult).then_inc(fresh_ready, 1)

                    if norm is not None:
                        fresh_chunk(0)
                    for k in range(KD):
                        if norm is not None and k + 1 < KD:
                            fresh_chunk(k + 1)
                        dve.wait_ge(src_hi_ready, k + 1)
                        one = fresh[:, k % 2, :] if norm is not None else split[:, k, 0:n]
                        v.tensor_tensor(lo[:, k, 0:n], one, hi[:, k, 0:n].bitcast(F32), ALU.subtract).then_inc(src_ready, 1)
                        if k == 0:
                            for s in range(h):
                                split_lo(s, s % 2, s % R)
                else:
                    for s in range(h):
                        split_lo(s, s % 2, s % R)

                def body(i, n_, u):
                    for s in range(h):
                        k = (u + 1) * h + s
                        split_lo((i + 1) * h + s, k % 2, k % R)
                    finish_dve(dve, i, u, tile_banks(u), own)
                repeat(dve, m - 1, 4, body)
                finish_dve(dve, m - 1, (m - 1) % 4, tile_banks((m - 1) % 4), own)

    def project(self, weights, m, dst, norm=None, n=T, prefetched=False, then=None):
        def copy(dve, i, u, bank, own):
            dve.wait_ge(own["part_done"], i + 3)
            self.nc.vector.tensor_copy(chunk(dst[:, :, 0:n], i), bank).then_inc(own["bank_free"], 1)
        self.product(weights, m, 1, (self.src_hi, self.src_lo), lambda *a: None, copy, norm=norm, n=n,
                     prefetched=prefetched, then=then)

    def add_to_residual(self, weights, h, source, factor, split=None, prefetched=False, then=None):
        nc = self.nc

        def square(act, i, u, bank, own):
            act.wait_ge(own["bank_free"], i + 3)
            nc.scalar.activation(self.temps[:, 6, :], chunk(self.x, i), ACT.Square).then_inc(own["x_squared"], 1)

        def add(dve, i, u, bank, own):
            dve.wait_ge(own["part_done"], (i + 1) * h + 2)
            nc.vector.scalar_tensor_tensor(chunk(self.x, i), bank, float(factor), chunk(self.x, i),
                                           ALU.mult, ALU.add).then_inc(own["bank_free"], 1)
            dve.wait_ge(own["x_squared"], i + 1)
            dve.wait_ge(own["sum_done"], i + 1)
            nc.vector.tensor_tensor(self.squares, self.squares, self.temps[:, 6, :], ALU.add).then_inc(own["sum_done"], 1)

        self.product(weights, KD, h, source, square, add, split=split, prefetched=prefetched, then=then,
                     own=("x_squared", "sum_done"),
                     begin_dve=lambda dve, own: nc.vector.memset(self.squares, 0.0).then_inc(own["sum_done"], 1))

    def gated(self, weights, norm, taps=None, tap_bias=None, prefetched=False, then=None):
        nc = self.nc
        opened, conv, prod = self.temps[:, 0:2, :], self.temps[:, 2:4, :], self.temps[:, 4:6, :]
        raw = self.gate_room

        def open_gate(act, i, u, bank, own):
            if taps is None:
                act.wait_ge(own["part_done"], 2 * i + 4)
                nc.scalar.activation(opened[:, u % 2, :], bank[0], ACT.Silu).then_inc(own["activated"], 1)
            else:
                act.wait_ge(own["convolved"], i + 1)
                nc.scalar.activation(opened[:, u % 2, :], conv[:, u % 2, :], ACT.Silu, bias=column(tap_bias, i)).then_inc(own["activated"], 1)
            act.wait_ge(own["bank_free"], i + 3)
            nc.scalar.activation(chunk(self.hid_hi, i), prod[:, u % 2, :], ACT.Copy).then_inc(own["hid_hi_ready"], 1)

        def multiply(dve, i, u, bank, own):
            v = nc.vector
            dve.wait_ge(own["part_done"], 2 * i + 4)
            if taps is not None:
                chain = own["chain"]
                u2 = u % 2
                v.tensor_copy(raw[:, u2, 2:T + 2], bank[0]).then_inc(chain, 1)
                dve.wait_ge(chain, 3 * i + 2)
                v.tensor_scalar(conv[:, u2, :], raw[:, u2, 0:T], column(taps[0], i), None, ALU.mult).then_inc(chain, 1)
                dve.wait_ge(chain, 3 * i + 3)
                v.scalar_tensor_tensor(conv[:, u2, :], raw[:, u2, 1:T + 1], column(taps[1], i), conv[:, u2, :],
                                       ALU.mult, ALU.add).then_inc(chain, 1)
                dve.wait_ge(chain, 3 * i + 4)
                v.scalar_tensor_tensor(conv[:, u2, :], raw[:, u2, 2:T + 2], column(taps[2], i), conv[:, u2, :],
                                       ALU.mult, ALU.add).then_inc(own["convolved"], 1)
            dve.wait_ge(own["activated"], i + 1)
            v.tensor_tensor(prod[:, u % 2, :], opened[:, u % 2, :], bank[1], ALU.mult).then_inc(own["bank_free"], 1)
            dve.wait_ge(own["hid_hi_ready"], i + 1)
            v.tensor_tensor(chunk(self.hid_lo, i), prod[:, u % 2, :], chunk(self.hid_hi, i).bitcast(F32), ALU.subtract)

        self.product(weights, KF, 2, (self.src_hi, self.src_lo), open_gate, multiply, norm=norm,
                     prefetched=prefetched, then=then, separate=True, own=("activated", "convolved", "chain", "hid_hi_ready"),
                     clear=raw[:, :, 0:2] if taps is not None else None)

    def ffn(self, gain, gate_up, down, factor, taps=None, tap_bias=None, prefetched=False, then=None):
        self.gated(gate_up, (self.x, gain, False), taps, tap_bias, prefetched, down)
        self.add_to_residual(down, 2, (self.hid_hi, self.hid_lo), factor, None, True, then)

    def transposes(self, groups):
        nc, banks = self.nc, self.banks
        with self.phases.phase("turned", "copied_a", "copied_v") as (block, turned, copied_a, copied_v):
            def shape(g):
                blocks, out = groups[g]
                rows, cols = out.shape[0], out.shape[2]
                return banks[g % 4][0:rows, 0:len(blocks) * cols], rows, cols

            @block.tensor
            def _(pe):
                for g, (blocks, out) in enumerate(groups):
                    if g >= 4:
                        pe.wait_ge(copied_v if g % 2 else copied_a, (g - 4) // 2 + 1)
                    bank, rows, cols = shape(g)
                    for j, b in enumerate(blocks):
                        t = nc.tensor.transpose(bank[:, j * cols:(j + 1) * cols], b, self.c("ident", cols, cols))
                    t.then_inc(turned, 1)

            @block.scalar
            def _(act):
                for g in range(0, len(groups), 2):
                    act.wait_ge(turned, g + 1)
                    bank, rows, cols = shape(g)
                    nc.scalar.activation(groups[g][1], bank.rearrange("p (n c) -> p n c", c=cols),
                                         ACT.Copy).then_inc(copied_a, 1)

            @block.vector
            def _(dve):
                for g in range(1, len(groups), 2):
                    dve.wait_ge(turned, g + 1)
                    bank, rows, cols = shape(g)
                    nc.vector.tensor_copy(groups[g][1], bank.rearrange("p (n c) -> p n c", c=cols)).then_inc(copied_v, 1)

    def to_tokens(self, src_chunks, dst):
        nt = src_chunks[0].shape[1] // P
        return [([s[:, i * P:(i + 1) * P] for i in range(nt)], dst[:, :, c * P:(c + 1) * P])
                for c, s in enumerate(src_chunks)]

    def to_features(self, src, dst_chunks, first=0):
        return [([src[:, i, (first + c) * P:(first + c + 1) * P] for i in range(NT)],
                 d.rearrange("p (n t) -> p n t", t=P)) for c, d in enumerate(dst_chunks)]

    def head_norm(self, items, div, eps):
        nc, banks = self.nc, self.banks
        n = len(items)
        sq = self.units("ring", 0, 2)
        lg = self.units("ring", 2, 2)
        rs = self.units("ring", 4, 2)
        with self.phases.phase("squared", "summed", "logged", "rstd_ready", "normed") as (
                block, squared, summed, logged, rstd_ready, normed):
            @block.scalar
            def _(act):
                for k in range(n + 1):
                    if k < n:
                        if k >= 2:
                            act.wait_ge(summed, k - 1)
                        nc.scalar.activation(sq[:, k % 2, :], items[k][0], ACT.Square,
                                             scale=items[k][3]).then_inc(squared, 1)
                    if k >= 1:
                        j = k - 1
                        act.wait_ge(summed, j + 1)
                        if j >= 2:
                            act.wait_ge(rstd_ready, j - 1)
                        nc.scalar.activation(lg[:, j % 2, :], banks[j % 2][:, :], ACT.Ln, bias=self.c(eps),
                                             scale=1.0 / div).then_inc(logged, 1)
                        act.wait_ge(logged, j + 1)
                        if j >= 2:
                            act.wait_ge(normed, j - 1)
                        nc.scalar.activation(rs[:, j % 2, :], lg[:, j % 2, :], ACT.Exp, scale=-0.5).then_inc(rstd_ready, 1)

            @block.tensor
            def _(pe):
                for k in range(n):
                    pe.wait_ge(squared, k + 1)
                    if k >= 2:
                        pe.wait_ge(logged, k - 1)
                    nc.tensor.matmul(banks[k % 2][:, :], self.c("head", P), sq[:, k % 2, :],
                                     start=True, stop=True).then_inc(summed, 1)

            @block.vector
            def _(dve):
                for k, (src, gain, dst, _) in enumerate(items):
                    dve.wait_ge(rstd_ready, k + 1)
                    nc.vector.scalar_tensor_tensor(dst, src, gain, rs[:, k % 2, :], ALU.mult, ALU.mult).then_inc(normed, 1)

    def attention(self, tiles, scale):
        nc, banks = self.nc, self.banks
        n = len(tiles)
        S = self.units("ring", 0, 2)
        E = self.units("ring", 2, 2)
        ET = self.units("ring", 4, 2)
        top, ntop, den, rec = (self.small[:, i * 100:i * 100 + 100] for i in range(4))
        NEG_ROW = -1e20
        names = ("scored", "biased", "top_ready", "exped", "turned", "turned_copied", "weighed", "chain", "out_done")
        assert n <= 100
        keys = [t["k"].shape[1] for t in tiles]
        parts = [[(j * P, min(P, m - j * P)) for j in range(-(-m // P))] for m in keys]
        with self.phases.phase(*names) as (block, scored, biased, top_ready, exped, turned, turned_copied, weighed, chain, out_done):
            @block.tensor
            def _(pe):
                for s in range(n + 2):
                    if s < n:
                        if s >= 2:
                            pe.wait_ge(biased, s - 1)
                        nc.tensor.matmul(banks[s % 2][:, 0:keys[s]], tiles[s]["q"], tiles[s]["k"],
                                         start=True, stop=True).then_inc(scored, 1)
                    if 1 <= s <= n:
                        j = s - 1
                        pe.wait_ge(exped, j + 1)
                        if j >= 2:
                            pe.wait_ge(turned_copied, j - 1)
                        for a, w in parts[j]:
                            mm = nc.tensor.transpose(banks[2 + j % 2][0:w, a:a + P], E[:, j % 2, a:a + w], self.c("ident", P))
                        mm.then_inc(turned, 1)
                    if s >= 2:
                        j = s - 2
                        pe.wait_ge(turned_copied, j + 1)
                        if j >= 2:
                            pe.wait_ge(out_done, j - 1)
                        dv = tiles[j]["out"].shape[1]
                        for i, (a, w) in enumerate(parts[j]):
                            mm = nc.tensor.matmul(banks[4 + j % 2][:, 0:dv], ET[0:w, j % 2, a:a + P], tiles[j]["v"][i],
                                                  start=(i == 0), stop=(i == len(parts[j]) - 1))
                        mm.then_inc(weighed, 1)

            @block.scalar
            def _(act):
                for s in range(n + 1):
                    if s < n:
                        act.wait_ge(top_ready, s + 1)
                        if s >= 2:
                            act.wait_ge(turned, s - 1)
                        nc.scalar.activation(E[:, s % 2, 0:keys[s]], S[:, s % 2, 0:keys[s]], ACT.Exp,
                                             bias=ntop[:, s:s + 1], accum_out=den[:, s:s + 1]).then_inc(exped, 1)
                    if s >= 1:
                        j = s - 1
                        act.wait_ge(turned, j + 1)
                        if j >= 2:
                            act.wait_ge(weighed, j - 1)
                        w = min(P, keys[j])
                        m = len(parts[j]) * P
                        nc.scalar.activation(ET[0:w, j % 2, 0:m], banks[2 + j % 2][0:w, 0:m], ACT.Copy).then_inc(turned_copied, 1)

            @block.vector
            def _(dve):
                links = 0
                for s in range(n + 2):
                    if s < n:
                        dve.wait_ge(scored, s + 1)
                        if s >= 2:
                            dve.wait_ge(exped, s - 1)
                        nc.vector.tensor_tensor_reduce(
                            out=S[:, s % 2, 0:keys[s]], in0=banks[s % 2][:, 0:keys[s]], in1=tiles[s]["bias"],
                            scale=scale, scalar=NEG_ROW, op0=ALU.add, op1=ALU.max,
                            accum_out=top[:, s:s + 1]).then_inc(biased, 1)
                        dve.wait_ge(biased, s + 1)
                        nc.vector.tensor_scalar(ntop[:, s:s + 1], top[:, s:s + 1], -1.0, None, ALU.mult).then_inc(top_ready, 1)
                    if s >= 2:
                        j = s - 2
                        t = tiles[j]
                        dve.wait_ge(weighed, j + 1)
                        nc.vector.tensor_scalar(rec[:, j:j + 1], den[:, j:j + 1], 1e-30, None, ALU.max).then_inc(chain, 1)
                        links += 1
                        dve.wait_ge(chain, links)
                        nc.vector.reciprocal(rec[:, j:j + 1], rec[:, j:j + 1]).then_inc(chain, 1)
                        links += 1
                        dve.wait_ge(chain, links)
                        if t.get("gate") is not None:
                            nc.vector.tensor_tensor(rec[:, j:j + 1], rec[:, j:j + 1], t["gate"], ALU.mult).then_inc(chain, 1)
                            links += 1
                            dve.wait_ge(chain, links)
                        dv = t["out"].shape[1]
                        if t.get("add"):
                            if t["after"] is not None:
                                dve.wait_ge(out_done, t["after"] + 1)
                            nc.vector.scalar_tensor_tensor(t["out"], banks[4 + j % 2][:, 0:dv], rec[:, j:j + 1], t["out"],
                                                           ALU.mult, ALU.add).then_inc(out_done, 1)
                        else:
                            nc.vector.tensor_scalar(t["out"], banks[4 + j % 2][:, 0:dv], rec[:, j:j + 1], None,
                                                    ALU.mult).then_inc(out_done, 1)

    def pause(self):
        with self.phases.phase("unused"):
            pass

    def vector_phase(self, work):
        with self.phases.phase("step") as (block, step):
            @block.vector
            def _(dve):
                for n, do in enumerate(work):
                    if n:
                        dve.wait_ge(step, n)
                    do(self.nc.vector).then_inc(step, 1)

    def p1(self, name, at=0, n=1):
        a = PC1[name] + at
        return self.par1[:, a:a + n]

    def pj(self, c):
        return self.proj[:, c, 1:T + 1]

    def token_shift(self):
        nc = self.nc
        diff = self.units("h", 0, 4)
        with self.phases.phase("diff_ready", "shifted") as (block, diff_ready, shifted):
            @block.vector
            def _(dve):
                for c in range(12):
                    if c < 10:
                        if c >= 4:
                            dve.wait_ge(shifted, c - 3)
                        nc.vector.tensor_tensor(diff[:, c % 4, :], self.proj[:, c, 0:T], self.pj(c),
                                                ALU.subtract).then_inc(diff_ready, 1)
                    if c >= 2:
                        dve.wait_ge(diff_ready, c - 1)
                        nc.vector.scalar_tensor_tensor(self.pj(c - 2), diff[:, (c - 2) % 4, :], self.p1("mu", c - 2),
                                                       self.pj(c - 2), ALU.mult, ALU.add).then_inc(shifted, 1)

    def rwkv_gates(self):
        nc, banks = self.nc, self.banks
        x9, low = self.pj(9), self.units("h", 0, 1)[:, 0, :]
        lora = lambda a, b, c: self.par1[a:b, PC1["lora"] + c * P:PC1["lora"] + (c + 1) * P]
        sigw, a, g = self.units("arena", 0, 3), self.units("arena", 3, 3), [self.pj(16 + c) for c in range(RW)]
        with self.phases.phase("low_ready", "gate_product", "gates_read") as (block, low_ready, gate_product, gates_read):
            @block.scalar
            def _(act):
                nc.scalar.activation(low[0:32, :], x9[0:32, :], ACT.Tanh).then_inc(low_ready, 1)
                nc.scalar.activation(low[64:128, :], x9[64:128, :], ACT.Sigmoid).then_inc(low_ready, 1)
                for c in range(RW):
                    b = 3 * (c % 2)
                    act.wait_ge(gate_product, c + 1)
                    nc.scalar.activation(sigw[:, c, :], banks[b][:, :], ACT.Sigmoid, bias=self.p1("w0", c)).then_inc(gates_read, 1)
                    nc.scalar.activation(a[:, c, :], banks[b + 1][:, :], ACT.Sigmoid, bias=self.p1("a0", c)).then_inc(gates_read, 1)

            @block.vector
            def _(dve):
                nc.vector.tensor_copy(low[32:64, :], x9[32:64, :]).then_inc(low_ready, 1)
                for c in range(RW):
                    dve.wait_ge(gate_product, c + 1)
                    nc.vector.tensor_copy(g[c], banks[3 * (c % 2) + 2][:, :]).then_inc(gates_read, 1)

            @block.tensor
            def _(pe):
                pe.wait_ge(low_ready, 3)
                for c in range(RW):
                    b = 3 * (c % 2)
                    if c >= 2:
                        pe.wait_ge(gates_read, 6)
                    nc.tensor.matmul(banks[b][:, :], lora(0, 32, c), low[0:32, :], start=True, stop=True)
                    nc.tensor.matmul(banks[b + 1][:, :], lora(32, 64, c), low[32:64, :], start=True, stop=True)
                    nc.tensor.matmul(banks[b + 2][:, :], lora(64, 128, c), low[64:128, :], start=True, stop=True).then_inc(gate_product, 1)

    def rwkv_scale(self):
        nc, banks = self.nc, self.banks
        sigw, a, bonus = self.units("arena", 0, 3), self.units("arena", 3, 3), self.units("arena", 6, 3)
        cum, before, e_in, e_before, e_out, t1, rk = (self.units("h", i, 1)[:, 0, :] for i in range(1, 8))
        kappa = math.exp(-0.5)
        ends = self.small[:, 0:RW * NCH].rearrange("p (c n) -> p c n", c=RW)
        names = ("chain", "sums_ready", "exps_ready", "bonus_in", "bonus_sum", "chunk_done")
        with self.phases.phase(*names) as (block, chain, sums_ready, exps_ready, bonus_in, bonus_sum, chunk_done):
            @block.scalar
            def _(act):
                for c in range(RW):
                    act.wait_ge(sums_ready, c + 1)
                    if c:
                        act.wait_ge(chunk_done, c)
                    nc.scalar.activation(e_in, cum, ACT.Exp, scale=-kappa)
                    nc.scalar.activation(e_before, before, ACT.Exp, scale=-kappa)
                    nc.scalar.activation(e_out, cum, ACT.Exp, scale=kappa).then_inc(exps_ready, 1)

            @block.tensor
            def _(pe):
                for c in range(RW):
                    pe.wait_ge(bonus_in, c + 1)
                    nc.tensor.matmul(banks[c][:, :], self.c("head", P), rk, start=True, stop=True).then_inc(bonus_sum, 1)

            @block.vector
            def _(dve):
                v = nc.vector
                for c in range(RW):
                    r, k, val, at, bt = self.pj(c), self.pj(3 + c), self.pj(6 + c), self.pj(10 + c), self.pj(13 + c)
                    base = 6 * c
                    if c:
                        dve.wait_ge(chunk_done, c)
                    v.tensor_tensor_scan(cum, self.c("start64", T), sigw[:, c, :], 0.0, ALU.mult, ALU.add).then_inc(chain, 1)
                    v.tensor_scalar(t1, a[:, c, :], -1.0, self.p1("k_a", c), ALU.add, ALU.mult).then_inc(chain, 1)
                    dve.wait_ge(chain, base + 1)
                    v.tensor_tensor(before, cum, sigw[:, c, :], ALU.subtract).then_inc(sums_ready, 1)
                    dve.wait_ge(chain, base + 2)
                    v.scalar_tensor_tensor(k, t1, 1.0, k, ALU.add, ALU.mult).then_inc(chain, 1)
                    v.tensor_tensor(bt, at, a[:, c, :], ALU.mult).then_inc(chain, 1)
                    dve.wait_ge(chain, base + 3)
                    v.scalar_tensor_tensor(rk, r, self.p1("r_k", c), k, ALU.mult, ALU.mult).then_inc(bonus_in, 1)
                    dve.wait_ge(exps_ready, c + 1)
                    dve.wait_ge(chain, base + 4)
                    v.tensor_tensor(bt, bt, e_out, ALU.mult).then_inc(chain, 1)
                    v.scalar_tensor_tensor(at, at, -1.0, e_before, ALU.mult, ALU.mult).then_inc(chain, 1)
                    dve.wait_ge(bonus_in, c + 1)
                    v.tensor_tensor(r, r, e_in, ALU.mult)
                    v.tensor_tensor(k, k, e_out, ALU.mult)
                    v.tensor_copy(ends[:, c, :], e_in[:, CH - 1:T:CH])
                    dve.wait_ge(bonus_sum, c + 1)
                    v.tensor_tensor(bonus[:, c, :], banks[c][:, :], val, ALU.mult).then_inc(chunk_done, 1)

    def rwkv_pair(self, cc):
        nc, banks = self.nc, self.banks
        fa, fb, fr, fk = self.pj(10 + cc), self.pj(13 + cc), self.pj(cc), self.pj(3 + cc)
        At, Kt, Vt = (self.units("ring", i, 1)[:, 0, :] for i in range(3))
        Bt = self.units("arena", cc, 1)[:, 0, :]
        tok = lambda u: u.rearrange("p (n f) -> p n f", f=P)
        self.transposes([g for src, dst in ((fa, At), (fk, Kt), (self.pj(6 + cc), Vt), (fb, Bt))
                         for g in self.to_tokens([src], tok(dst))])
        buffers = [[self.units("h", i, 1)[:, 0, :] for i in range(8)], [self.units("ring", 3 + i, 1)[:, 0, :] for i in range(8)]]
        (L, LT, L2, L2T, I, IT, O32, O64) = zip(*buffers)
        UT, W, MV = (self.units("arena", u, 1)[:, 0, :] for u in (3 + cc, 9 + cc, 33))
        KV = self.units("arena", 12 + 2 * cc, 2)
        G = self.units("arena", 18 + 2 * cc, 2)
        RKV = self.units("arena", 24 + cc, 1)[:, 0, :]
        rows = [slice(0, HD), slice(HD, P)]
        tile = lambda u, i: u[:, i * P:(i + 1) * P]
        wide = lambda name: self.c(name, P).unsqueeze(1).to_broadcast([P, NT, P])
        names = ("scores_a", "scores_b", "masked_a", "masked_b", "values", "values_read",
                 "squares", "squares_copied", "updates", "updated", "corner", "corner_copied", "ends", "ends_read")
        with self.phases.phase(*names) as (block, scores_a, scores_b, masked_a, masked_b, values, values_read,
                                           squares, squares_copied, updates, updated, corner, corner_copied, ends, ends_read):
            @block.tensor
            def _(pe):
                def by_tile(bank, lhs, rhs, r=slice(0, P), out=slice(0, P)):
                    for i in range(NT):
                        mm = nc.tensor.matmul(tile(banks[bank][out, :], i), tile(lhs[r, :], i), tile(rhs[r, :], i), start=True, stop=True)
                    return mm
                for e in range(2):
                    by_tile(0 + e, fb, fa, rows[e])
                    by_tile(2 + e, fa, fb, rows[e])
                    by_tile(4 + e, fk, fa, rows[e])
                    by_tile(6 + e, fb, fr, rows[e]).then_inc(scores_a, 1)
                for e in range(2):
                    pe.wait_ge(masked_a, e + 1)
                    by_tile(0 + e, fk, fr, rows[e]).then_inc(scores_b, 1)
                pe.wait_ge(masked_b, 2)
                for e in range(2):
                    for i in range(NT):
                        nc.tensor.matmul(banks[4][:, i * P + e * HD:i * P + e * HD + HD], tile(L2[e], i),
                                         tile(Vt, i)[:, e * HD:e * HD + HD], start=True, stop=True)
                        mm = nc.tensor.matmul(tile(banks[5][rows[e], :], i), tile(Vt, i)[:, e * HD:e * HD + HD],
                                              tile(L2T[e], i), start=True, stop=True)
                mm.then_inc(values, 1)
                pw = [(L, LT), (L2, L2T)]
                pe.wait_ge(values_read, 2)
                for n in range(3):
                    (p, pt), (q, qt) = pw[n % 2], pw[(n + 1) % 2]
                    if n:
                        pe.wait_ge(squares_copied, 4 * n)
                    for e in range(2):
                        by_tile(0 + 2 * e, pt[e], p[e])
                        by_tile(1 + 2 * e, p[e], pt[e]).then_inc(squares, 1)
                    pe.wait_ge(squares_copied, 4 * n + 4)
                    if n:
                        pe.wait_ge(updated, 2 * n)
                    for e in range(2):
                        by_tile(4 + 2 * e, qt[e], I[e])
                        by_tile(5 + 2 * e, q[e], IT[e]).then_inc(updates, 1)
                pe.wait_ge(updated, 6)
                for e in range(2):
                    by_tile(e, O32[e], IT[e]).then_inc(corner, 1)
                pe.wait_ge(corner_copied, 2)
                for e in range(2):
                    by_tile(4 + 2 * e, L[e], I[e])
                    by_tile(5 + 2 * e, I[e], L[e]).then_inc(updates, 1)
                pe.wait_ge(updated, 8)
                for e in range(2):
                    by_tile(e, O64[e], IT[e]).then_inc(corner, 1)
                pe.wait_ge(corner_copied, 4)
                for e in range(2):
                    by_tile(5 + 2 * e, I[e], L[e]).then_inc(updates, 1)
                pe.wait_ge(updated, 10)
                for i in range(NT):
                    for e in range(2):
                        nc.tensor.matmul(tile(banks[0][rows[e], :], i), tile(At, i)[:, e * HD:e * HD + HD], tile(IT[e], i), start=True, stop=True)
                        nc.tensor.matmul(banks[1][:, i * P + e * HD:i * P + e * HD + HD], tile(IT[e], i),
                                         tile(MV, i)[:, e * HD:e * HD + HD], start=True, stop=True)
                for o in range(2):
                    for i in range(NT):
                        mm = nc.tensor.matmul(tile(banks[2 + o], i), tile(Kt[rows[o], :], i), tile(Vt[rows[o], :], i), start=True, stop=True)
                mm.then_inc(ends, 1)

            @block.scalar
            def _(act):
                act.wait_ge(values, 1)
                nc.scalar.activation(RKV, banks[5][:, :], ACT.Copy).then_inc(values_read, 1)
                pw = [(L, LT), (L2, L2T)]
                for n in range(3):
                    q, qt = pw[(n + 1) % 2]
                    for e in range(2):
                        act.wait_ge(squares, 2 * n + e + 1)
                        nc.scalar.activation(q[e], banks[0 + 2 * e][:, :], ACT.Copy).then_inc(squares_copied, 1)
                for n in range(2):
                    for e in range(2):
                        act.wait_ge(corner, 2 * n + e + 1)
                        nc.scalar.activation(L[e], banks[e][:, :], ACT.Copy).then_inc(corner_copied, 1)
                act.wait_ge(ends, 1)
                nc.scalar.activation(UT, banks[0][:, :], ACT.Copy)
                nc.scalar.activation(W, banks[1][:, :], ACT.Copy).then_inc(ends_read, 1)

            @block.vector
            def _(dve):
                v = nc.vector
                for e in range(2):
                    dve.wait_ge(scores_a, e + 1)
                    v.tensor_tensor(tok(LT[e]), tok(banks[0 + e][:, :]), wide("m16T"), ALU.mult)
                    v.tensor_tensor(tok(L[e]), tok(banks[2 + e][:, :]), wide("m16"), ALU.mult)
                    v.tensor_tensor(tok(O32[e]), tok(banks[2 + e][:, :]), wide("m32"), ALU.mult)
                    v.tensor_tensor(tok(O64[e]), tok(banks[2 + e][:, :]), wide("m64"), ALU.mult)
                    v.tensor_tensor(tok(L2[e]), tok(banks[4 + e][:, :]), wide("strictT"), ALU.mult)
                    v.tensor_tensor(tok(G[:, e, :]), tok(banks[6 + e][:, :]), wide("inclT"), ALU.mult).then_inc(masked_a, 1)
                    dve.wait_ge(masked_a, e + 1)
                    v.tensor_tensor(tok(IT[e]), tok(LT[e]), wide("ident"), ALU.add)
                    v.tensor_tensor(tok(I[e]), tok(L[e]), wide("ident"), ALU.add)
                for e in range(2):
                    dve.wait_ge(scores_b, e + 1)
                    v.tensor_tensor(tok(L2T[e]), tok(banks[0 + e][:, :]), wide("inclT"), ALU.mult).then_inc(masked_b, 1)
                dve.wait_ge(values, 1)
                v.tensor_copy(MV, banks[4][:, :]).then_inc(values_read, 1)
                pw = [(L, LT), (L2, L2T)]
                for n in range(3):
                    q, qt = pw[(n + 1) % 2]
                    for e in range(2):
                        dve.wait_ge(squares, 2 * n + e + 1)
                        v.tensor_copy(qt[e], banks[1 + 2 * e][:, :]).then_inc(squares_copied, 1)
                    for e in range(2):
                        dve.wait_ge(updates, 2 * n + e + 1)
                        v.tensor_tensor(I[e], I[e], banks[4 + 2 * e][:, :], ALU.add)
                        v.tensor_tensor(IT[e], IT[e], banks[5 + 2 * e][:, :], ALU.add).then_inc(updated, 1)
                for e in range(2):
                    dve.wait_ge(updates, 6 + e + 1)
                    v.tensor_tensor(I[e], I[e], banks[4 + 2 * e][:, :], ALU.add)
                    v.tensor_tensor(IT[e], IT[e], banks[5 + 2 * e][:, :], ALU.add).then_inc(updated, 1)
                for e in range(2):
                    dve.wait_ge(updates, 8 + e + 1)
                    v.tensor_tensor(IT[e], IT[e], banks[5 + 2 * e][:, :], ALU.add).then_inc(updated, 1)
                dve.wait_ge(ends, 1)
                for o in range(2):
                    v.tensor_tensor(tok(KV[:, o, :]), tok(banks[2 + o][:, :]), wide("head"), ALU.mult)

    def rwkv_states(self):
        nc, banks = self.nc, self.banks
        Bt, UT, W = self.units("arena", 0, 3), self.units("arena", 3, 3), self.units("arena", 9, 3)
        KV, S, SA = self.units("arena", 12, 6), self.units("arena", 27, 6), self.units("ring", 0, 3)
        ends = self.small[:, 0:RW * NCH].rearrange("p (c n) -> p c n", c=RW)
        ends_mask, kept, kept2, change = (self.units("ring", 3 + i, 1)[:, 0, 0:RW * P].rearrange("p (c f) -> p c f", c=RW) for i in range(4))
        state = lambda c: S.rearrange("p u t -> p (u t)")[:, c * RW * P:(c + 1) * RW * P].rearrange("p (c f) -> p c f", c=RW)
        three = lambda bank: bank[:, 0:RW * P].rearrange("p (c f) -> p c f", c=RW)
        with self.phases.phase("state_ready", "sa_product", "sa_ready", "update", "chain") as (
                block, state_ready, sa_product, sa_ready, update, chain):
            @block.tensor
            def _(pe):
                for c in range(NCH):
                    i, o = c // 2, slice(HD * (c % 2), HD * (c % 2) + HD)
                    pe.wait_ge(state_ready, c + 1)
                    for cc in range(RW):
                        mm = nc.tensor.matmul(three(banks[c % 2])[o, cc, :], UT[:, cc, c * CH:(c + 1) * CH], state(c)[:, cc, :],
                                              start=True, stop=True)
                    mm.then_inc(sa_product, 1)
                    if c < NCH - 1:
                        pe.wait_ge(sa_ready, c + 1)
                        for cc in range(RW):
                            mm = nc.tensor.matmul(three(banks[2 + c % 2])[:, cc, :], Bt[o, cc, i * P:(i + 1) * P],
                                                  SA[o, cc, i * P:(i + 1) * P], start=True, stop=True)
                        mm.then_inc(update, 1)

            @block.vector
            def _(dve):
                v = nc.vector
                v.memset(state(0), 0.0).then_inc(state_ready, 1)
                for c in range(NCH):
                    i, o = c // 2, slice(HD * (c % 2), HD * (c % 2) + HD)
                    dve.wait_ge(sa_product, c + 1)
                    v.tensor_tensor(SA[o, :, i * P:(i + 1) * P], three(banks[c % 2])[o, :, :], W[o, :, i * P:(i + 1) * P],
                                    ALU.add).then_inc(sa_ready, 1)
                    if c < NCH - 1:
                        end = ends[:, :, c:c + 1].to_broadcast([P, RW, P])
                        n = 3 * c
                        v.tensor_tensor(ends_mask, self.c("head", P).unsqueeze(1).to_broadcast([P, RW, P]), end, ALU.mult).then_inc(chain, 1)
                        kv = KV.rearrange("p (c o) t -> p c o t", o=2)[:, :, c % 2, i * P:(i + 1) * P]
                        dve.wait_ge(state_ready, c + 1)
                        v.tensor_tensor(kept, state(c), kv, ALU.add).then_inc(chain, 1)
                        dve.wait_ge(chain, n + 2)
                        v.tensor_tensor(kept2, kept, end, ALU.mult)
                        dve.wait_ge(update, c + 1)
                        v.tensor_tensor(change, three(banks[2 + c % 2]), ends_mask, ALU.mult).then_inc(chain, 1)
                        dve.wait_ge(chain, n + 3)
                        v.tensor_tensor(state(c + 1), change, kept2, ALU.add).then_inc(state_ready, 1)

    def rwkv_output(self):
        nc, banks = self.nc, self.banks
        S, SA, G = self.units("arena", 27, 6), self.units("ring", 0, 3), self.units("arena", 18, 6)
        RKV, bonus = self.units("arena", 24, 3), self.units("arena", 6, 3)
        state = lambda c: S.rearrange("p u t -> p (u t)")[:, c * RW * P:(c + 1) * RW * P].rearrange("p (c f) -> p c f", c=RW)
        y, sq, lg = self.units("h", 0, 3), self.units("h", 3, 2), self.units("h", 5, 2)
        rs = self.units("ring", 3, 3)
        names = ("y_product", "y_ready", "mean_sum", "centred", "squared", "var_sum", "logged", "rstd_ready", "chain")
        with self.phases.phase(*names) as (block, y_product, y_ready, mean_sum, centred, squared, var_sum, logged, rstd_ready, chain):
            @block.tensor
            def _(pe):
                for cc in range(RW):
                    for i in range(NT):
                        for c in (2 * i, 2 * i + 1):
                            nc.tensor.matmul(banks[cc][:, c * CH:(c + 1) * CH], state(c)[:, cc, :], self.pj(cc)[:, c * CH:(c + 1) * CH],
                                             start=(c == 0), stop=False, skip_group_check=True)
                        for e in range(2):
                            mm = nc.tensor.matmul(banks[cc][e * HD:(e + 1) * HD, i * P:(i + 1) * P],
                                                  SA[:, cc, i * P + e * HD:i * P + (e + 1) * HD], G[:, 2 * cc + e, i * P:(i + 1) * P],
                                                  start=False, stop=(i == NT - 1), skip_group_check=True)
                    mm.then_inc(y_product, 1)
                for cc in range(RW):
                    pe.wait_ge(y_ready, cc + 1)
                    nc.tensor.matmul(banks[3 + cc % 2][:, :], self.c("head", P), y[:, cc, :], start=True, stop=True).then_inc(mean_sum, 1)
                    pe.wait_ge(squared, cc + 1)
                    nc.tensor.matmul(banks[5 + cc % 2][:, :], self.c("head", P), sq[:, cc % 2, :], start=True, stop=True).then_inc(var_sum, 1)

            @block.scalar
            def _(act):
                for cc in range(RW):
                    act.wait_ge(centred, cc + 1)
                    nc.scalar.activation(sq[:, cc % 2, :], y[:, cc, :], ACT.Square).then_inc(squared, 1)
                    act.wait_ge(var_sum, cc + 1)
                    nc.scalar.activation(lg[:, cc % 2, :], banks[5 + cc % 2][:, :], ACT.Ln, bias=self.c("eps_gn"), scale=1.0 / HD).then_inc(logged, 1)
                    act.wait_ge(logged, cc + 1)
                    nc.scalar.activation(rs[:, cc, :], lg[:, cc % 2, :], ACT.Exp, scale=-0.5).then_inc(rstd_ready, 1)

            @block.vector
            def _(dve):
                v = nc.vector
                for cc in range(RW):
                    dve.wait_ge(y_product, cc + 1)
                    v.tensor_tensor(y[:, cc, :], banks[cc][:, :], RKV[:, cc, :], ALU.add).then_inc(y_ready, 1)
                for cc in range(RW):
                    dve.wait_ge(mean_sum, cc + 1)
                    v.scalar_tensor_tensor(y[:, cc, :], banks[3 + cc % 2][:, :], -1.0 / HD, y[:, cc, :], ALU.mult, ALU.add).then_inc(centred, 1)
                    dve.wait_ge(rstd_ready, cc + 1)
                    v.scalar_tensor_tensor(y[:, cc, :], y[:, cc, :], self.p1("ln_w", cc), rs[:, cc, :], ALU.mult, ALU.mult).then_inc(chain, 1)
                    dve.wait_ge(chain, 2 * cc + 1)
                    v.scalar_tensor_tensor(y[:, cc, :], y[:, cc, :], self.p1("ln_b", cc), bonus[:, cc, :], ALU.add, ALU.add).then_inc(chain, 1)
                    dve.wait_ge(chain, 2 * cc + 2)
                    v.tensor_tensor(self.mix[:, cc, :], y[:, cc, :], self.pj(16 + cc), ALU.mult)

    def dilated_attention(self):
        nc = self.nc
        self.head_norm([(self.pj(10 + c), self.p1("q_norm"), self.pj(10 + c), 1.0) for c in range(AT)]
                       + [(self.pj(13 + c), self.p1("k_norm"), self.pj(13 + c), 1.0) for c in range(AT)], HD, "eps6")
        vt = self.units("arena", 0, 3).rearrange("p u t -> p (u t)").rearrange("p (n f) -> p n f", f=AT * P)
        out = self.units("arena", 3, 3).rearrange("p u t -> p (u t)").rearrange("p (n f) -> p n f", f=AT * P)
        bias = self.units("arena", 6, 6)
        self.transposes(self.to_tokens([self.pj(16 + c) for c in range(AT)], vt))
        self.vector_phase([lambda v, h=h, s=s: v.scalar_tensor_tensor(bias[:, h, :], self.c("dist", T), -8.0 * s,
                                                                    self.c("log_count", T), ALU.mult, ALU.add)
                           for h, s in enumerate(dilated_slopes())])
        tiles = []
        for h in range(2 * AT):
            r = slice(HD * (h % 2), HD * (h % 2) + HD)
            for i in range(NT):
                tiles.append(dict(q=self.pj(10 + h // 2)[r, i * P:(i + 1) * P], k=self.pj(13 + h // 2)[r, 0:(i + 1) * P],
                                  bias=bias[:, h, T - (i + 1) * P:T], v=[vt[:, j, h * HD:(h + 1) * HD] for j in range(i + 1)],
                                  out=out[:, i, h * HD:(h + 1) * HD]))
        self.attention(tiles, HD ** -0.5)
        self.transposes(self.to_features(out, [self.mix[:, RW + c, :] for c in range(AT)]))

    def conv_mixer(self):
        nc, banks = self.nc, self.banks
        pad = TAPS - 1
        z = self.arena[:, 0:CV * (T + pad)].rearrange("p (c t) -> p c t", c=CV)
        sg, acc = self.units("arena", 3, 2), self.units("arena", 5, 2)
        sq, lg, rs = self.units("arena", 7, 2), self.units("arena", 9, 1)[:, 0, :], self.units("arena", 10, 1)[:, 0, :]
        names = ("opened", "z_ready", "tap", "mean_sum", "centred", "squared", "var_sum", "logged", "rstd_ready", "normed")
        with self.phases.phase(*names) as (block, opened, z_ready, tap, mean_sum, centred, squared, var_sum, logged, rstd_ready, normed):
            @block.scalar
            def _(act):
                for c in range(CV):
                    nc.scalar.activation(sg[:, c, :], self.pj(21 + c), ACT.Sigmoid).then_inc(opened, 1)
                for c in range(CV):
                    act.wait_ge(centred, c + 1)
                    nc.scalar.activation(sq[:, c, :], acc[:, c, :], ACT.Square).then_inc(squared, 1)
                act.wait_ge(var_sum, 1)
                nc.scalar.activation(lg, banks[1][:, :], ACT.Ln, bias=self.c("eps5"), scale=1.0 / (CV * P)).then_inc(logged, 1)
                act.wait_ge(logged, 1)
                nc.scalar.activation(rs, lg, ACT.Exp, scale=-0.5).then_inc(rstd_ready, 1)
                for c in range(CV):
                    act.wait_ge(normed, c + 1)
                    nc.scalar.activation(self.mix[:, RW + AT + c, :], acc[:, c, :], ACT.Silu, bias=self.p1("cln_b", c))

            @block.tensor
            def _(pe):
                pe.wait_ge(tap, CV * TAPS)
                for c in range(CV):
                    mm = nc.tensor.matmul(banks[0][:, :], self.c("ones", P), acc[:, c, :], start=(c == 0), stop=(c == CV - 1))
                mm.then_inc(mean_sum, 1)
                for c in range(CV):
                    pe.wait_ge(squared, c + 1)
                    mm = nc.tensor.matmul(banks[1][:, :], self.c("ones", P), sq[:, c, :], start=(c == 0), stop=(c == CV - 1))
                mm.then_inc(var_sum, 1)

            @block.vector
            def _(dve):
                v = nc.vector
                v.memset(z[:, :, 0:pad], 0.0).then_inc(z_ready, 1)
                for c in range(CV):
                    dve.wait_ge(opened, c + 1)
                    v.tensor_tensor(z[:, c, pad:], self.pj(19 + c), sg[:, c, :], ALU.mult).then_inc(z_ready, 1)
                dve.wait_ge(z_ready, 1 + CV)
                for j in range(TAPS):
                    for c in range(CV):
                        w = self.p1("dw", j * CV + c)
                        if j == 0:
                            v.tensor_scalar(acc[:, c, :], z[:, c, 0:T], w, self.p1("dw_b", c), ALU.mult, ALU.add).then_inc(tap, 1)
                        else:
                            dve.wait_ge(tap, CV * (j - 1) + c + 1)
                            v.scalar_tensor_tensor(acc[:, c, :], z[:, c, j:j + T], w, acc[:, c, :], ALU.mult, ALU.add).then_inc(tap, 1)
                dve.wait_ge(mean_sum, 1)
                for c in range(CV):
                    v.scalar_tensor_tensor(acc[:, c, :], banks[0][:, :], -1.0 / (CV * P), acc[:, c, :], ALU.mult, ALU.add).then_inc(centred, 1)
                dve.wait_ge(rstd_ready, 1)
                for c in range(CV):
                    v.scalar_tensor_tensor(acc[:, c, :], acc[:, c, :], self.p1("cln_w", c), rs, ALU.mult, ALU.mult).then_inc(normed, 1)

    def first_layer(self, layer):
        self.load_layer(layer)
        gains = lambda n: self.p1(n, 0, KD)
        down1, down2 = ("down1", layer * 2 * KD, KF // 2), ("down2", layer * 2 * KD, KF // 2)
        w_in, w_out, gu2 = ("w_in", layer * M_IN, KD), ("w_out", layer * KD, KD), ("gu2", layer * 2 * KF, KD)
        self.ffn(gains("norm_ffn1"), ("gu1", layer * 2 * KF, KD), down1, 0.5, then=w_in)
        self.project(w_in, M_IN, self.proj[:, :, 1:T + 1], norm=(self.x, gains("norm_mix"), False), prefetched=True)
        self.vector_phase([lambda v: v.memset(self.proj[:, :, 0:1], 0.0)])
        self.load_masks()
        self.dilated_attention()
        self.conv_mixer()
        self.token_shift()
        self.rwkv_gates()
        self.head_norm([(self.pj(3 + c), self.p1("k_k", c), self.pj(10 + c), self.p1("k_k", c)) for c in range(RW)], 1, "eps12")
        self.rwkv_scale()
        for cc in range(RW):
            self.rwkv_pair(cc)
        self.rwkv_states()
        self.rwkv_output()
        self.add_to_residual(w_out, 1, (self.src_hi, self.src_lo), 1.0, split=self.mix, then=gu2)
        self.ffn(gains("norm_ffn2"), gu2, down2, 0.5, prefetched=True)

    def p2(self, name, at=0, n=1):
        a = PC2[name] + at
        return self.par2[:, a:a + n]

    def memory_kv(self, layer, then):
        with self.phases.phase("loaded") as (block, loaded):
            @block.sync
            def _(sp):
                sp.dma_start(self.mix[:, :, 0:MEM_T], self.dram["mem"]).then_inc(loaded, 16)
                sp.wait_ge(loaded, 16)
        self.project(("w_mem", layer * KD, KD), KD, self.mix, norm=(self.mix, self.p2("g_mem", KD * layer, KD), True),
                     n=MEM_T, prefetched=layer > 0, then=then)
        at = 19 * (T + 1)
        self.mk = self.big[:, at:at + 2 * T].rearrange("p (h t) -> p h t", h=4)
        self.mv = self.big[:, at + 2 * T:at + 4 * T].rearrange("p (n f) -> p n f", f=T)
        self.vector_phase([lambda v: v.tensor_copy(self.mk, self.mix[:, 0:4, 0:MEM_T])])
        self.transposes(self.to_tokens([self.mix[:, 4 + c, 0:MEM_T] for c in range(4)], self.mv))

    def whole_source(self):
        h = self.units("ring", 0, 8)
        self.vector_phase([lambda v, k=k: v.tensor_tensor(h[:, k, :], self.src_hi[:, k, :].bitcast(F32),
                                                          self.src_lo[:, k, :].bitcast(F32), ALU.add) for k in range(KD)])
        return h

    def memory_attention(self, first, out, done):
        tiles = [dict(q=self.pj(first + h)[:, i * P:(i + 1) * P], k=self.mk[:, h, :], bias=self.c("zero", MEM_T),
                      v=[self.mv[:, j, h * P:(h + 1) * P] for j in range(2)], out=out[:, i, h * P:(h + 1) * P])
                 for h in range(4) for i in range(NT)]
        self.attention(tiles, P ** -0.5)
        self.transposes(self.to_features(out, done))

    def gla_decays(self, h):
        nc, banks = self.nc, self.banks
        small = self.pj(17)[:, 0:3 * P]
        alr, z, low, mag, ex, lg, la, cum, ein, eout = (self.units("arena", i, 1)[:, 0, :] for i in range(10))
        kt = self.units("arena", 10, 2)
        ends = self.small[:, 0:2 * NGC].rearrange("p (c n) -> p c n", c=2)
        names = ("loaded", "alr_product", "alr_ready", "z_product", "z_ready", "chain", "magnitude", "exped", "logged",
                 "summed_up", "decays_ready", "chunk_done")
        with self.phases.phase(*names) as (block, loaded, alr_product, alr_ready, z_product, z_ready, chain, magnitude,
                                           exped, logged, summed_up, decays_ready, chunk_done):
            @block.sync
            def _(sp):
                sp.dma_start(small, self.dram["gla_small"]).then_inc(loaded, 16)

            @block.tensor
            def _(pe):
                pe.wait_ge(loaded, 16)
                for k in range(KD):
                    mm = nc.tensor.matmul(banks[0][0:16, :], small[:, 16 * k:16 * k + 16], h[:, k, :], start=(k == 0), stop=(k == KD - 1))
                mm.then_inc(alr_product, 1)
                pe.wait_ge(alr_ready, 1)
                for cc in range(2):
                    nc.tensor.matmul(banks[1 + cc][:, :], small[0:16, P + cc * P:P + (cc + 1) * P], alr[0:16, :], start=True, stop=True).then_inc(z_product, 1)

            @block.scalar
            def _(act):
                for cc in range(2):
                    act.wait_ge(magnitude, cc + 1)
                    nc.scalar.activation(ex, mag, ACT.Exp, scale=-1.0).then_inc(exped, 1)
                    act.wait_ge(exped, cc + 1)
                    nc.scalar.activation(lg, ex, ACT.Ln, bias=self.c("one")).then_inc(logged, 1)
                    act.wait_ge(summed_up, cc + 1)
                    nc.scalar.activation(ein, cum, ACT.Exp, scale=1.0 / 16)
                    nc.scalar.activation(eout, cum, ACT.Exp, scale=-1.0 / 16).then_inc(decays_ready, 1)

            @block.vector
            def _(dve):
                v = nc.vector
                dve.wait_ge(alr_product, 1)
                v.tensor_copy(alr[0:16, :], banks[0][0:16, :]).then_inc(alr_ready, 1)
                for cc in range(2):
                    q, k = self.pj(cc), self.pj(2 + cc)
                    n = 2 * cc
                    dve.wait_ge(z_product, cc + 1)
                    if cc:
                        dve.wait_ge(chunk_done, cc)
                    v.tensor_scalar(z, banks[1 + cc][:, :], self.p2("b_alpha", cc), None, ALU.add).then_inc(z_ready, 1)
                    dve.wait_ge(z_ready, cc + 1)
                    v.tensor_scalar(low, z, 0.0, None, ALU.min)
                    v.scalar_tensor_tensor(mag, z, -1.0, z, ALU.mult, ALU.max).then_inc(magnitude, 1)
                    dve.wait_ge(logged, cc + 1)
                    v.tensor_tensor(la, low, lg, ALU.subtract).then_inc(chain, 1)
                    dve.wait_ge(chain, n + 1)
                    v.tensor_tensor_scan(cum, self.c("start32", T), la, 0.0, ALU.mult, ALU.add).then_inc(summed_up, 1)
                    dve.wait_ge(decays_ready, cc + 1)
                    v.scalar_tensor_tensor(q, q, 0.125, ein, ALU.mult, ALU.mult)
                    v.tensor_tensor(k, k, eout, ALU.mult).then_inc(chain, 1)
                    v.tensor_copy(ends[:, cc, :], ein[:, GC - 1:T:GC])
                    dve.wait_ge(chain, n + 2)
                    v.tensor_tensor(kt[:, cc, :].rearrange("p (c t) -> p c t", t=GC), k.rearrange("p (c t) -> p c t", t=GC),
                                    ein.rearrange("p (c t) -> p c t", t=GC)[:, :, GC - 1:GC].to_broadcast([P, NGC, GC]),
                                    ALU.mult).then_inc(chunk_done, 1)

    def gla_mix(self):
        nc, banks = self.nc, self.banks
        flat = lambda w, f: self.units(*w).rearrange("p u t -> p (u t)").rearrange("p (n f) -> p n f", f=f)
        Vt, Kh = flat(("arena", 0, 4), T), flat(("arena", 4, 2), 2 * P)
        self.transposes(self.to_tokens([self.pj(4 + c) for c in range(4)], Vt)
                        + self.to_tokens([self.units("arena", 10 + c, 1)[:, 0, :] for c in range(2)], Kh))
        S = self.units("arena", 12, 8).rearrange("p u t -> p (u t)").rearrange("p (c n f) -> p c n f", c=2, f=P)
        A = self.units("arena", 20, 4)
        ends = self.small[:, 0:2 * NGC].rearrange("p (c n) -> p c n", c=2)
        rows = [slice(0, HD), slice(HD, P)]
        tile = lambda u, i: u[:, i * P:(i + 1) * P]
        with self.phases.phase("kv_product", "state_ready") as (block, kv_product, state_ready):
            @block.tensor
            def _(pe):
                for cc in range(2):
                    for g in range(4):
                        r = slice(GC * g, GC * g + GC)
                        for i in range(NT):
                            for e in range(2):
                                mm = nc.tensor.matmul(tile(banks[4 * cc + g][rows[e], :], i),
                                                      Kh[r, i, cc * P + e * HD:cc * P + (e + 1) * HD],
                                                      Vt[r, i, (2 * cc + e) * P:(2 * cc + e + 1) * P], start=True, stop=True,
                                                      tile_position=(GC * g, HD * e))
                    mm.then_inc(kv_product, 1)

            @block.vector
            def _(dve):
                v = nc.vector
                v.memset(S[:, :, 0, :], 0.0).then_inc(state_ready, 1)
                dve.wait_ge(kv_product, 2)
                for c in range(NGC - 1):
                    for cc in range(2):
                        dve.wait_ge(state_ready, max(1, 2 * c + cc))
                        v.scalar_tensor_tensor(S[:, cc, c + 1, :], S[:, cc, c, :], ends[:, cc, c:c + 1],
                                               tile(banks[4 * cc + c % 4], c // 4), ALU.mult, ALU.add).then_inc(state_ready, 1)

        o, sr = self.units("arena", 24, 4), self.units("h", 0, 4)
        sq, lg, rs = self.units("ring", 0, 2), self.units("ring", 2, 2), self.units("ring", 4, 2)
        names = ("scores", "masked", "product", "stored", "squared", "summed", "logged", "rstd_ready", "opened", "normed")
        with self.phases.phase(*names) as (block, scores, masked, product, stored, squared, summed, logged, rstd_ready, opened, normed):
            @block.tensor
            def _(pe):
                for h in range(4):
                    cc, r = h // 2, rows[h % 2]
                    for i in range(NT):
                        mm = nc.tensor.matmul(tile(banks[h], i), tile(self.pj(2 + cc)[r, :], i), tile(self.pj(cc)[r, :], i), start=True, stop=True)
                    mm.then_inc(scores, 1)
                for h in range(4):
                    cc, r = h // 2, rows[h % 2]
                    pe.wait_ge(masked, h + 1)
                    for i in range(NT):
                        nc.tensor.matmul(tile(banks[4 + h], i), Vt[:, i, h * P:(h + 1) * P], tile(A[:, h, :], i), start=True, stop=False)
                        for c in range(4 * i, 4 * i + 4):
                            mm = nc.tensor.matmul(banks[4 + h][:, c * GC:(c + 1) * GC], S[r, cc, c, :], self.pj(cc)[r, c * GC:(c + 1) * GC],
                                                  start=False, stop=(c == 4 * i + 3))
                    mm.then_inc(product, 1)
                for h in range(4):
                    pe.wait_ge(squared, h + 1)
                    nc.tensor.matmul(banks[h % 2][:, :], self.c("ones", P), sq[:, h % 2, :], start=True, stop=True).then_inc(summed, 1)

            @block.scalar
            def _(act):
                for h in range(4):
                    nc.scalar.activation(sr[:, h, :], self.pj(8 + h), ACT.Silu).then_inc(opened, 1)
                for h in range(4):
                    act.wait_ge(stored, h + 1)
                    if h >= 2:
                        act.wait_ge(summed, h - 1)
                    nc.scalar.activation(sq[:, h % 2, :], o[:, h, :], ACT.Square).then_inc(squared, 1)
                    act.wait_ge(summed, h + 1)
                    nc.scalar.activation(lg[:, h % 2, :], banks[h % 2][:, :], ACT.Ln, bias=self.c("eps6"), scale=1.0 / P).then_inc(logged, 1)
                    act.wait_ge(logged, h + 1)
                    if h >= 2:
                        act.wait_ge(normed, h - 1)
                    nc.scalar.activation(rs[:, h % 2, :], lg[:, h % 2, :], ACT.Exp, scale=-0.5).then_inc(rstd_ready, 1)

            @block.vector
            def _(dve):
                v = nc.vector
                for h in range(4):
                    dve.wait_ge(scores, h + 1)
                    v.tensor_tensor(A[:, h, :].rearrange("p (n t) -> p n t", t=P), banks[h][:, :].rearrange("p (n t) -> p n t", t=P),
                                    self.c("incl32T", P).unsqueeze(1).to_broadcast([P, NT, P]), ALU.mult).then_inc(masked, 1)
                for h in range(4):
                    dve.wait_ge(product, h + 1)
                    v.tensor_copy(o[:, h, :], banks[4 + h][:, :]).then_inc(stored, 1)
                for h in range(4):
                    dve.wait_ge(rstd_ready, h + 1)
                    v.scalar_tensor_tensor(o[:, h, :], o[:, h, :], self.p2("g_head"), rs[:, h % 2, :], ALU.mult, ALU.mult).then_inc(normed, 1)
                    dve.wait_ge(normed, h + 1)
                    dve.wait_ge(opened, h + 1)
                    v.tensor_tensor(self.mix[:, h, :], o[:, h, :], sr[:, h, :], ALU.mult)

    def gla_layer(self):
        a_in, a_out, gu3 = ("a_in", 0, KD), ("a_out", 0, KD), ("gu3", 0, KD)
        self.memory_kv(0, a_in)
        self.project(a_in, 16, self.proj[:, :, 1:T + 1], norm=(self.x, self.p2("g_mix", 0, KD), False), prefetched=True)
        h = self.whole_source()
        self.load_masks()
        self.gla_decays(h)
        self.gla_mix()
        out = self.units("arena", 0, 4).rearrange("p u t -> p (u t)").rearrange("p (n f) -> p n f", f=T)
        self.memory_attention(12, out, [self.mix[:, 4 + c, :] for c in range(4)])
        self.add_to_residual(a_out, 1, (self.src_hi, self.src_lo), 1.0, split=self.mix, then=gu3)
        self.conv_ffn(0, ("w_mem", KD, KD))

    def conv_ffn(self, layer, then):
        taps = [self.p2("cw", (3 * layer + j) * KF, KF) for j in range(3)]
        self.ffn(self.p2("g_ffn", layer * KD, KD), ("gu3", layer * 2 * KF, KD), ("down3", layer * 2 * KD, KF // 2), 1.0,
                 taps, self.p2("cb", layer * KF, KF), prefetched=True, then=then)

    def compress(self, src, pe_name, weights, w2, out_k, out_v):
        nc, banks = self.nc, self.banks
        GELU = math.sqrt(2.0 / math.pi)
        early, late = self.units("ring", 0, 1)[:, 0, :], self.units("ring", 1, 1)[:, 0, :]
        w = self.arena[:, 8 * T:24 * T].rearrange("p (j f) -> p j f", f=256)
        wb = self.units("ring", 2, 1)[:, 0, 0:P]
        hid, cube, act_in, th, ge = (self.units("ring", 3 + i, 1)[:, 0, 0:4 * 32].rearrange("p (n b) -> p n b", b=32)[:, :, 0:NCMP] for i in range(5))
        names = ("loaded", "shifted", "product", "chain", "argument", "tanh_ready", "gelu_ready", "out_product")
        with self.phases.phase(*names) as (block, loaded, shifted, product, chain, argument, tanh_ready, gelu_ready, out_product):
            @block.sync
            def _(sp):
                for half in range(2):
                    sp.dma_start(w[half * HD:(half + 1) * HD, :, :], self.dram[weights]).then_inc(loaded, 16)
                sp.dma_start(wb, self.dram[w2]).then_inc(loaded, 16)

            @block.tensor
            def _(pe):
                pe.wait_ge(loaded, 48)
                pe.wait_ge(shifted, 2)
                for g in range(2):
                    r = slice(g * HD, (g + 1) * HD)
                    for m in range(2):
                        for j in range(32):
                            tokens = (early if j < 16 else late)[r, j:j + 16 * NCMP - 15:16]
                            mm = nc.tensor.matmul(banks[2 * g + m][:, 0:NCMP], w[r, j, m * P:(m + 1) * P], tokens, start=(j == 0), stop=(j == 31))
                mm.then_inc(product, 1)
                pe.wait_ge(gelu_ready, 1)
                for g in range(2):
                    for m in range(2):
                        if out_k is not None:
                            mm = nc.tensor.matmul(banks[4][g * HD:(g + 1) * HD, 0:NCMP], wb[:, m * HD:(m + 1) * HD], ge[:, 2 * g + m, :],
                                                  start=(m == 0), stop=(m == 1))
                        else:
                            mm = nc.tensor.matmul(banks[4][0:NCMP, g * HD:(g + 1) * HD], ge[:, 2 * g + m, :], wb[:, m * HD:(m + 1) * HD],
                                                  start=(m == 0), stop=(m == 1))
                mm.then_inc(out_product, 1)

            @block.scalar
            def _(act):
                act.wait_ge(argument, 1)
                nc.scalar.activation(th, act_in, ACT.Tanh, scale=GELU).then_inc(tanh_ready, 1)

            @block.vector
            def _(dve):
                v = nc.vector
                both = lambda half: self.p2(pe_name, 16 * half, 16).unsqueeze(1).to_broadcast([P, 32, 16])
                blocks = lambda u: u.rearrange("p (m j) -> p m j", j=16)
                v.tensor_tensor(blocks(early), blocks(src), both(0), ALU.add).then_inc(shifted, 1)
                v.tensor_tensor(blocks(late), blocks(src), both(1), ALU.add).then_inc(shifted, 1)
                dve.wait_ge(product, 1)
                for n in range(4):
                    v.tensor_copy(hid[:, n, :], banks[n][:, 0:NCMP]).then_inc(chain, 1)
                dve.wait_ge(chain, 4)
                v.tensor_tensor(cube, hid, hid, ALU.mult).then_inc(chain, 1)
                dve.wait_ge(chain, 5)
                v.tensor_scalar(cube, cube, 0.044715, 1.0, ALU.mult, ALU.add).then_inc(chain, 1)
                dve.wait_ge(chain, 6)
                v.tensor_tensor(act_in, cube, hid, ALU.mult).then_inc(argument, 1)
                dve.wait_ge(argument, 1)
                v.tensor_scalar(cube, hid, 0.5, None, ALU.mult).then_inc(chain, 1)
                dve.wait_ge(chain, 7)
                dve.wait_ge(tanh_ready, 1)
                v.scalar_tensor_tensor(ge, th, 1.0, cube, ALU.add, ALU.mult).then_inc(gelu_ready, 1)
                dve.wait_ge(out_product, 1)
                if out_k is not None:
                    v.tensor_copy(out_k, banks[4][:, 0:NCMP])
                else:
                    v.tensor_copy(out_v, banks[4][0:NCMP, 0:P])

    def nsa_gates(self, h, gates):
        nc, banks = self.nc, self.banks
        w = self.pj(17)[:, 0:KD * 24].rearrange("p (k c) -> p k c", c=24)
        with self.phases.phase("loaded", "product") as (block, loaded, product):
            @block.sync
            def _(sp):
                sp.dma_start(w, self.dram["w_gates"]).then_inc(loaded, 16)

            @block.tensor
            def _(pe):
                pe.wait_ge(loaded, 16)
                for i in range(NT):
                    for k in range(KD):
                        mm = nc.tensor.matmul(banks[0][:, i * 24:(i + 1) * 24], h[:, k, i * P:(i + 1) * P], w[:, k, :],
                                              start=(k == 0), stop=(k == KD - 1))
                mm.then_inc(product, 1)

            @block.scalar
            def _(act):
                act.wait_ge(product, 1)
                nc.scalar.activation(gates, banks[0][:, 0:NT * 24], ACT.Sigmoid)

    def nsa_layer(self):
        w_kv, b_in = ("w_kv", 0, KD), ("b_in", 0, KD)
        self.memory_kv(1, w_kv)
        at = 10 * (T + 1)
        kv = self.big[:, at:at + 6 * T].rearrange("p (n t) -> p n t", t=T)
        self.project(w_kv, 6, kv, norm=(self.x, self.p2("g_kv", 0, KD), False), prefetched=True)
        self.project(b_in, 8, self.proj[:, :, 1:T + 1], norm=(self.x, self.p2("g_mix", KD, KD), False))
        h = self.whole_source()
        gates_flat = self.small[:, 400:400 + NT * 24]
        self.nsa_gates(h, gates_flat)
        self.load_masks()
        k_cmp, v_cmp = self.pj(9)[:, 0:NCMP], self.pj(9)[0:NCMP, 64:64 + P]
        self.compress(kv[:, 0, :], "pe_k", "w_ck1", "w_ck2", k_cmp, None)
        self.compress(kv[:, 1, :], "pe_v", "w_cv1", "w_cv2", None, v_cmp)
        gate = lambda i, h, b: gates_flat[:, i * 24 + h * 3 + b:i * 24 + h * 3 + b + 1]
        flat = lambda w, f: self.units(*w).rearrange("p u t -> p (u t)").rearrange("p (n f) -> p n f", f=f)
        vs, vw = flat(("arena", 6, 1), P), flat(("arena", 7, 1), P)
        self.transposes(self.to_tokens([kv[:, 3, :]], vs) + self.to_tokens([kv[:, 5, :]], vw))
        out = flat(("arena", 8, 4), T)
        bias = self.units("arena", 12, 8)
        cmp_bias = self.units("arena", 20, 2).rearrange("p u t -> p (u t)")[:, 0:8 * 124].rearrange("p (h c) -> p h c", h=8)
        self.vector_phase(
            [lambda v, h=h, s=s: v.scalar_tensor_tensor(bias[:, h, :], self.c("dist", T), -8.0 * s, self.c("causal", T), ALU.mult, ALU.add)
             for h, s in enumerate(NSA_SLOPES)]
            + [lambda v, h=h, s=s: v.scalar_tensor_tensor(cmp_bias[:, h, :], self.c("cmp_dist", NT * NCMP), -8.0 * s,
                                                          self.c("cmp_mask", NT * NCMP), ALU.mult, ALU.add)
               for h, s in enumerate(NSA_SLOPES)])
        tiles = []
        for h in range(8):
            g = h // 4
            r = slice(HD * g, HD * (g + 1))
            for i in range(NT):
                q, o = self.pj(h % 4)[r, i * P:(i + 1) * P], out[:, i, h * HD:(h + 1) * HD]
                n = len(tiles)
                tiles.append(dict(q=q, k=k_cmp[r, :], bias=cmp_bias[:, h, i * NCMP:(i + 1) * NCMP], v=[v_cmp[:, r]],
                                  out=o, gate=gate(i, h, 0)))
                for b, kk, vv in ((1, kv[:, 2, :], vs), (2, kv[:, 4, :], vw)):
                    tiles.append(dict(q=q, k=kk[r, 0:(i + 1) * P], bias=bias[:, h, T - (i + 1) * P:T],
                                      v=[vv[:, j, HD * g:HD * (g + 1)] for j in range(i + 1)], out=o, gate=gate(i, h, b),
                                      add=True, after=n + b - 1))
        self.attention(tiles, HD ** -0.5)
        self.transposes(self.to_features(out, [self.mix[:, c, :] for c in range(4)]))
        self.memory_attention(4, out, [self.mix[:, 4 + c, :] for c in range(4)])
        self.add_to_residual(("b_out", 0, KD), 1, (self.src_hi, self.src_lo), 1.0, split=self.mix, then=("gu3", 2 * KF, KD))
        self.conv_ffn(1, None)

    def store(self):
        nc = self.nc
        y, logm, rstd = self.units("arena", 0, KD), self.temps[:, 2, :], self.temps[:, 3, :]
        gain = self.p2("g_final", 0, KD)
        with self.phases.phase("summed", "logged", "rstd_ready", "normed", "written") as (
                block, summed, logged, rstd_ready, normed, written):
            @block.tensor
            def _(pe):
                nc.tensor.matmul(self.banks[7][:, :], self.c("ones", P), self.squares, start=True, stop=True).then_inc(summed, 1)

            @block.scalar
            def _(act):
                act.wait_ge(summed, 1)
                nc.scalar.activation(logm, self.banks[7][:, :], ACT.Ln, bias=self.c("eps6"), scale=1.0 / D).then_inc(logged, 1)
                act.wait_ge(logged, 1)
                nc.scalar.activation(rstd, logm, ACT.Exp, scale=-0.5).then_inc(rstd_ready, 1)

            @block.vector
            def _(dve):
                dve.wait_ge(rstd_ready, 1)
                for k in range(KD):
                    nc.vector.scalar_tensor_tensor(y[:, k, :], self.x[:, k, :], gain[:, k:k + 1], rstd,
                                                   ALU.mult, ALU.mult).then_inc(normed, 1)

            @block.sync
            def _(sp):
                for k in range(KD):
                    sp.wait_ge(normed, k + 1)
                    sp.dma_start(self.dram["out"][:, k, :], y[:, k, :]).then_inc(written, 16)
                sp.wait_ge(written, 16 * KD)


def build(nc, dram, parts=3):
    with ExitStack() as ctx:
        core = Core(nc, ctx, dram)
        core.load_start()
        with nc.Fori(0, 2) as layer:
            core.first_layer(layer)
            if core.phases.n % 2:
                core.pause()
        core.gla_layer()
        core.nsa_layer()
        core.store()


def feature_columns(v):
    return np.ascontiguousarray(v.reshape(-1, P).T)


def tiles_of(w, kc):
    n, k, m = w.shape
    t = w.reshape(n, k // (kc * P), kc, P, m // P, P).transpose(0, 4, 1, 3, 2, 5)
    return t.reshape(-1, P, kc * P)


def in_turn(a, b):
    return np.stack([tiles_of(a, KD), tiles_of(b, KD)], axis=1).reshape(-1, P, KD * P)


def layouts(i):
    two = lambda v: np.concatenate([v, v]).reshape(P, 1)
    par1 = []
    for l in range(2):
        cols = [feature_columns(i[n][l]) for n in ("norm_ffn1", "norm_mix", "norm_ffn2", "shift_mu", "rwkv_w0", "rwkv_a0",
                                                    "rwkv_k_k", "rwkv_k_a", "rwkv_r_k", "rwkv_ln_w", "rwkv_ln_b")]
        cols += [two(i["attn_q_norm"][l]), two(i["attn_k_norm"][l])]
        cols += [feature_columns(i[n][l]) for n in ("conv_dw_w", "conv_dw_b", "conv_ln_w", "conv_ln_b")]
        cols += [np.concatenate([i["rwkv_w2"][l], i["rwkv_a2"][l], i["rwkv_g2"][l]])]
        par1.append(np.concatenate(cols, axis=1))
    cols = [feature_columns(i[n]) for n in ("g_mix_2", "g_ffn_2", "g_mem_2", "conv_w_2", "conv_b_2", "a_b_alpha_2",
                                             "a_g_head_2", "g_kv_2", "g_final_2")]
    cols += [np.concatenate([i[n].T, i[n].T]) for n in ("pe_k_2", "pe_v_2")]
    a = i["a_w_in_2"]
    q, mq = i["b_w_in_2"][:, :, 0:512], i["b_w_in_2"][:, :, 536:1048]
    q = q.reshape(1, D, 2, 4, HD).transpose(0, 1, 3, 2, 4).reshape(1, D, 512)
    alr = a[0, :, 1536:1552].reshape(KD, P, 16).transpose(1, 0, 2).reshape(P, P)
    w_alpha = np.concatenate([i["a_w_alpha_2"][0]] * 8)
    halves = lambda w: w.reshape(2, P, HD).transpose(1, 0, 2).reshape(P, P)
    return {
        "consts": constants()[0],
        "masks": constants()[1],
        "x": i["x"][0].T.reshape(KD, P, T).transpose(1, 0, 2),
        "mem": i["mem_2"][0].T.reshape(KD, P, MEM_T).transpose(1, 0, 2),
        "par1": np.stack(par1),
        "par2": np.concatenate(cols, axis=1),
        "gu1": in_turn(i["ffn1_w_gate"], i["ffn1_w_up"]),
        "down1": tiles_of(i["ffn1_w_down"], KF // 2),
        "w_in": tiles_of(i["w_in"], KD),
        "w_out": tiles_of(i["w_out"], KD),
        "gu2": in_turn(i["ffn2_w_gate"], i["ffn2_w_up"]),
        "down2": tiles_of(i["ffn2_w_down"], KF // 2),
        "w_mem": tiles_of(i["w_mem_kv_2"], KD),
        "gu3": in_turn(i["w_up_2"][:, :, 0:FF], i["w_up_2"][:, :, FF:]),
        "down3": tiles_of(i["w_down_2"], KF // 2),
        "a_in": tiles_of(np.concatenate([a[:, :, 0:1536], a[:, :, 1552:]], axis=2), KD),
        "a_out": tiles_of(i["a_w_out_2"], KD),
        "gla_small": np.concatenate([alr, w_alpha], axis=1),
        "w_kv": tiles_of(i["w_kv_2"][None], KD),
        "w_ck1": i["w_ck1_2"].reshape(32, HD, 256).transpose(1, 0, 2),
        "w_ck2": halves(i["w_ck2_2"]),
        "w_cv1": i["w_cv1_2"].reshape(32, HD, 256).transpose(1, 0, 2),
        "w_cv2": halves(i["w_cv2_2"]),
        "w_gates": i["b_w_in_2"][0, :, 512:536].reshape(KD, P, 24).transpose(1, 0, 2),
        "b_in": tiles_of(np.concatenate([q, mq], axis=2), KD),
        "b_out": tiles_of(i["b_w_out_2"], KD),
    }


def kernel(**inputs):
    import concourse.bacc as bacc
    from concourse.bass_utils import run_bass_kernel_spmd

    nc = bacc.Bacc("TRN2", target_bir_lowering=False, num_devices=1)
    arrays = {n: np.ascontiguousarray(a) for n, a in layouts({n: np.asarray(v) for n, v in inputs.items()}).items()}
    dram = {n: nc.dram_tensor(f"in_{n}", a.shape, F32, kind="ExternalInput").ap() for n, a in arrays.items()}
    dram["out"] = nc.dram_tensor("out_x", (P, KD, T), F32, kind="ExternalOutput").ap()
    build(nc, dram)
    r = run_bass_kernel_spmd(nc, [{f"in_{n}": a for n, a in arrays.items()}], core_ids=[0])
    out = np.asarray(r.results[0]["out_x"])
    return out.transpose(2, 1, 0).reshape(1, T, D)
```

```python
import math
from contextlib import ExitStack, contextmanager

import numpy as np

import concourse.bass as bass
from concourse import mybir

F32 = mybir.dt.float32
F32R = mybir.dt.float32r
ALU = mybir.AluOpType
ACT = mybir.ActivationFunctionType
AX = mybir.AxisListType

P = 128
D = 1024
T = 512
NT = T // P
KD = D // P
FF = 2816
KF = FF // P
HD = 64
MEM_T = 256
D_IN = 2944
M_IN = D_IN // P
RW = 3
AT = 3
CV = 2
TAPS = 31
CH = 64
NCH = T // CH
GC = 32
NGC = T // GC
NCMP = 31
NEG = -1e30

def columns(widths):
    at, out = 0, {}
    for name, n in widths:
        out[name] = at
        at += n
    return out, at


PC1, NP1 = columns([
    ("norm_ffn1", KD), ("norm_mix", KD), ("norm_ffn2", KD), ("mu", 10), ("w0", RW), ("a0", RW),
    ("k_k", RW), ("k_a", RW), ("r_k", RW), ("ln_w", RW), ("ln_b", RW), ("q_norm", 1), ("k_norm", 1),
    ("dw", TAPS * CV), ("dw_b", CV), ("cln_w", CV), ("cln_b", CV), ("lora", 3 * P)])
PC2, NP2 = columns([
    ("g_mix", 2 * KD), ("g_ffn", 2 * KD), ("g_mem", 2 * KD), ("cw", 2 * 3 * KF), ("cb", 2 * KF),
    ("b_alpha", 2), ("g_head", 1), ("g_kv", KD), ("g_final", KD), ("pe_k", 32), ("pe_v", 32)])
CA, NCA = columns([("ident", P), ("ones", P), ("head", P), ("eps6", 1), ("eps12", 1), ("eps_gn", 1), ("eps5", 1), ("one", 1)])
CB, NCB = columns([
    ("m16", P), ("m32", P), ("m64", P), ("m16T", P), ("strictT", P), ("inclT", P), ("incl32T", P), ("dist", T),
    ("log_count", T), ("causal", T), ("start64", T), ("start32", T), ("cmp_dist", NT * NCMP),
    ("cmp_mask", NT * NCMP), ("zero", T)])


def constants():
    i = np.arange(P)
    same = lambda n: (i[:, None] // n == i[None, :] // n).astype(np.float32)
    below = (i[:, None] > i[None, :]).astype(np.float32)
    upto = (i[:, None] <= i[None, :]).astype(np.float32)
    dist = (i[:, None] + (T - P) - np.arange(T)[None, :]).astype(np.int64)
    count = (dist <= 128).astype(int) + (dist % 4 == 0) + (dist % 16 == 0)
    count = np.where(dist >= 0, count, 0)
    t = np.arange(T)
    cmp_dist = np.concatenate([(P * b + i)[:, None] - (16 * np.arange(NCMP) + 31)[None, :] for b in range(NT)], axis=1)
    row = lambda v: np.broadcast_to(np.asarray(v, np.float32)[None, :], (P, len(v)))
    col = lambda v: np.full((P, 1), v, np.float32)
    always = [np.eye(P), np.ones((P, P)), same(HD), col(1e-6), col(1e-12), col(64e-5), col(1e-5), col(1.0)]
    mixers = [
        below * same(16), below * (same(32) - same(16)), below * (same(64) - same(32)), (below * same(16)).T,
        (below * same(64)).T, upto * same(64), upto * same(32), dist,
        np.where(count > 0, 8.0 * np.log(np.maximum(count, 1)), NEG), np.where(dist >= 0, 0.0, NEG),
        row(t % CH != 0), row(t % GC != 0), cmp_dist, np.where(cmp_dist >= 0, 0.0, NEG), np.zeros((P, T))]
    return [np.concatenate([np.asarray(p, np.float32) for p in parts], axis=1) for parts in (always, mixers)]


def dilated_slopes():
    pow2 = lambda m: [(2.0 ** (-8.0 / m)) ** (i + 1) for i in range(m)]
    return pow2(4) + pow2(8)[0::2][:2]


NSA_SLOPES = [2.0 ** (-(h + 1)) for h in range(8)]


class Phases:

    FIRST, SIZE = 110, 40

    def __init__(self, nc):
        self.nc, self.n = nc, 0

    @contextmanager
    def phase(self, *names):
        nc = self.nc
        own = self.FIRST + self.SIZE * (self.n % 2)
        other = self.FIRST + self.SIZE * ((self.n + 1) % 2)
        self.n += 1
        assert len(names) <= self.SIZE
        with ExitStack() as ctx:
            sems = [ctx.enter_context(nc.semaphore(f"{n}_{self.n}", num=own + i)) for i, n in enumerate(names)]
            block = ctx.enter_context(nc.Block())

            @block.gpsimd
            def _(pool):
                pool.sem_clear(range(other, other + self.SIZE))

            yield (block, *sems)


def repeat(eng, total, unroll, body):
    whole = total // unroll
    if whole >= 2:
        with eng.Fori(0, whole) as n:
            for u in range(unroll):
                body(n * unroll + u, n, u)
    else:
        whole = 0
    for i in range(whole * unroll, total):
        body(i, i // unroll, i % unroll)


def uses(n, per, k, slots):
    assert per % slots == 0
    return n * (per // slots) + k // slots + 1


def chunk(ap, i):
    if isinstance(i, int):
        return ap[:, i, :]
    return ap[:, bass.ds(i, 1), :].rearrange("p a t -> p (a t)")


def column(ap, i):
    return ap[:, i:i + 1] if isinstance(i, int) else ap[:, bass.ds(i, 1)]


class Core:

    SLOTS = 4
    SLOT = 11 * P
    align = lambda n: -(-n // 8) * 8
    SMALL = 400 + NT * 24
    AT_X = 0
    AT_FIXED = AT_X + KD * T
    AT_PAR1 = AT_FIXED + align(NCA)
    AT_PAR2 = AT_PAR1 + align(NP1)
    AT_SMALL = AT_PAR2 + align(NP2)
    AT_TEMPS = AT_SMALL + SMALL
    N_TEMPS = align(NCB)
    AT_WORK = AT_TEMPS + N_TEMPS
    AT_SPLIT = AT_WORK + SLOTS * SLOT
    AT_SRC = AT_SPLIT + 4 * SLOT
    AT_HID = AT_SRC + 2 * KD * T
    AT_BIG = AT_WORK + 53 * T
    AT_MIX = AT_BIG + align(M_IN * (T + 1))

    def __init__(self, nc, ctx, dram):
        self.nc, self.dram, self.phases, self.products = nc, dram, Phases(nc), 0
        base = -(-nc.sbuf_base // 32) * 32
        at = lambda name, shape, offset, dt=F32: nc.alloc_sbuf_tensor_at(name, shape, dt, offset=base + 4 * offset)
        self.x = at("x_res", [P, KD, T], self.AT_X)
        self.const = at("const", [P, NCA], self.AT_FIXED)
        self.par1 = at("par1", [P, NP1], self.AT_PAR1)
        self.par2 = at("par2", [P, NP2], self.AT_PAR2)
        self.small = at("small", [P, self.SMALL], self.AT_SMALL)
        temps = at("temps", [P, self.N_TEMPS], self.AT_TEMPS)
        self.temps = temps[:, 0:8 * T].rearrange("p (n t) -> p n t", t=T)
        self.gate_room = temps[:, 6 * T:6 * T + 2 * (T + 2)].rearrange("p (s t) -> p s t", s=2)
        self.masks = at("masks", [P, NCB], self.AT_TEMPS)
        self.raw = at("raw_tiles", [P, self.SLOTS, self.SLOT], self.AT_WORK)
        self.tile_hi = at("tile_hi", [P, 2, self.SLOT], self.AT_SPLIT, F32R)
        self.tile_lo = at("tile_lo", [P, 2, self.SLOT], self.AT_SPLIT + 2 * self.SLOT, F32R)
        self.src_hi = at("src_hi", [P, KD, T], self.AT_SRC, F32R)
        self.src_lo = at("src_lo", [P, KD, T], self.AT_SRC + KD * T, F32R)
        self.hid_hi = at("hid_hi", [P, KF, T], self.AT_HID, F32R)
        self.hid_lo = at("hid_lo", [P, KF, T], self.AT_HID + KF * T, F32R)
        self.arena = at("arena", [P, 34 * T], self.AT_WORK)
        self.hspace = at("hspace", [P, 8 * T], self.AT_WORK + 34 * T)
        self.ring = at("ring", [P, 11 * T], self.AT_WORK + 42 * T)
        self.big = at("big", [P, M_IN * (T + 1)], self.AT_BIG)
        self.mix = at("mix", [P, KD, T], self.AT_MIX)
        assert 8 * T + 4 <= self.N_TEMPS and self.AT_HID + 2 * KF * T <= self.AT_MIX + KD * T
        assert self.AT_BIG >= self.AT_HID
        assert base + 4 * (self.AT_MIX + KD * T) <= nc.sbuf_usable_end, (base + 4 * (self.AT_MIX + KD * T), nc.sbuf_usable_end)
        self.banks = [ctx.enter_context(nc.psum_tensor(f"bank{i}", [P, T], F32)) for i in range(8)]
        self.slot_sems = [[ctx.enter_context(nc.semaphore(f"raw_slot{r}_{s}", num=100 + 4 * s + r)) for r in range(4)] for s in range(2)]
        self.proj = self.big[:, :].rearrange("p (m t) -> p m t", t=T + 1)
        self.squares = self.temps[:, 7, :]
        self.kept_rstd = self.hspace[:, 7 * T:8 * T]
        self.mem_squares = self.temps[:, 6, :]

    def c(self, name, n=1, rows=P, at=0):
        if name in CA:
            return self.const[0:rows, CA[name] + at:CA[name] + at + n]
        return self.masks[0:rows, CB[name] + at:CB[name] + at + n]

    def units(self, *where):
        mem, first, n = where
        flat = {"arena": self.arena, "big": self.big, "ring": self.ring, "h": self.hspace}[mem]
        return flat[:, first * T:(first + n) * T].rearrange("p (n t) -> p n t", t=T)

    def load_start(self):
        dram = self.dram
        with self.phases.phase("loaded") as (block, loaded):
            @block.sync
            def _(sp):
                sp.dma_start(self.x[:, :, :], dram["x"]).then_inc(loaded, 16)
                sp.dma_start(self.const[:, :], dram["consts"]).then_inc(loaded, 16)
                sp.dma_start(self.par2[:, :], dram["par2"]).then_inc(loaded, 16)
                sp.wait_ge(loaded, 48)
        self.sum_squares()

    def load_layer(self, layer):
        with self.phases.phase("loaded") as (block, loaded):
            @block.sync
            def _(sp):
                src = self.dram["par1"][bass.ds(layer, 1), :, :].rearrange("a p c -> p (a c)")
                sp.dma_start(self.par1[:, :], src).then_inc(loaded, 16)
                sp.wait_ge(loaded, 16)

    def masks_load(self):
        return self.masks[:, :], self.dram["masks"]

    def sum_squares(self):
        nc = self.nc
        with self.phases.phase("squared", "added") as (block, squared, added):
            @block.scalar
            def _(act):
                for k in range(KD):
                    if k >= 2:
                        act.wait_ge(added, k - 1)
                    nc.scalar.activation(self.temps[:, k % 2, :], self.x[:, k, :], ACT.Square).then_inc(squared, 1)

            @block.vector
            def _(dve):
                for k in range(KD):
                    dve.wait_ge(squared, k + 1)
                    if k == 0:
                        nc.vector.tensor_copy(self.squares, self.temps[:, 0, :]).then_inc(added, 1)
                    else:
                        dve.wait_ge(added, k)
                        nc.vector.tensor_tensor(self.squares, self.squares, self.temps[:, k % 2, :], ALU.add).then_inc(added, 1)

    def weight_part(self, name, first, j):
        at = j + first
        src = self.dram[name][at:at + 1, :, :] if isinstance(at, int) else self.dram[name][bass.ds(at, 1), :, :]
        return src.rearrange("a p c -> p (a c)")

    def product(self, weights, m, h, source, finish_act, finish_dve, norm=None, split=None, n=T,
                prefetched=False, then=None, own=(), begin_dve=None, separate=False, clear=None,
                beside=(), ready_split=False):
        nc, banks, R = self.nc, self.banks, self.SLOTS
        name, first, kc = weights
        hi, lo = source
        parts = m * h
        landed = self.slot_sems[self.products % 2]
        landed_next = self.slot_sems[(self.products + 1) % 2]
        self.products += 1
        sq, fresh = self.temps[:, 0:2, 0:n], self.temps[:, 4:6, 0:n]
        rstd = norm[3][:, 0:n] if norm is not None else None
        make_source = split is not None or (norm is not None and not ready_split)
        squares = self.mem_squares[:, 0:n] if norm is not None and norm[2] else self.squares[:, 0:n]
        tile_banks = lambda u: [banks[2 * (u % 2) + s][:, 0:n] for s in range(h)] if separate else banks[u % 2][:, 0:n]
        names = ("tile_split", "hi_ready", "part_done", "bank_free", "square_ready", "added", "squares_ready", "summed",
                 "logged", "rstd_ready", "fresh_ready", "src_hi_ready", "src_ready", "beside_loaded", *own)
        with self.phases.phase(*names) as (block, tile_split, hi_ready, part_done, bank_free, square_ready, added,
                                           squares_ready, summed, logged, rstd_ready, fresh_ready, src_hi_ready,
                                           src_ready, beside_loaded, *more):
            own = dict(zip(own, more), part_done=part_done, bank_free=bank_free, rstd=rstd, rstd_ready=rstd_ready)

            @block.sync
            def _(sp):
                sp.sem_clear(range(landed_next[0].num, landed_next[0].num + R))
                if not prefetched:
                    for j in range(min(R, parts)):
                        sp.dma_start(self.raw[:, j, 0:kc * P], self.weight_part(name, first, j)).then_inc(landed[j], 16)

                if beside:
                    sp.wait_ge(src_ready, KD)
                    sp.wait_ge(rstd_ready, 1)
                for to, src in beside:
                    sp.dma_start(to, src).then_inc(beside_loaded, 16)

                def load(j, n_, u):
                    sp.wait_ge(tile_split, j + R + 1)
                    sp.dma_start(self.raw[:, u, 0:kc * P], self.weight_part(name, first, j + R)).then_inc(landed[u], 16)
                if parts > R:
                    repeat(sp, parts - R, R, load)
                if then is not None:
                    name2, first2, kc2 = then
                    assert parts % R == 0
                    for r in range(R):
                        sp.wait_ge(tile_split, parts + r + 1)
                        sp.dma_start(self.raw[:, r, 0:kc2 * P], self.weight_part(name2, first2, r)).then_inc(landed_next[r], 16)

                if beside:
                    sp.wait_ge(beside_loaded, 16 * len(beside))

            @block.tensor
            def _(pe):
                pe.sem_inc(part_done, 2)
                if norm is not None:
                    pe.wait_ge(squares_ready, 1)
                    nc.tensor.matmul(banks[7][:, 0:n], self.c("ones", P), squares, start=True, stop=True).then_inc(summed, 1)

                def body(i, n_, u):
                    pe.wait_ge(bank_free, i + 1)
                    for s in range(h):
                        t = (u * h + s) % 2
                        pe.wait_ge(tile_split, i * h + s + 1 + R)
                        bank = tile_banks(u)[s] if separate else tile_banks(u)
                        for k in range(kc):
                            kk = k if separate else s * kc + k
                            if make_source:
                                pe.wait_ge(src_ready, kk + 1)
                            wh, wl = (w[:, t, k * P:(k + 1) * P] for w in (self.tile_hi, self.tile_lo))
                            nc.tensor.matmul(bank, wh, hi[:, kk, 0:n], start=(kk == 0), stop=False)
                            nc.tensor.matmul(bank, wh, lo[:, kk, 0:n], start=False, stop=False)
                            mm = nc.tensor.matmul(bank, wl, hi[:, kk, 0:n], start=False, stop=(k == kc - 1 and (separate or s == h - 1)))
                        mm.then_inc(part_done, 1)
                repeat(pe, m, 4, body)

            @block.scalar
            def _(act):
                def split_hi(j, t, r, used):
                    act.wait_ge(landed[r], 16 * used)
                    act.wait_ge(part_done, j + 1)
                    nc.scalar.activation(self.tile_hi[:, t, 0:kc * P], self.raw[:, r, 0:kc * P], ACT.Copy).then_inc(hi_ready, 1)

                def rstd_now():
                    act.wait_ge(summed, 1)
                    nc.scalar.activation(rstd, banks[7][:, 0:n], ACT.Ln, bias=self.c("eps6"), scale=1.0 / D).then_inc(logged, 1)
                    act.wait_ge(logged, 1)
                    nc.scalar.activation(rstd, rstd, ACT.Exp, scale=-0.5).then_inc(rstd_ready, 1)

                if norm is not None and norm[2]:
                    for k in range(KD):
                        if k >= 2:
                            act.wait_ge(added, k - 1)
                        nc.scalar.activation(sq[:, k % 2, :], norm[0][:, k, 0:n], ACT.Square).then_inc(square_ready, 1)
                if make_source:
                    for k in range(KD):
                        if norm is not None:
                            act.wait_ge(fresh_ready, k + 1)
                        one = fresh[:, k % 2, :] if norm is not None else split[:, k, 0:n]
                        nc.scalar.activation(hi[:, k, 0:n], one, ACT.Copy).then_inc(src_hi_ready, 1)
                        if k == 0:
                            for s in range(h):
                                split_hi(s, s % 2, s % R, 1)
                else:
                    for s in range(h):
                        split_hi(s, s % 2, s % R, 1)
                if norm is not None:
                    rstd_now()

                def body(i, n_, u):
                    for s in range(h):
                        k = (u + 1) * h + s
                        split_hi((i + 1) * h + s, k % 2, k % R, uses(n_, 4 * h, k, R))
                    finish_act(act, i, u, tile_banks(u), own)
                repeat(act, m - 1, 4, body)
                finish_act(act, m - 1, (m - 1) % 4, tile_banks((m - 1) % 4), own)

            @block.vector
            def _(dve):
                v = nc.vector

                def split_lo(j, t, r):
                    dve.wait_ge(hi_ready, j + 1)
                    v.tensor_tensor(self.tile_lo[:, t, 0:kc * P], self.raw[:, r, 0:kc * P],
                                    self.tile_hi[:, t, 0:kc * P].bitcast(F32), ALU.subtract).then_inc(tile_split, 1)

                dve.sem_inc(tile_split, R)
                dve.sem_inc(bank_free, 2)
                if begin_dve is not None:
                    begin_dve(dve, own)
                if norm is not None:
                    x, gain, own_squares = norm[0:3]
                    if own_squares:
                        for k in range(KD):
                            dve.wait_ge(square_ready, k + 1)
                            if k == 0:
                                v.tensor_copy(squares, sq[:, 0, :]).then_inc(added, 1)
                            else:
                                dve.wait_ge(added, k)
                                v.tensor_tensor(squares, squares, sq[:, k % 2, :], ALU.add).then_inc(added, 1)
                        dve.wait_ge(added, KD)
                    dve.sem_inc(squares_ready, 1)
                if make_source:
                    def fresh_chunk(k):
                        if k >= 2:
                            dve.wait_ge(src_ready, k - 1)
                        v.tensor_scalar(fresh[:, k % 2, :], x[:, k, 0:n], gain[:, k:k + 1], None, ALU.mult).then_inc(fresh_ready, 1)

                    if norm is not None:
                        fresh_chunk(0)
                    for k in range(KD):
                        if norm is not None and k + 1 < KD:
                            fresh_chunk(k + 1)
                        dve.wait_ge(src_hi_ready, k + 1)
                        one = fresh[:, k % 2, :] if norm is not None else split[:, k, 0:n]
                        v.tensor_tensor(lo[:, k, 0:n], one, hi[:, k, 0:n].bitcast(F32), ALU.subtract).then_inc(src_ready, 1)
                        if k == 0:
                            for s in range(h):
                                split_lo(s, s % 2, s % R)
                else:
                    dve.sem_inc(src_ready, KD)
                    for s in range(h):
                        split_lo(s, s % 2, s % R)
                if clear is not None:
                    dve.wait_ge(rstd_ready, 1)
                    v.memset(clear, 0.0).then_inc(own["chain"], 1)

                def body(i, n_, u):
                    for s in range(h):
                        k = (u + 1) * h + s
                        split_lo((i + 1) * h + s, k % 2, k % R)
                    finish_dve(dve, i, u, tile_banks(u), own)
                repeat(dve, m - 1, 4, body)
                finish_dve(dve, m - 1, (m - 1) % 4, tile_banks((m - 1) % 4), own)

    def project(self, weights, m, dst, norm=None, n=T, prefetched=False, then=None, beside=(), ready_split=False):
        def scale(dve, i, u, bank, own):
            dve.wait_ge(own["part_done"], i + 3)
            dve.wait_ge(own["rstd_ready"], 1)
            self.nc.vector.tensor_tensor(chunk(dst[:, :, 0:n], i), bank, own["rstd"], ALU.mult).then_inc(own["bank_free"], 1)
        self.product(weights, m, 1, (self.src_hi, self.src_lo), lambda *a: None, scale, norm=(*norm, self.kept_rstd), n=n,
                     prefetched=prefetched, then=then, beside=beside, ready_split=ready_split)

    def add_to_residual(self, weights, h, source, factor, split=None, prefetched=False, then=None, next_gain=None):
        nc = self.nc
        fresh = self.temps[:, 4:6, :]

        def square(act, i, u, bank, own):
            act.wait_ge(own["bank_free"], i + 3)
            nc.scalar.activation(self.temps[:, 6, :], chunk(self.x, i), ACT.Square).then_inc(own["x_squared"], 1)
            if next_gain is not None:
                act.wait_ge(own["next_ready"], i + 1)
                nc.scalar.activation(chunk(self.src_hi, i), fresh[:, u % 2, :], ACT.Copy).then_inc(own["next_hi"], 1)

        def add(dve, i, u, bank, own):
            dve.wait_ge(own["part_done"], (i + 1) * h + 2)
            nc.vector.scalar_tensor_tensor(chunk(self.x, i), bank, float(factor), chunk(self.x, i),
                                           ALU.mult, ALU.add).then_inc(own["bank_free"], 1)
            if next_gain is not None:
                dve.wait_ge(own["bank_free"], i + 3)
                nc.vector.tensor_scalar(fresh[:, u % 2, :], chunk(self.x, i), column(next_gain, i), None, ALU.mult).then_inc(own["next_ready"], 1)
            dve.wait_ge(own["x_squared"], i + 1)
            dve.wait_ge(own["sum_done"], i + 1)
            nc.vector.tensor_tensor(self.squares, self.squares, self.temps[:, 6, :], ALU.add).then_inc(own["sum_done"], 1)
            if next_gain is not None:
                dve.wait_ge(own["next_hi"], i + 1)
                nc.vector.tensor_tensor(chunk(self.src_lo, i), fresh[:, u % 2, :], chunk(self.src_hi, i).bitcast(F32), ALU.subtract).then_inc(own["next_lo"], 1)

        self.product(weights, KD, h, source, square, add, split=split, prefetched=prefetched, then=then,
                     own=("x_squared", "sum_done", "next_ready", "next_hi", "next_lo"),
                     begin_dve=lambda dve, own: nc.vector.memset(self.squares, 0.0).then_inc(own["sum_done"], 1))

    def gated(self, weights, norm, taps=None, tap_bias=None, prefetched=False, then=None, ready_split=False):
        nc = self.nc
        gate, prod = self.temps[:, 0:2, :], self.temps[:, 4:6, :]
        raw = self.gate_room

        def open_gate(act, i, u, bank, own):
            act.wait_ge(own["gate_ready"], i + 1)
            one = gate[:, u % 2, :]
            if taps is None:
                nc.scalar.activation(one, one, ACT.Silu).then_inc(own["activated"], 1)
            else:
                nc.scalar.activation(one, one, ACT.Silu, bias=column(tap_bias, i)).then_inc(own["activated"], 1)
            act.wait_ge(own["prod_ready"], i + 1)
            nc.scalar.activation(chunk(self.hid_hi, i), prod[:, u % 2, :], ACT.Copy).then_inc(own["hid_hi_ready"], 1)

        def multiply(dve, i, u, bank, own):
            v, u2, rstd = nc.vector, u % 2, own["rstd"]
            dve.wait_ge(own["part_done"], 2 * i + 4)
            dve.wait_ge(own["rstd_ready"], 1)
            if taps is None:
                v.tensor_tensor(gate[:, u2, :], bank[0], rstd, ALU.mult).then_inc(own["gate_ready"], 1)
                v.tensor_tensor(prod[:, u2, :], bank[1], rstd, ALU.mult).then_inc(own["bank_free"], 1)
            else:
                chain = own["chain"]
                v.tensor_tensor(raw[:, u2, 2:T + 2], bank[0], rstd, ALU.mult).then_inc(chain, 1)
                v.tensor_tensor(prod[:, u2, :], bank[1], rstd, ALU.mult).then_inc(own["bank_free"], 1)
                dve.wait_ge(chain, 3 * i + 2)
                v.tensor_scalar(gate[:, u2, :], raw[:, u2, 0:T], column(taps[0], i), None, ALU.mult).then_inc(chain, 1)
                dve.wait_ge(chain, 3 * i + 3)
                v.scalar_tensor_tensor(gate[:, u2, :], raw[:, u2, 1:T + 1], column(taps[1], i), gate[:, u2, :],
                                       ALU.mult, ALU.add).then_inc(chain, 1)
                dve.wait_ge(chain, 3 * i + 4)
                v.scalar_tensor_tensor(gate[:, u2, :], raw[:, u2, 2:T + 2], column(taps[2], i), gate[:, u2, :],
                                       ALU.mult, ALU.add).then_inc(own["gate_ready"], 1)
            dve.wait_ge(own["activated"], i + 1)
            dve.wait_ge(own["bank_free"], i + 3)
            v.tensor_tensor(prod[:, u2, :], prod[:, u2, :], gate[:, u2, :], ALU.mult).then_inc(own["prod_ready"], 1)
            dve.wait_ge(own["hid_hi_ready"], i + 1)
            v.tensor_tensor(chunk(self.hid_lo, i), prod[:, u2, :], chunk(self.hid_hi, i).bitcast(F32), ALU.subtract)

        self.product(weights, KF, 2, (self.src_hi, self.src_lo), open_gate, multiply, norm=(*norm, self.temps[:, 2, :]),
                     prefetched=prefetched, then=then, separate=True, ready_split=ready_split,
                     own=("activated", "gate_ready", "prod_ready", "chain", "hid_hi_ready"),
                     clear=raw[:, :, 0:2] if taps is not None else None)

    def ffn(self, gain, gate_up, down, factor, taps=None, tap_bias=None, prefetched=False, then=None,
            ready_split=False, next_gain=None):
        self.gated(gate_up, (self.x, gain, False), taps, tap_bias, prefetched, down, ready_split)
        self.add_to_residual(down, 2, (self.hid_hi, self.hid_lo), factor, None, True, then, next_gain)

    def mixed_source(self):
        return self.hid_hi[:, 0:KD, :], self.hid_lo[:, 0:KD, :]

    def transposes(self, groups):
        nc, banks = self.nc, self.banks
        with self.phases.phase("turned", "copied_a", "copied_v") as (block, turned, copied_a, copied_v):
            def shape(g):
                blocks, out = groups[g]
                rows, cols = out.shape[0], out.shape[2]
                return banks[g % 4][0:rows, 0:len(blocks) * cols], rows, cols

            @block.tensor
            def _(pe):
                for g, (blocks, out) in enumerate(groups):
                    if g >= 4:
                        pe.wait_ge(copied_v if g % 2 else copied_a, (g - 4) // 2 + 1)
                    bank, rows, cols = shape(g)
                    for j, b in enumerate(blocks):
                        t = nc.tensor.transpose(bank[:, j * cols:(j + 1) * cols], b, self.c("ident", cols, cols))
                    t.then_inc(turned, 1)

            @block.scalar
            def _(act):
                for g in range(0, len(groups), 2):
                    act.wait_ge(turned, g + 1)
                    bank, rows, cols = shape(g)
                    nc.scalar.activation(groups[g][1], bank.rearrange("p (n c) -> p n c", c=cols),
                                         ACT.Copy).then_inc(copied_a, 1)

            @block.vector
            def _(dve):
                for g in range(1, len(groups), 2):
                    dve.wait_ge(turned, g + 1)
                    bank, rows, cols = shape(g)
                    nc.vector.tensor_copy(groups[g][1], bank.rearrange("p (n c) -> p n c", c=cols)).then_inc(copied_v, 1)

    def to_tokens(self, src_chunks, dst):
        nt = src_chunks[0].shape[1] // P
        return [([s[:, i * P:(i + 1) * P] for i in range(nt)], dst[:, :, c * P:(c + 1) * P])
                for c, s in enumerate(src_chunks)]

    def to_features(self, src, dst_chunks, first=0):
        return [([src[:, i, (first + c) * P:(first + c + 1) * P] for i in range(NT)],
                 d.rearrange("p (n t) -> p n t", t=P)) for c, d in enumerate(dst_chunks)]

    def head_norm(self, items, div, eps):
        nc, banks = self.nc, self.banks
        n = len(items)
        sq, rs = self.units("ring", 0, 2), self.units("ring", 2, n)
        with self.phases.phase("squared", "summed", "logged", "rstd_ready") as (
                block, squared, summed, logged, rstd_ready):
            @block.scalar
            def _(act):
                for k in range(n):
                    if k >= 2:
                        act.wait_ge(summed, k - 1)
                    nc.scalar.activation(sq[:, k % 2, :], items[k][0], ACT.Square, scale=items[k][3]).then_inc(squared, 1)
                for k in range(n):
                    act.wait_ge(summed, k + 1)
                    nc.scalar.activation(rs[:, k, :], banks[k][:, :], ACT.Ln, bias=self.c(eps), scale=1.0 / div).then_inc(logged, 1)
                for k in range(n):
                    act.wait_ge(logged, k + 1)
                    nc.scalar.activation(rs[:, k, :], rs[:, k, :], ACT.Exp, scale=-0.5).then_inc(rstd_ready, 1)

            @block.tensor
            def _(pe):
                for k in range(n):
                    pe.wait_ge(squared, k + 1)
                    nc.tensor.matmul(banks[k][:, :], self.c("head", P), sq[:, k % 2, :],
                                     start=True, stop=True).then_inc(summed, 1)

            @block.vector
            def _(dve):
                for k, (src, gain, dst, _) in enumerate(items):
                    dve.wait_ge(rstd_ready, k + 1)
                    nc.vector.scalar_tensor_tensor(dst, src, gain, rs[:, k, :], ALU.mult, ALU.mult)

    def attention(self, tiles, scale, beside=None):
        nc, banks = self.nc, self.banks
        n = len(tiles)
        S, E, ET = (self.units("ring", 3 * i, 3) for i in range(3))
        score_bank = lambda s: banks[(0, 1, 6)[s % 3]]
        turn_bank = lambda s: banks[(2, 3, 7)[s % 3]]
        ntop, den, rec = (self.small[:, i * 100:i * 100 + 100] for i in range(3))
        NEG_ROW = -1e20
        names = ("scored", "biased", "exped", "turned", "turned_copied", "weighed", "chain", "out_done", "beside_a", "beside_b", "beside_c")
        assert n <= 100
        keys = [t["k"].shape[1] for t in tiles]
        parts = [[(j * P, min(P, m - j * P)) for j in range(-(-m // P))] for m in keys]
        with self.phases.phase(*names) as (block, scored, biased, exped, turned, turned_copied, weighed, chain, out_done, beside_a, beside_b, beside_c):
            if beside is not None:
                @block.gpsimd
                def _(pool):
                    beside[0](pool, beside_a, beside_b, beside_c)

            @block.tensor
            def _(pe):
                for s in range(n + 3):
                    if s < n:
                        if s >= 3:
                            pe.wait_ge(biased, s - 2)
                        nc.tensor.matmul(score_bank(s)[:, 0:keys[s]], tiles[s]["q"], tiles[s]["k"],
                                         start=True, stop=True).then_inc(scored, 1)
                    if 2 <= s <= n + 1:
                        j = s - 2
                        pe.wait_ge(exped, j + 1)
                        if j >= 3:
                            pe.wait_ge(turned_copied, j - 2)
                        for a, w in parts[j]:
                            mm = nc.tensor.transpose(turn_bank(j)[0:w, a:a + P], E[:, j % 3, a:a + w], self.c("ident", P))
                        mm.then_inc(turned, 1)
                    if s >= 3:
                        j = s - 3
                        pe.wait_ge(turned_copied, j + 1)
                        if j >= 2:
                            pe.wait_ge(out_done, j - 1)
                        dv = tiles[j]["v"][0].shape[1]
                        for i, (a, w) in enumerate(parts[j]):
                            mm = nc.tensor.matmul(banks[4 + j % 2][:, 0:dv], ET[0:w, j % 3, a:a + P], tiles[j]["v"][i],
                                                  start=(i == 0), stop=(i == len(parts[j]) - 1))
                        mm.then_inc(weighed, 1)

            @block.scalar
            def _(act):
                for s in range(n + 2):
                    if s < n:
                        act.wait_ge(biased, s + 1)
                        if s >= 3:
                            act.wait_ge(turned, s - 2)
                        nc.scalar.activation(E[:, s % 3, 0:keys[s]], S[:, s % 3, 0:keys[s]], ACT.Exp, scale=-1.0,
                                             bias=ntop[:, s:s + 1], accum_out=den[:, s:s + 1]).then_inc(exped, 1)
                    if s >= 2:
                        j = s - 2
                        act.wait_ge(turned, j + 1)
                        if j >= 3:
                            act.wait_ge(weighed, j - 2)
                        w = min(P, keys[j])
                        m = len(parts[j]) * P
                        nc.scalar.activation(ET[0:w, j % 3, 0:m], turn_bank(j)[0:w, 0:m], ACT.Copy).then_inc(turned_copied, 1)
                        if beside is not None:
                            beside[1](act, j, beside_a, beside_b, beside_c)

            @block.vector
            def _(dve):
                count, last = 0, {}

                def steps(t, at):
                    d, r, v = den[:, at:at + 1], rec[:, at:at + 1], nc.vector
                    out = [lambda: v.reciprocal(r, d)]
                    if t.get("may_be_empty"):
                        out.insert(0, lambda: v.tensor_scalar(d, d, 1e-30, None, ALU.max))
                    if t.get("gate") is not None:
                        out.append(lambda: v.tensor_tensor(r, r, t["gate"], ALU.mult))
                    return out

                def step(j, k):
                    nonlocal count
                    if 0 <= j < n and k < len(steps(tiles[j], j)):
                        if k == 0:
                            dve.wait_ge(exped, j + 1)
                        else:
                            dve.wait_ge(chain, last[j])
                        steps(tiles[j], j)[k]().then_inc(chain, 1)
                        count += 1
                        last[j] = count

                for s in range(n + 3):
                    step(s - 2, 2)
                    if s < n:
                        dve.wait_ge(scored, s + 1)
                        if s >= 3:
                            dve.wait_ge(exped, s - 2)
                        nc.vector.tensor_tensor_reduce(
                            out=S[:, s % 3, 0:keys[s]], in0=score_bank(s)[:, 0:keys[s]], in1=tiles[s]["bias"],
                            scale=-scale, scalar=-NEG_ROW, op0=ALU.add, op1=ALU.min,
                            accum_out=ntop[:, s:s + 1]).then_inc(biased, 1)
                    step(s - 1, 0)
                    if s >= 3:
                        j = s - 3
                        t = tiles[j]
                        dve.wait_ge(weighed, j + 1)
                        dve.wait_ge(chain, last[j])
                        at = t.get("at", 0)
                        result = banks[4 + j % 2][:, at:at + t["out"].shape[1]]
                        if t.get("add"):
                            if t["after"] is not None:
                                dve.wait_ge(out_done, t["after"] + 1)
                            nc.vector.scalar_tensor_tensor(t["out"], result, rec[:, j:j + 1], t["out"],
                                                           ALU.mult, ALU.add).then_inc(out_done, 1)
                        else:
                            nc.vector.tensor_scalar(t["out"], result, rec[:, j:j + 1], None,
                                                    ALU.mult).then_inc(out_done, 1)
                    step(s - 1, 1)

    def pause(self):
        with self.phases.phase("unused"):
            pass

    def by_head(self, chunks, dst):
        nc = self.nc
        with self.phases.phase("unused") as (block, _):
            @block.gpsimd
            def _(pool):
                for i in range(len(chunks)):
                    for e in range(2):
                        nc.gpsimd.memset(dst[(1 - e) * HD:(2 - e) * HD, 2 * i + e, :], 0.0)

            @block.vector
            def _(dve):
                for i, src in enumerate(chunks):
                    nc.vector.tensor_copy(dst[0:HD, 2 * i, :], src[0:HD, :])

            @block.scalar
            def _(act):
                for i, src in enumerate(chunks):
                    nc.scalar.activation(dst[HD:P, 2 * i + 1, :], src[HD:P, :], ACT.Copy)

    def vector_phase(self, work):
        with self.phases.phase("step") as (block, step):
            @block.vector
            def _(dve):
                for n, do in enumerate(work):
                    if n:
                        dve.wait_ge(step, n)
                    do(self.nc.vector).then_inc(step, 1)

    def p1(self, name, at=0, n=1):
        a = PC1[name] + at
        return self.par1[:, a:a + n]

    def pj(self, c):
        return self.proj[:, c, 1:T + 1]

    def shift_sums(self, pool, diff_ready, scaled, shifted):
        diff, step = self.units("h", 0, 4), self.units("h", 4, 4)
        for c in range(10 + 2):
            if c < 10:
                if c >= 4:
                    pool.wait_ge(scaled, c - 3)
                self.nc.gpsimd.tensor_tensor(diff[:, c % 4, :], self.proj[:, c, 0:T], self.pj(c), ALU.subtract).then_inc(diff_ready, 1)
            if c >= 2:
                k = c - 2
                pool.wait_ge(scaled, k + 1)
                self.nc.gpsimd.tensor_tensor(self.pj(k), self.pj(k), step[:, k % 4, :], ALU.add).then_inc(shifted, 1)

    def shift_scale(self, act, tile, diff_ready, scaled, shifted):
        k = tile // 2
        if tile % 2 == 0 and k < 10:
            diff, step = self.units("h", 0, 4), self.units("h", 4, 4)
            act.wait_ge(diff_ready, k + 1)
            if k >= 4:
                act.wait_ge(shifted, k - 3)
            self.nc.scalar.activation(step[:, k % 4, :], diff[:, k % 4, :], ACT.Copy, scale=self.p1("mu", k)).then_inc(scaled, 1)

    def lora_apart(self):
        return self.units("arena", 9, 3).rearrange("p u t -> p (u t)")[:, 0:3 * RW * P].rearrange("p (k f) -> p k f", k=3)

    def rwkv_gates(self):
        nc, banks = self.nc, self.banks
        x9, low = self.pj(9), self.units("h", 0, 1)[:, 0, :]
        lora = self.lora_apart()
        sigw, a, g = self.units("arena", 0, 3), self.units("arena", 3, 3), [self.pj(16 + c) for c in range(RW)]
        with self.phases.phase("low_ready", "gate_product", "gates_read") as (block, low_ready, gate_product, gates_read):
            @block.scalar
            def _(act):
                nc.scalar.activation(low[0:32, :], x9[0:32, :], ACT.Tanh).then_inc(low_ready, 1)
                nc.scalar.activation(low[64:128, :], x9[64:128, :], ACT.Sigmoid).then_inc(low_ready, 1)
                for c in range(RW):
                    b = 3 * (c % 2)
                    act.wait_ge(gate_product, c + 1)
                    nc.scalar.activation(sigw[:, c, :], banks[b][:, :], ACT.Sigmoid, bias=self.p1("w0", c)).then_inc(gates_read, 1)
                    nc.scalar.activation(a[:, c, :], banks[b + 1][:, :], ACT.Sigmoid, bias=self.p1("a0", c)).then_inc(gates_read, 1)

            @block.vector
            def _(dve):
                nc.vector.tensor_copy(low[32:64, :], x9[32:64, :]).then_inc(low_ready, 1)
                for c in range(RW):
                    dve.wait_ge(gate_product, c + 1)
                    nc.vector.tensor_copy(g[c], banks[3 * (c % 2) + 2][:, :]).then_inc(gates_read, 1)

            @block.tensor
            def _(pe):
                pe.wait_ge(low_ready, 3)
                for c in range(RW):
                    b = 3 * (c % 2)
                    if c >= 2:
                        pe.wait_ge(gates_read, 6)
                    nc.tensor.matmul(banks[b][:, :], lora[:, 0, c * P:(c + 1) * P], low, start=True, stop=True)
                    nc.tensor.matmul(banks[b + 1][:, :], lora[:, 1, c * P:(c + 1) * P], low, start=True, stop=True)
                    nc.tensor.matmul(banks[b + 2][:, :], lora[:, 2, c * P:(c + 1) * P], low, start=True, stop=True).then_inc(gate_product, 1)

    def rwkv_scale(self):
        nc, banks = self.nc, self.banks
        sigw, a, bonus = self.units("arena", 0, 3), self.units("arena", 3, 3), self.units("arena", 6, 3)
        cum, before, e_in, e_before, e_out, t1, rk = (self.units("h", i, 1)[:, 0, :] for i in range(1, 8))
        kappa = math.exp(-0.5)
        ends = self.small[:, 0:RW * NCH].rearrange("p (c n) -> p c n", c=RW)
        names = ("chain", "sums_ready", "exps_ready", "bonus_in", "bonus_sum", "chunk_done")
        with self.phases.phase(*names) as (block, chain, sums_ready, exps_ready, bonus_in, bonus_sum, chunk_done):
            @block.gpsimd
            def _(pool):
                for pair in self.heads_apart():
                    for e in range(2):
                        nc.gpsimd.memset(pair[e][(1 - e) * HD:(2 - e) * HD, :], 0.0)

            @block.scalar
            def _(act):
                for c in range(RW):
                    act.wait_ge(sums_ready, c + 1)
                    if c:
                        act.wait_ge(chunk_done, c)
                    nc.scalar.activation(e_in, cum, ACT.Exp, scale=-kappa)
                    nc.scalar.activation(e_before, before, ACT.Exp, scale=-kappa)
                    nc.scalar.activation(e_out, cum, ACT.Exp, scale=kappa).then_inc(exps_ready, 1)

            @block.tensor
            def _(pe):
                for c in range(RW):
                    pe.wait_ge(bonus_in, c + 1)
                    nc.tensor.matmul(banks[c][:, :], self.c("head", P), rk, start=True, stop=True).then_inc(bonus_sum, 1)

            @block.vector
            def _(dve):
                v = nc.vector
                for c in range(RW):
                    r, k, val, at, bt = self.pj(c), self.pj(3 + c), self.pj(6 + c), self.pj(10 + c), self.pj(13 + c)
                    base = 6 * c
                    if c:
                        dve.wait_ge(chunk_done, c)
                    v.tensor_tensor_scan(cum, self.c("start64", T), sigw[:, c, :], 0.0, ALU.mult, ALU.add).then_inc(chain, 1)
                    v.tensor_scalar(t1, a[:, c, :], -1.0, self.p1("k_a", c), ALU.add, ALU.mult).then_inc(chain, 1)
                    dve.wait_ge(chain, base + 1)
                    v.tensor_tensor(before, cum, sigw[:, c, :], ALU.subtract).then_inc(sums_ready, 1)
                    dve.wait_ge(chain, base + 2)
                    v.scalar_tensor_tensor(k, t1, 1.0, k, ALU.add, ALU.mult).then_inc(chain, 1)
                    v.tensor_tensor(bt, at, a[:, c, :], ALU.mult).then_inc(chain, 1)
                    dve.wait_ge(chain, base + 3)
                    v.scalar_tensor_tensor(rk, r, self.p1("r_k", c), k, ALU.mult, ALU.mult).then_inc(bonus_in, 1)
                    dve.wait_ge(exps_ready, c + 1)
                    dve.wait_ge(chain, base + 4)
                    v.tensor_tensor(bt, bt, e_out, ALU.mult).then_inc(chain, 1)
                    v.scalar_tensor_tensor(at, at, -1.0, e_before, ALU.mult, ALU.mult).then_inc(chain, 1)
                    dve.wait_ge(bonus_in, c + 1)
                    v.tensor_tensor(r, r, e_in, ALU.mult)
                    v.tensor_tensor(k, k, e_out, ALU.mult)
                    v.tensor_copy(ends[:, c, :], e_in[:, CH - 1:T:CH])
                    dve.wait_ge(bonus_sum, c + 1)
                    v.tensor_tensor(bonus[:, c, :], banks[c][:, :], val, ALU.mult).then_inc(chunk_done, 1)

    def heads_apart(self):
        return [self.pj(19), self.pj(20)], [self.pj(21), self.pj(22)], [self.mix[:, 0, :], self.mix[:, 1, :]]

    def rwkv_pair(self, cc):
        nc, banks = self.nc, self.banks
        fa, fb, fr, fk = self.pj(10 + cc), self.pj(13 + cc), self.pj(cc), self.pj(3 + cc)
        At, Kt, Vt = (self.units("ring", i, 1)[:, 0, :] for i in range(3))
        Bt = self.units("arena", cc, 1)[:, 0, :]
        tok = lambda u: u.rearrange("p (n f) -> p n f", f=P)
        self.transposes([g for src, dst in ((fa, At), (fk, Kt), (self.pj(6 + cc), Vt), (fb, Bt))
                         for g in self.to_tokens([src], tok(dst))])
        buffers = [[self.units("h", i, 1)[:, 0, :] for i in range(8)], [self.units("ring", 3 + i, 1)[:, 0, :] for i in range(8)]]
        (L, LT, L2, L2T, I, IT, O32, O64) = zip(*buffers)
        UT, W, MV = (self.units("arena", u, 1)[:, 0, :] for u in (3 + cc, 9 + cc, 33))
        KV = self.units("arena", 12 + 2 * cc, 2)
        G = self.units("arena", 18 + 2 * cc, 2)
        RKV = self.units("arena", 24 + cc, 1)[:, 0, :]
        rows = [slice(0, HD), slice(HD, P)]
        FB, FA, FK = self.heads_apart()
        RKT = [self.units("arena", 32, 1)[:, 0, :], self.mix[:, 2, :]]
        tile = lambda u, i: u[:, i * P:(i + 1) * P]
        wide = lambda name: self.c(name, P).unsqueeze(1).to_broadcast([P, NT, P])
        names = ("scores_l", "masked_l", "masked_corners", "started", "scores_a", "scores_b", "masked_a", "masked_b", "values", "values_read",
                 "squares", "squares_copied", "updates", "updated", "corner", "corner_copied", "ends", "ends_read",
                 "by_head", "turned", "turned_copied", "term_ready", "added")
        with self.phases.phase(*names) as (block, scores_l, masked_l, masked_corners, started, scores_a, scores_b, masked_a, masked_b, values, values_read,
                                           squares, squares_copied, updates, updated, corner, corner_copied, ends, ends_read,
                                           by_head, turned, turned_copied, term_ready, added):
            @block.gpsimd
            def _(pool):
                self.conv_sums(pool, self.conv_part(cc, RW), term_ready, added)

            @block.tensor
            def _(pe):
                def by_tile(bank, lhs, rhs, r=slice(0, P), out=slice(0, P)):
                    for i in range(NT):
                        mm = nc.tensor.matmul(tile(banks[bank][out, :], i), tile(lhs[r, :], i), tile(rhs[r, :], i), start=True, stop=True)
                    return mm
                pe.wait_ge(by_head, 6)
                for e in range(2):
                    by_tile(0 + e, FB[e], fa)
                    by_tile(2 + e, FA[e], fb).then_inc(scores_l, 1)
                for e in range(2):
                    by_tile(4 + e, FK[e], fa)
                    by_tile(6 + e, FB[e], fr).then_inc(scores_a, 1)
                pw = [(L, LT), (L2, L2T)]
                pe.wait_ge(masked_l, 2)
                for n in range(3):
                    (p, pt), (q, qt) = pw[n % 2], pw[(n + 1) % 2]
                    if n:
                        pe.wait_ge(squares_copied, 4 * n)
                    for e in range(2):
                        if n == 0 and e == 1:
                            pe.wait_ge(masked_corners, 2)
                        mm = by_tile(0 + 2 * e, pt[e], p[e])
                        if n < 2:
                            mm = by_tile(1 + 2 * e, p[e], pt[e])
                        mm.then_inc(squares, 1)
                    if n == 0:
                        for e in range(2):
                            pe.wait_ge(masked_a, e + 1)
                            by_tile(4 + e, FK[e], fr).then_inc(scores_b, 1)
                        pe.wait_ge(masked_b, 2)
                        for e in range(2):
                            for i in range(NT):
                                nc.tensor.matmul(banks[6][:, i * P + e * HD:i * P + e * HD + HD], tile(I[e], i),
                                                 tile(Vt, i)[:, e * HD:e * HD + HD], start=True, stop=True)
                                mm = nc.tensor.matmul(tile(banks[4][rows[e], :], i), tile(Vt, i)[:, e * HD:e * HD + HD],
                                                      tile(RKT[e], i), start=True, stop=True)
                        mm.then_inc(values, 1)
                        pe.wait_ge(started, 2)
                    pe.wait_ge(squares_copied, 4 * n + (4 if n < 2 else 2))
                    if n:
                        pe.wait_ge(updated, 2 * n)
                    for e in range(2):
                        by_tile(5 + 2 * e, q[e], IT[e]).then_inc(updates, 1)
                pe.wait_ge(updated, 6)
                pe.wait_ge(values_read, 2)
                for e in range(2):
                    for i in range(NT):
                        mm = nc.tensor.transpose(tile(banks[4 + 2 * e], i), tile(IT[e], i), self.c("ident", P))
                    mm.then_inc(turned, 1)
                for e in range(2):
                    by_tile(e, O32[e], IT[e]).then_inc(corner, 1)
                pe.wait_ge(corner_copied, 2)
                pe.wait_ge(turned_copied, 2)
                for e in range(2):
                    by_tile(4 + 2 * e, L[e], I[e])
                    by_tile(5 + 2 * e, I[e], L[e]).then_inc(updates, 1)
                pe.wait_ge(updated, 8)
                for e in range(2):
                    by_tile(e, O64[e], IT[e]).then_inc(corner, 1)
                pe.wait_ge(corner_copied, 4)
                for e in range(2):
                    by_tile(5 + 2 * e, I[e], L[e]).then_inc(updates, 1)
                pe.wait_ge(updated, 10)
                for i in range(NT):
                    for e in range(2):
                        nc.tensor.matmul(tile(banks[0][rows[e], :], i), tile(At, i)[:, e * HD:e * HD + HD], tile(IT[e], i), start=True, stop=True)
                        nc.tensor.matmul(banks[1][:, i * P + e * HD:i * P + e * HD + HD], tile(IT[e], i),
                                         tile(MV, i)[:, e * HD:e * HD + HD], start=True, stop=True)
                for o in range(2):
                    for i in range(NT):
                        mm = nc.tensor.matmul(tile(banks[2 + o], i), tile(Kt[rows[o], :], i), tile(Vt[rows[o], :], i), start=True, stop=True)
                mm.then_inc(ends, 1)

            @block.scalar
            def _(act):
                for src, dst in ((fb, FB), (fa, FA), (fk, FK)):
                    nc.scalar.activation(dst[1][rows[1], :], src[rows[1], :], ACT.Copy).then_inc(by_head, 1)
                taps = self.conv_part(cc, RW)
                terms = lambda first, n: self.conv_terms(act, taps, first, n, term_ready, added)
                terms(0, 4)
                pw = [(L, LT), (L2, L2T)]
                for n in range(3):
                    q, qt = pw[(n + 1) % 2]
                    for e in range(2):
                        act.wait_ge(squares, 2 * n + e + 1)
                        nc.scalar.activation(q[e], banks[0 + 2 * e][:, :], ACT.Copy).then_inc(squares_copied, 1)
                    terms(4 + 4 * n, 4)
                    if n == 0:
                        act.wait_ge(values, 1)
                        nc.scalar.activation(RKV, banks[4][:, :], ACT.Copy).then_inc(values_read, 1)
                for n in range(2):
                    for e in range(2):
                        if n == 0:
                            act.wait_ge(turned, e + 1)
                            nc.scalar.activation(I[e], banks[4 + 2 * e][:, :], ACT.Copy).then_inc(turned_copied, 1)
                    for e in range(2):
                        act.wait_ge(corner, 2 * n + e + 1)
                        nc.scalar.activation(L[e], banks[e][:, :], ACT.Copy).then_inc(corner_copied, 1)
                    terms(16 + 3 * n, 3)
                act.wait_ge(ends, 1)
                nc.scalar.activation(UT, banks[0][:, :], ACT.Copy)
                nc.scalar.activation(W, banks[1][:, :], ACT.Copy).then_inc(ends_read, 1)

            @block.vector
            def _(dve):
                v = nc.vector
                for src, dst in ((fb, FB), (fa, FA), (fk, FK)):
                    v.tensor_copy(dst[0][rows[0], :], src[rows[0], :]).then_inc(by_head, 1)
                for e in range(2):
                    dve.wait_ge(scores_l, e + 1)
                    v.tensor_tensor(tok(LT[e]), tok(banks[0 + e][:, :]), wide("m16T"), ALU.mult)
                    v.tensor_tensor(tok(L[e]), tok(banks[2 + e][:, :]), wide("m16"), ALU.mult).then_inc(masked_l, 1)
                for e in range(2):
                    v.tensor_tensor(tok(O32[e]), tok(banks[2 + e][:, :]), wide("m32"), ALU.mult)
                    v.tensor_tensor(tok(O64[e]), tok(banks[2 + e][:, :]), wide("m64"), ALU.mult).then_inc(masked_corners, 1)
                for e in range(2):
                    dve.wait_ge(scores_a, e + 1)
                    v.tensor_tensor(tok(I[e]), tok(banks[4 + e][:, :]), wide("strictT"), ALU.mult)
                    v.tensor_tensor(tok(G[:, e, :]), tok(banks[6 + e][:, :]), wide("inclT"), ALU.mult).then_inc(masked_a, 1)
                for e in range(2):
                    dve.wait_ge(masked_l, e + 1)
                    v.tensor_tensor(tok(IT[e]), tok(LT[e]), wide("ident"), ALU.add).then_inc(started, 1)
                for e in range(2):
                    dve.wait_ge(squares, e + 1)
                    v.tensor_copy(L2T[e], banks[1 + 2 * e][:, :]).then_inc(squares_copied, 1)
                for e in range(2):
                    dve.wait_ge(scores_b, e + 1)
                    v.tensor_tensor(tok(RKT[e]), tok(banks[4 + e][:, :]), wide("inclT"), ALU.mult).then_inc(masked_b, 1)
                dve.wait_ge(values, 1)
                v.tensor_copy(MV, banks[6][:, :]).then_inc(values_read, 1)
                pw = [(L, LT), (L2, L2T)]
                for n in range(3):
                    q, qt = pw[(n + 1) % 2]
                    if n == 1:
                        for e in range(2):
                            dve.wait_ge(squares, 2 * n + e + 1)
                            v.tensor_copy(qt[e], banks[1 + 2 * e][:, :]).then_inc(squares_copied, 1)
                    for e in range(2):
                        dve.wait_ge(updates, 2 * n + e + 1)
                        v.tensor_tensor(IT[e], IT[e], banks[5 + 2 * e][:, :], ALU.add).then_inc(updated, 1)
                for e in range(2):
                    dve.wait_ge(updates, 6 + e + 1)
                    v.tensor_tensor(I[e], I[e], banks[4 + 2 * e][:, :], ALU.add)
                    v.tensor_tensor(IT[e], IT[e], banks[5 + 2 * e][:, :], ALU.add).then_inc(updated, 1)
                for e in range(2):
                    dve.wait_ge(updates, 8 + e + 1)
                    v.tensor_tensor(IT[e], IT[e], banks[5 + 2 * e][:, :], ALU.add).then_inc(updated, 1)
                dve.wait_ge(ends, 1)
                for o in range(2):
                    v.tensor_tensor(tok(KV[:, o, :]), tok(banks[2 + o][:, :]), wide("head"), ALU.mult)

    def rwkv_states(self):
        nc, banks = self.nc, self.banks
        Bt, UT, W = self.units("arena", 0, 3), self.units("arena", 3, 3), self.units("arena", 9, 3)
        KV, S, SA = self.units("arena", 12, 6), self.units("arena", 27, 6), self.units("ring", 0, 3)
        ends = self.small[:, 0:RW * NCH].rearrange("p (c n) -> p c n", c=RW)
        ends_mask, kept, kept2, change = (self.units("ring", 3 + i, 1)[:, 0, 0:RW * P].rearrange("p (c f) -> p c f", c=RW) for i in range(4))
        state = lambda c: S.rearrange("p u t -> p (u t)")[:, c * RW * P:(c + 1) * RW * P].rearrange("p (c f) -> p c f", c=RW)
        three = lambda bank: bank[:, 0:RW * P].rearrange("p (c f) -> p c f", c=RW)
        with self.phases.phase("state_ready", "sa_product", "sa_ready", "update", "chain", "mean_sum", "centred",
                               "squared", "var_sum", "logged", "rstd_ready", "normed") as (
                block, state_ready, sa_product, sa_ready, update, chain, mean_sum, centred, squared, var_sum, logged,
                rstd_ready, normed):
            @block.scalar
            def _(act):
                self.conv_activations(act, centred, squared, var_sum, logged, rstd_ready, normed)

            @block.tensor
            def _(pe):
                for c in range(NCH):
                    i, o = c // 2, slice(HD * (c % 2), HD * (c % 2) + HD)
                    pe.wait_ge(state_ready, c + 1)
                    for cc in range(RW):
                        mm = nc.tensor.matmul(three(banks[c % 2])[o, cc, :], UT[:, cc, c * CH:(c + 1) * CH], state(c)[:, cc, :],
                                              start=True, stop=True)
                    mm.then_inc(sa_product, 1)
                    if c == 0:
                        self.conv_mean(mean_sum)
                    if c == 3:
                        self.conv_variance(pe, squared, var_sum)
                    if c < NCH - 1:
                        pe.wait_ge(sa_ready, c + 1)
                        for cc in range(RW):
                            mm = nc.tensor.matmul(three(banks[2 + c % 2])[:, cc, :], Bt[o, cc, i * P:(i + 1) * P],
                                                  SA[o, cc, i * P:(i + 1) * P], start=True, stop=True)
                        mm.then_inc(update, 1)

            @block.vector
            def _(dve):
                v = nc.vector
                v.memset(state(0), 0.0).then_inc(state_ready, 1)
                for c in range(NCH):
                    i, o = c // 2, slice(HD * (c % 2), HD * (c % 2) + HD)
                    dve.wait_ge(sa_product, c + 1)
                    v.tensor_tensor(SA[o, :, i * P:(i + 1) * P], three(banks[c % 2])[o, :, :], W[o, :, i * P:(i + 1) * P],
                                    ALU.add).then_inc(sa_ready, 1)
                    if c < NCH - 1:
                        end = ends[:, :, c:c + 1].to_broadcast([P, RW, P])
                        n = 3 * c
                        v.tensor_tensor(ends_mask, self.c("head", P).unsqueeze(1).to_broadcast([P, RW, P]), end, ALU.mult).then_inc(chain, 1)
                        kv = KV.rearrange("p (c o) t -> p c o t", o=2)[:, :, c % 2, i * P:(i + 1) * P]
                        dve.wait_ge(state_ready, c + 1)
                        v.tensor_tensor(kept, state(c), kv, ALU.add).then_inc(chain, 1)
                        dve.wait_ge(chain, n + 2)
                        v.tensor_tensor(kept2, kept, end, ALU.mult)
                        dve.wait_ge(update, c + 1)
                        v.tensor_tensor(change, three(banks[2 + c % 2]), ends_mask, ALU.mult).then_inc(chain, 1)
                        dve.wait_ge(chain, n + 3)
                        v.tensor_tensor(state(c + 1), change, kept2, ALU.add).then_inc(state_ready, 1)
                    if c == 1:
                        self.conv_centre(dve, mean_sum, centred)
                    if c == 6:
                        self.conv_norm(dve, rstd_ready, normed)

    def rwkv_output(self):
        nc, banks = self.nc, self.banks
        S, SA, G = self.units("arena", 27, 6), self.units("ring", 0, 3), self.units("arena", 18, 6)
        RKV, bonus = self.units("arena", 24, 3), self.units("arena", 6, 3)
        state = lambda c: S.rearrange("p u t -> p (u t)")[:, c * RW * P:(c + 1) * RW * P].rearrange("p (c f) -> p c f", c=RW)
        y, sq, rs = self.units("h", 0, 3), self.units("h", 3, 3), self.units("ring", 3, 3)
        names = ("y_product", "y_ready", "mean_sum", "centred", "squared", "var_sum", "logged", "rstd_ready", "chain")
        with self.phases.phase(*names) as (block, y_product, y_ready, mean_sum, centred, squared, var_sum, logged, rstd_ready, chain):
            @block.tensor
            def _(pe):
                for cc in range(RW):
                    for i in range(NT):
                        for c in (2 * i, 2 * i + 1):
                            nc.tensor.matmul(banks[cc][:, c * CH:(c + 1) * CH], state(c)[:, cc, :], self.pj(cc)[:, c * CH:(c + 1) * CH],
                                             start=(c == 0), stop=False, skip_group_check=True)
                        for e in range(2):
                            mm = nc.tensor.matmul(banks[cc][e * HD:(e + 1) * HD, i * P:(i + 1) * P],
                                                  SA[:, cc, i * P + e * HD:i * P + (e + 1) * HD], G[:, 2 * cc + e, i * P:(i + 1) * P],
                                                  start=False, stop=(i == NT - 1), skip_group_check=True)
                    mm.then_inc(y_product, 1)
                for cc in range(RW):
                    pe.wait_ge(y_ready, cc + 1)
                    nc.tensor.matmul(banks[3 + cc][:, :], self.c("head", P), y[:, cc, :], start=True, stop=True).then_inc(mean_sum, 1)
                for cc in range(RW):
                    pe.wait_ge(squared, cc + 1)
                    bank = banks[(6, 7, 0)[cc]]
                    nc.tensor.matmul(bank[:, :], self.c("head", P), sq[:, cc, :], start=True, stop=True).then_inc(var_sum, 1)

            @block.scalar
            def _(act):
                for cc in range(RW):
                    act.wait_ge(centred, cc + 1)
                    nc.scalar.activation(sq[:, cc, :], y[:, cc, :], ACT.Square).then_inc(squared, 1)
                for cc in range(RW):
                    act.wait_ge(var_sum, cc + 1)
                    nc.scalar.activation(rs[:, cc, :], banks[(6, 7, 0)[cc]][:, :], ACT.Ln, bias=self.c("eps_gn"), scale=1.0 / HD).then_inc(logged, 1)
                for cc in range(RW):
                    act.wait_ge(logged, cc + 1)
                    nc.scalar.activation(rs[:, cc, :], rs[:, cc, :], ACT.Exp, scale=-0.5).then_inc(rstd_ready, 1)

            @block.vector
            def _(dve):
                v = nc.vector
                for cc in range(RW):
                    dve.wait_ge(y_product, cc + 1)
                    v.tensor_tensor(y[:, cc, :], banks[cc][:, :], RKV[:, cc, :], ALU.add).then_inc(y_ready, 1)
                for cc in range(RW):
                    dve.wait_ge(mean_sum, cc + 1)
                    v.scalar_tensor_tensor(y[:, cc, :], banks[3 + cc][:, :], -1.0 / HD, y[:, cc, :], ALU.mult, ALU.add).then_inc(centred, 1)
                for cc in range(RW):
                    dve.wait_ge(rstd_ready, cc + 1)
                    v.scalar_tensor_tensor(y[:, cc, :], y[:, cc, :], self.p1("ln_w", cc), rs[:, cc, :], ALU.mult, ALU.mult).then_inc(chain, 1)
                    dve.wait_ge(chain, 2 * cc + 1)
                    v.scalar_tensor_tensor(y[:, cc, :], y[:, cc, :], self.p1("ln_b", cc), bonus[:, cc, :], ALU.add, ALU.add).then_inc(chain, 1)
                    dve.wait_ge(chain, 2 * cc + 2)
                    v.tensor_tensor(self.mix[:, cc, :], y[:, cc, :], self.pj(16 + cc), ALU.mult)

    def dilated_attention(self):
        nc = self.nc
        self.head_norm([(self.pj(10 + c), self.p1("q_norm"), self.pj(10 + c), 1.0) for c in range(AT)]
                       + [(self.pj(13 + c), self.p1("k_norm"), self.pj(13 + c), 1.0) for c in range(AT)], HD, "eps6")
        vt = self.units("arena", 0, 3).rearrange("p u t -> p (u t)").rearrange("p (n f) -> p n f", f=AT * P)
        out = self.units("arena", 3, 3).rearrange("p u t -> p (u t)").rearrange("p (n f) -> p n f", f=AT * P)
        bias = self.units("arena", 6, 6)
        self.transposes(self.to_tokens([self.pj(16 + c) for c in range(AT)], vt))
        self.vector_phase([lambda v, h=h, s=s: v.scalar_tensor_tensor(bias[:, h, :], self.c("dist", T), -8.0 * s,
                                                                    self.c("log_count", T), ALU.mult, ALU.add)
                           for h, s in enumerate(dilated_slopes())])
        queries = self.units("arena", 12, 6)
        self.by_head([self.pj(10 + c) for c in range(AT)], queries)
        tiles = []
        for h in range(2 * AT):
            pair = slice(h // 2 * P, h // 2 * P + P)
            for i in range(NT):
                tiles.append(dict(q=queries[:, h, i * P:(i + 1) * P], k=self.pj(13 + h // 2)[:, 0:(i + 1) * P],
                                  bias=bias[:, h, T - (i + 1) * P:T], v=[vt[:, j, pair] for j in range(i + 1)],
                                  at=HD * (h % 2), out=out[:, i, h * HD:(h + 1) * HD]))
        self.attention(tiles, HD ** -0.5, beside=(self.shift_sums, self.shift_scale))
        self.transposes(self.to_features(out, [self.mix[:, RW + c, :] for c in range(AT)]))

    def conv_memory(self):
        z = self.units("arena", 27, 3).rearrange("p u t -> p (u t)")[:, 0:CV * (T + TAPS - 1)].rearrange("p (c t) -> p c t", c=CV)
        return z, self.mix[:, RW + AT:RW + AT + CV, :]

    def conv_open(self):
        nc = self.nc
        z, _ = self.conv_memory()
        sg = self.units("arena", 32, 2)
        lora = self.lora_apart()
        with self.phases.phase("opened", "cleared") as (block, opened, cleared):
            @block.gpsimd
            def _(pool):
                self.nc.gpsimd.memset(lora, 0.0).then_inc(cleared, 1)

            @block.scalar
            def _(act):
                for c in range(CV):
                    nc.scalar.activation(sg[:, c, :], self.pj(21 + c), ACT.Sigmoid).then_inc(opened, 1)

            @block.vector
            def _(dve):
                nc.vector.memset(z[:, :, 0:TAPS - 1], 0.0)
                for c in range(CV):
                    dve.wait_ge(opened, c + 1)
                    nc.vector.tensor_tensor(z[:, c, TAPS - 1:], self.pj(19 + c), sg[:, c, :], ALU.mult)
                dve.wait_ge(cleared, 1)
                for k, r in enumerate((slice(0, 32), slice(32, 64), slice(64, P))):
                    nc.vector.tensor_copy(lora[r, k, :], self.par1[r, PC1["lora"]:PC1["lora"] + RW * P])

    def conv_part(self, part, parts):
        taps = [(j, c) for j in range(TAPS) for c in range(CV)]
        return taps[len(taps) * part // parts:len(taps) * (part + 1) // parts]

    def conv_terms(self, act, taps, first, n, term_ready, added):
        z, acc = self.conv_memory()
        slots = [self.c(name, T) for name in ("dist", "log_count", "causal", "zero")]
        for k in range(first, min(first + n, len(taps))):
            j, c = taps[k]
            if k >= 4:
                act.wait_ge(added, k - 3)
            w = self.p1("dw", j * CV + c)
            if j == 0:
                self.nc.scalar.activation(acc[:, c, :], z[:, c, 0:T], ACT.Identity, bias=self.p1("dw_b", c), scale=w).then_inc(term_ready, 1)
            else:
                self.nc.scalar.activation(slots[k % 4], z[:, c, j:j + T], ACT.Copy, scale=w).then_inc(term_ready, 1)

    def conv_sums(self, pool, taps, term_ready, added):
        _, acc = self.conv_memory()
        slots = [self.c(name, T) for name in ("dist", "log_count", "causal", "zero")]
        for k, (j, c) in enumerate(taps):
            pool.wait_ge(term_ready, k + 1)
            if j == 0:
                pool.sem_inc(added, 1)
            else:
                if k >= CV:
                    pool.wait_ge(added, k - CV + 1)
                self.nc.gpsimd.tensor_tensor(acc[:, c, :], acc[:, c, :], slots[k % 4], ALU.add).then_inc(added, 1)

    def conv_mean(self, mean_sum):
        _, acc = self.conv_memory()
        for c in range(CV):
            mm = self.nc.tensor.matmul(self.banks[4][:, :], self.c("ones", P), acc[:, c, :], start=(c == 0), stop=(c == CV - 1))
        mm.then_inc(mean_sum, 1)

    def conv_variance(self, pe, squared, var_sum):
        for c in range(CV):
            pe.wait_ge(squared, c + 1)
            mm = self.nc.tensor.matmul(self.banks[5][:, :], self.c("ones", P), self.units("h", c, 1)[:, 0, :],
                                       start=(c == 0), stop=(c == CV - 1))
        mm.then_inc(var_sum, 1)

    def conv_centre(self, dve, mean_sum, centred):
        _, acc = self.conv_memory()
        dve.wait_ge(mean_sum, 1)
        for c in range(CV):
            self.nc.vector.scalar_tensor_tensor(acc[:, c, :], self.banks[4][:, :], -1.0 / (CV * P), acc[:, c, :],
                                                ALU.mult, ALU.add).then_inc(centred, 1)

    def conv_norm(self, dve, rstd_ready, normed):
        _, acc = self.conv_memory()
        dve.wait_ge(rstd_ready, 1)
        for c in range(CV):
            self.nc.vector.scalar_tensor_tensor(acc[:, c, :], acc[:, c, :], self.p1("cln_w", c), self.units("h", 3, 1)[:, 0, :],
                                                ALU.mult, ALU.mult).then_inc(normed, 1)

    def conv_activations(self, act, centred, squared, var_sum, logged, rstd_ready, normed):
        _, acc = self.conv_memory()
        sq, lg, rs = self.units("h", 0, 2), self.units("h", 2, 1)[:, 0, :], self.units("h", 3, 1)[:, 0, :]
        for c in range(CV):
            act.wait_ge(centred, c + 1)
            self.nc.scalar.activation(sq[:, c, :], acc[:, c, :], ACT.Square).then_inc(squared, 1)
        act.wait_ge(var_sum, 1)
        self.nc.scalar.activation(lg, self.banks[5][:, :], ACT.Ln, bias=self.c("eps5"), scale=1.0 / (CV * P)).then_inc(logged, 1)
        act.wait_ge(logged, 1)
        self.nc.scalar.activation(rs, lg, ACT.Exp, scale=-0.5).then_inc(rstd_ready, 1)
        for c in range(CV):
            act.wait_ge(normed, c + 1)
            self.nc.scalar.activation(acc[:, c, :], acc[:, c, :], ACT.Silu, bias=self.p1("cln_b", c))

    def first_layer(self, layer):
        self.load_layer(layer)
        gains = lambda n: self.p1(n, 0, KD)
        down1, down2 = ("down1", layer * 2 * KD, KF // 2), ("down2", layer * 2 * KD, KF // 2)
        w_in, w_out, gu2 = ("w_in", layer * M_IN, KD), ("w_out", layer * KD, KD), ("gu2", layer * 2 * KF, KD)
        self.ffn(gains("norm_ffn1"), ("gu1", layer * 2 * KF, KD), down1, 0.5, then=w_in, next_gain=gains("norm_mix"))
        self.project(w_in, M_IN, self.proj[:, :, 1:T + 1], norm=(self.x, gains("norm_mix"), False), prefetched=True,
                     beside=[self.masks_load()], ready_split=True)
        self.vector_phase([lambda v: v.memset(self.proj[:, :, 0:1], 0.0)])
        self.dilated_attention()
        self.conv_open()
        self.rwkv_gates()
        self.head_norm([(self.pj(3 + c), self.p1("k_k", c), self.pj(10 + c), self.p1("k_k", c)) for c in range(RW)], 1, "eps12")
        self.rwkv_scale()
        for cc in range(RW):
            self.rwkv_pair(cc)
        self.rwkv_states()
        self.rwkv_output()
        self.add_to_residual(w_out, 1, self.mixed_source(), 1.0, split=self.mix, then=gu2, next_gain=gains("norm_ffn2"))
        self.ffn(gains("norm_ffn2"), gu2, down2, 0.5, prefetched=True, ready_split=True)

    def p2(self, name, at=0, n=1):
        a = PC2[name] + at
        return self.par2[:, a:a + n]

    def memory_kv(self, layer, then):
        with self.phases.phase("loaded") as (block, loaded):
            @block.sync
            def _(sp):
                sp.dma_start(self.mix[:, :, 0:MEM_T], self.dram["mem"]).then_inc(loaded, 16)
                sp.wait_ge(loaded, 16)
        self.project(("w_mem", layer * KD, KD), KD, self.mix, norm=(self.mix, self.p2("g_mem", KD * layer, KD), True),
                     n=MEM_T, prefetched=layer > 0, then=then)
        at = 19 * (T + 1)
        self.mk = self.big[:, at:at + 2 * T].rearrange("p (h t) -> p h t", h=4)
        self.mv = self.big[:, at + 2 * T:at + 4 * T].rearrange("p (n f) -> p n f", f=T)
        self.vector_phase([lambda v: v.tensor_copy(self.mk, self.mix[:, 0:4, 0:MEM_T])])
        self.transposes(self.to_tokens([self.mix[:, 4 + c, 0:MEM_T] for c in range(4)], self.mv))

    def whole_source(self):
        h = self.units("arena", 0, 8)
        rstd = self.kept_rstd.unsqueeze(1).to_broadcast([P, KD, T])
        self.vector_phase([lambda v: v.tensor_tensor(h, self.src_hi[:, :, :].bitcast(F32), self.src_lo[:, :, :].bitcast(F32), ALU.add),
                           lambda v: v.tensor_tensor(h, h, rstd, ALU.mult)])
        return h

    def memory_attention(self, first, out, done):
        tiles = [dict(q=self.pj(first + h)[:, i * P:(i + 1) * P], k=self.mk[:, h, :], bias=self.c("zero", MEM_T),
                      v=[self.mv[:, j, h * P:(h + 1) * P] for j in range(2)], out=out[:, i, h * P:(h + 1) * P])
                 for h in range(4) for i in range(NT)]
        self.attention(tiles, P ** -0.5)
        self.transposes(self.to_features(out, done))

    def gla_decays(self, h):
        nc, banks = self.nc, self.banks
        small = self.pj(17)[:, 0:3 * P]
        alr, z, low, mag, ex, lg, la, cum, ein, eout = (self.units("arena", i, 1)[:, 0, :] for i in range(10))
        kt = self.units("arena", 10, 2)
        ends = self.small[:, 0:2 * NGC].rearrange("p (c n) -> p c n", c=2)
        names = ("loaded", "alr_product", "alr_ready", "z_product", "z_ready", "chain", "magnitude", "exped", "logged",
                 "summed_up", "decays_ready", "chunk_done")
        with self.phases.phase(*names) as (block, loaded, alr_product, alr_ready, z_product, z_ready, chain, magnitude,
                                           exped, logged, summed_up, decays_ready, chunk_done):
            @block.sync
            def _(sp):
                sp.dma_start(small, self.dram["gla_small"]).then_inc(loaded, 16)

            @block.tensor
            def _(pe):
                pe.wait_ge(loaded, 16)
                for k in range(KD):
                    mm = nc.tensor.matmul(banks[0][0:16, :], small[:, 16 * k:16 * k + 16], h[:, k, :], start=(k == 0), stop=(k == KD - 1))
                mm.then_inc(alr_product, 1)
                pe.wait_ge(alr_ready, 1)
                for cc in range(2):
                    nc.tensor.matmul(banks[1 + cc][:, :], small[0:16, P + cc * P:P + (cc + 1) * P], alr[0:16, :], start=True, stop=True).then_inc(z_product, 1)

            @block.scalar
            def _(act):
                for cc in range(2):
                    act.wait_ge(magnitude, cc + 1)
                    nc.scalar.activation(ex, mag, ACT.Exp, scale=-1.0).then_inc(exped, 1)
                    act.wait_ge(exped, cc + 1)
                    nc.scalar.activation(lg, ex, ACT.Ln, bias=self.c("one")).then_inc(logged, 1)
                    act.wait_ge(summed_up, cc + 1)
                    nc.scalar.activation(ein, cum, ACT.Exp, scale=1.0 / 16)
                    nc.scalar.activation(eout, cum, ACT.Exp, scale=-1.0 / 16).then_inc(decays_ready, 1)

            @block.vector
            def _(dve):
                v = nc.vector
                dve.wait_ge(alr_product, 1)
                v.tensor_copy(alr[0:16, :], banks[0][0:16, :]).then_inc(alr_ready, 1)
                for cc in range(2):
                    q, k = self.pj(cc), self.pj(2 + cc)
                    n = 2 * cc
                    dve.wait_ge(z_product, cc + 1)
                    if cc:
                        dve.wait_ge(chunk_done, cc)
                    v.tensor_scalar(z, banks[1 + cc][:, :], self.p2("b_alpha", cc), None, ALU.add).then_inc(z_ready, 1)
                    dve.wait_ge(z_ready, cc + 1)
                    v.tensor_scalar(low, z, 0.0, None, ALU.min)
                    v.scalar_tensor_tensor(mag, z, -1.0, z, ALU.mult, ALU.max).then_inc(magnitude, 1)
                    dve.wait_ge(logged, cc + 1)
                    v.tensor_tensor(la, low, lg, ALU.subtract).then_inc(chain, 1)
                    dve.wait_ge(chain, n + 1)
                    v.tensor_tensor_scan(cum, self.c("start32", T), la, 0.0, ALU.mult, ALU.add).then_inc(summed_up, 1)
                    dve.wait_ge(decays_ready, cc + 1)
                    v.scalar_tensor_tensor(q, q, 0.125, ein, ALU.mult, ALU.mult)
                    v.tensor_tensor(k, k, eout, ALU.mult).then_inc(chain, 1)
                    v.tensor_copy(ends[:, cc, :], ein[:, GC - 1:T:GC])
                    dve.wait_ge(chain, n + 2)
                    v.tensor_tensor(kt[:, cc, :].rearrange("p (c t) -> p c t", t=GC), k.rearrange("p (c t) -> p c t", t=GC),
                                    ein.rearrange("p (c t) -> p c t", t=GC)[:, :, GC - 1:GC].to_broadcast([P, NGC, GC]),
                                    ALU.mult).then_inc(chunk_done, 1)

    def gla_mix(self):
        nc, banks = self.nc, self.banks
        flat = lambda w, f: self.units(*w).rearrange("p u t -> p (u t)").rearrange("p (n f) -> p n f", f=f)
        Vt, Kh = flat(("arena", 0, 4), T), flat(("arena", 4, 2), 2 * P)
        self.transposes(self.to_tokens([self.pj(4 + c) for c in range(4)], Vt)
                        + self.to_tokens([self.units("arena", 10 + c, 1)[:, 0, :] for c in range(2)], Kh))
        S = self.units("arena", 12, 8).rearrange("p u t -> p (u t)").rearrange("p (c n f) -> p c n f", c=2, f=P)
        A = self.units("arena", 20, 4)
        ends = self.small[:, 0:2 * NGC].rearrange("p (c n) -> p c n", c=2)
        rows = [slice(0, HD), slice(HD, P)]
        tile = lambda u, i: u[:, i * P:(i + 1) * P]
        with self.phases.phase("kv_product", "state_ready") as (block, kv_product, state_ready):
            @block.tensor
            def _(pe):
                for cc in range(2):
                    for g in range(4):
                        r = slice(GC * g, GC * g + GC)
                        for i in range(NT):
                            for e in range(2):
                                mm = nc.tensor.matmul(tile(banks[4 * cc + g][rows[e], :], i),
                                                      Kh[r, i, cc * P + e * HD:cc * P + (e + 1) * HD],
                                                      Vt[r, i, (2 * cc + e) * P:(2 * cc + e + 1) * P], start=True, stop=True,
                                                      tile_position=(GC * g, HD * e))
                    mm.then_inc(kv_product, 1)

            @block.vector
            def _(dve):
                v = nc.vector
                v.memset(S[:, :, 0, :], 0.0).then_inc(state_ready, 1)
                dve.wait_ge(kv_product, 2)
                for c in range(NGC - 1):
                    for cc in range(2):
                        dve.wait_ge(state_ready, max(1, 2 * c + cc))
                        v.scalar_tensor_tensor(S[:, cc, c + 1, :], S[:, cc, c, :], ends[:, cc, c:c + 1],
                                               tile(banks[4 * cc + c % 4], c // 4), ALU.mult, ALU.add).then_inc(state_ready, 1)

        o, sr = self.units("arena", 24, 4), self.units("h", 0, 4)
        sq, lg, rs = self.units("ring", 0, 2), self.units("ring", 2, 2), self.units("ring", 4, 2)
        names = ("scores", "masked", "product", "stored", "squared", "summed", "logged", "rstd_ready", "opened", "normed")
        with self.phases.phase(*names) as (block, scores, masked, product, stored, squared, summed, logged, rstd_ready, opened, normed):
            @block.tensor
            def _(pe):
                for h in range(4):
                    cc, r = h // 2, rows[h % 2]
                    for i in range(NT):
                        mm = nc.tensor.matmul(tile(banks[h], i), tile(self.pj(2 + cc)[r, :], i), tile(self.pj(cc)[r, :], i), start=True, stop=True)
                    mm.then_inc(scores, 1)
                for h in range(4):
                    cc, r = h // 2, rows[h % 2]
                    pe.wait_ge(masked, h + 1)
                    for i in range(NT):
                        nc.tensor.matmul(tile(banks[4 + h], i), Vt[:, i, h * P:(h + 1) * P], tile(A[:, h, :], i), start=True, stop=False)
                        for c in range(4 * i, 4 * i + 4):
                            mm = nc.tensor.matmul(banks[4 + h][:, c * GC:(c + 1) * GC], S[r, cc, c, :], self.pj(cc)[r, c * GC:(c + 1) * GC],
                                                  start=False, stop=(c == 4 * i + 3))
                    mm.then_inc(product, 1)
                for h in range(4):
                    pe.wait_ge(squared, h + 1)
                    nc.tensor.matmul(banks[h % 2][:, :], self.c("ones", P), sq[:, h % 2, :], start=True, stop=True).then_inc(summed, 1)

            @block.scalar
            def _(act):
                for h in range(4):
                    nc.scalar.activation(sr[:, h, :], self.pj(8 + h), ACT.Silu).then_inc(opened, 1)
                for h in range(4):
                    act.wait_ge(stored, h + 1)
                    if h >= 2:
                        act.wait_ge(summed, h - 1)
                    nc.scalar.activation(sq[:, h % 2, :], o[:, h, :], ACT.Square).then_inc(squared, 1)
                    act.wait_ge(summed, h + 1)
                    nc.scalar.activation(lg[:, h % 2, :], banks[h % 2][:, :], ACT.Ln, bias=self.c("eps6"), scale=1.0 / P).then_inc(logged, 1)
                    act.wait_ge(logged, h + 1)
                    if h >= 2:
                        act.wait_ge(normed, h - 1)
                    nc.scalar.activation(rs[:, h % 2, :], lg[:, h % 2, :], ACT.Exp, scale=-0.5).then_inc(rstd_ready, 1)

            @block.vector
            def _(dve):
                v = nc.vector
                for h in range(4):
                    dve.wait_ge(scores, h + 1)
                    v.tensor_tensor(A[:, h, :].rearrange("p (n t) -> p n t", t=P), banks[h][:, :].rearrange("p (n t) -> p n t", t=P),
                                    self.c("incl32T", P).unsqueeze(1).to_broadcast([P, NT, P]), ALU.mult).then_inc(masked, 1)
                for h in range(4):
                    dve.wait_ge(product, h + 1)
                    v.tensor_copy(o[:, h, :], banks[4 + h][:, :]).then_inc(stored, 1)
                for h in range(4):
                    dve.wait_ge(rstd_ready, h + 1)
                    v.scalar_tensor_tensor(o[:, h, :], o[:, h, :], self.p2("g_head"), rs[:, h % 2, :], ALU.mult, ALU.mult).then_inc(normed, 1)
                    dve.wait_ge(normed, h + 1)
                    dve.wait_ge(opened, h + 1)
                    v.tensor_tensor(self.mix[:, h, :], o[:, h, :], sr[:, h, :], ALU.mult)

    def gla_layer(self):
        a_in, a_out, gu3 = ("a_in", 0, KD), ("a_out", 0, KD), ("gu3", 0, KD)
        self.memory_kv(0, a_in)
        self.project(a_in, 16, self.proj[:, :, 1:T + 1], norm=(self.x, self.p2("g_mix", 0, KD), False), prefetched=True,
                     beside=[self.masks_load()])
        h = self.whole_source()
        self.gla_decays(h)
        self.gla_mix()
        out = self.units("arena", 0, 4).rearrange("p u t -> p (u t)").rearrange("p (n f) -> p n f", f=T)
        self.memory_attention(12, out, [self.mix[:, 4 + c, :] for c in range(4)])
        self.add_to_residual(a_out, 1, self.mixed_source(), 1.0, split=self.mix, then=gu3, next_gain=self.p2("g_ffn", 0, KD))
        self.conv_ffn(0, ("w_mem", KD, KD))

    def conv_ffn(self, layer, then):
        taps = [self.p2("cw", (3 * layer + j) * KF, KF) for j in range(3)]
        self.ffn(self.p2("g_ffn", layer * KD, KD), ("gu3", layer * 2 * KF, KD), ("down3", layer * 2 * KD, KF // 2), 1.0,
                 taps, self.p2("cb", layer * KF, KF), prefetched=True, then=then, ready_split=True)

    def compress(self, sources, pes, w1s, w2s, out_k, out_v):
        nc, banks = self.nc, self.banks
        GELU = math.sqrt(2.0 / math.pi)
        GB = 2 * NCMP
        z = [self.units("arena", 8 + 2 * n, 2).rearrange("p u t -> p (u t)")[:, 0:16 * GB].rearrange("p (j g b) -> p j g b", g=2, b=NCMP)
             for n in range(2)]
        hid, cube, act_in, th, ge = ([self.units("arena", 12 + 2 * i + n, 1)[0:GB, 0, 0:256] for n in range(2)] for i in range(5))
        geT = [self.units("arena", 22 + n, 1)[:, 0, 0:2 * GB].rearrange("p (m x) -> p m x", m=2) for n in range(2)]
        names = ("arranged", "product", "chain", "argument", "tanh_ready", "gelu_ready", "turned", "turned_copied", "out_product")
        with self.phases.phase(*names) as (block, arranged, product, chain, argument, tanh_ready, gelu_ready, turned,
                                           turned_copied, out_product):
            @block.tensor
            def _(pe):
                for n in range(2):
                    pe.wait_ge(arranged, 4 * n + 4)
                    for j in range(16):
                        mm = nc.tensor.matmul(banks[n][0:GB, 0:256], z[n][:, j].rearrange("p g b -> p (g b)"), w1s[n][:, j, :],
                                              start=(j == 0), stop=(j == 15))
                    mm.then_inc(product, 1)
                for n in range(2):
                    pe.wait_ge(gelu_ready, n + 1)
                    for m in range(2):
                        mm = nc.tensor.transpose(banks[2 + n][:, m * GB:(m + 1) * GB], ge[n][:, m * P:(m + 1) * P], self.c("ident", GB, GB))
                    mm.then_inc(turned, 1)
                for n in range(2):
                    pe.wait_ge(turned_copied, n + 1)
                    for g in range(2):
                        for m in range(2):
                            w, blocks = w2s[n][:, m * HD:(m + 1) * HD], geT[n][:, m, g * NCMP:(g + 1) * NCMP]
                            if n == 0:
                                mm = nc.tensor.matmul(banks[4][g * HD:(g + 1) * HD, 0:NCMP], w, blocks, start=(m == 0), stop=(m == 1))
                            else:
                                mm = nc.tensor.matmul(banks[5][0:NCMP, g * HD:(g + 1) * HD], blocks, w, start=(m == 0), stop=(m == 1))
                    mm.then_inc(out_product, 1)

            @block.scalar
            def _(act):
                for n in range(2):
                    act.wait_ge(argument, n + 1)
                    nc.scalar.activation(th[n], act_in[n], ACT.Tanh, scale=GELU).then_inc(tanh_ready, 1)

            @block.vector
            def _(dve):
                v = nc.vector
                for n in range(2):
                    for g in range(2):
                        for half in range(2):
                            src = sources[n][g * HD:(g + 1) * HD, 16 * half:16 * (half + NCMP)].rearrange("p (b j) -> p j b", j=16)
                            pe_half = self.p2(pes[n], 16 * half, 16)[g * HD:(g + 1) * HD, :].unsqueeze(2).to_broadcast([HD, 16, NCMP])
                            v.tensor_tensor(z[n][half * HD:(half + 1) * HD, :, g, :], src, pe_half, ALU.add).then_inc(arranged, 1)
                for n in range(2):
                    k = 4 * n
                    dve.wait_ge(product, n + 1)
                    v.tensor_copy(hid[n], banks[n][0:GB, 0:256]).then_inc(chain, 1)
                    dve.wait_ge(chain, k + 1)
                    v.tensor_tensor(cube[n], hid[n], hid[n], ALU.mult).then_inc(chain, 1)
                    dve.wait_ge(chain, k + 2)
                    v.tensor_scalar(cube[n], cube[n], 0.044715, 1.0, ALU.mult, ALU.add).then_inc(chain, 1)
                    dve.wait_ge(chain, k + 3)
                    v.tensor_tensor(act_in[n], cube[n], hid[n], ALU.mult).then_inc(argument, 1)
                    dve.wait_ge(argument, n + 1)
                    v.tensor_scalar(cube[n], hid[n], 0.5, None, ALU.mult).then_inc(chain, 1)
                    dve.wait_ge(chain, k + 4)
                    dve.wait_ge(tanh_ready, n + 1)
                    v.scalar_tensor_tensor(ge[n], th[n], 1.0, cube[n], ALU.add, ALU.mult).then_inc(gelu_ready, 1)
                for n in range(2):
                    dve.wait_ge(turned, n + 1)
                    v.tensor_copy(geT[n], banks[2 + n][:, 0:2 * GB].rearrange("p (m x) -> p m x", m=2)).then_inc(turned_copied, 1)
                dve.wait_ge(out_product, 1)
                v.tensor_copy(out_k, banks[4][:, 0:NCMP])
                dve.wait_ge(out_product, 2)
                v.tensor_copy(out_v, banks[5][0:NCMP, 0:P])

    def nsa_gates(self, h, gates):
        nc, banks = self.nc, self.banks
        w = self.pj(17)[:, 0:KD * 24].rearrange("p (k c) -> p k c", c=24)
        with self.phases.phase("loaded", "product") as (block, loaded, product):
            @block.sync
            def _(sp):
                sp.dma_start(w, self.dram["w_gates"]).then_inc(loaded, 16)

            @block.tensor
            def _(pe):
                pe.wait_ge(loaded, 16)
                for i in range(NT):
                    for k in range(KD):
                        mm = nc.tensor.matmul(banks[0][:, i * 24:(i + 1) * 24], h[:, k, i * P:(i + 1) * P], w[:, k, :],
                                              start=(k == 0), stop=(k == KD - 1))
                mm.then_inc(product, 1)

            @block.scalar
            def _(act):
                act.wait_ge(product, 1)
                nc.scalar.activation(gates, banks[0][:, 0:NT * 24], ACT.Sigmoid)

    def nsa_layer(self):
        w_kv, b_in = ("w_kv", 0, KD), ("b_in", 0, KD)
        self.memory_kv(1, w_kv)
        at = 10 * (T + 1)
        by_token = lambda u: u.rearrange("p u t -> p (u t)").rearrange("p (j f) -> p j f", f=256)
        w1_k, w1_v = by_token(self.mix), by_token(self.units("ring", 0, 8))
        w2 = self.units("ring", 8, 1)[:, 0, 0:2 * P].rearrange("p (n f) -> p n f", f=P)
        kv = self.big[:, at:at + 6 * T].rearrange("p (n t) -> p n t", t=T)
        self.project(w_kv, 6, kv, norm=(self.x, self.p2("g_kv", 0, KD), False), prefetched=True,
                     beside=[(w1_k, self.dram["w_ck1"]), (w2[:, 0], self.dram["w_ck2"]), (w2[:, 1], self.dram["w_cv2"])])
        self.project(b_in, 8, self.proj[:, :, 1:T + 1], norm=(self.x, self.p2("g_mix", KD, KD), False),
                     beside=[(w1_v, self.dram["w_cv1"]), self.masks_load()])
        h = self.whole_source()
        gates_flat = self.small[:, 400:400 + NT * 24]
        self.nsa_gates(h, gates_flat)
        k_cmp, v_cmp = self.pj(9)[:, 0:NCMP], self.pj(9)[0:NCMP, 64:64 + P]
        self.compress([kv[:, 0, :], kv[:, 1, :]], ["pe_k", "pe_v"], [w1_k, w1_v], [w2[:, 0], w2[:, 1]], k_cmp, v_cmp)
        gate = lambda i, h, b: gates_flat[:, i * 24 + h * 3 + b:i * 24 + h * 3 + b + 1]
        flat = lambda w, f: self.units(*w).rearrange("p u t -> p (u t)").rearrange("p (n f) -> p n f", f=f)
        vs, vw = flat(("arena", 6, 1), P), flat(("arena", 7, 1), P)
        self.transposes(self.to_tokens([kv[:, 3, :]], vs) + self.to_tokens([kv[:, 5, :]], vw))
        out = flat(("arena", 8, 4), T)
        bias = self.units("arena", 12, 8)
        cmp_bias = self.units("arena", 20, 2).rearrange("p u t -> p (u t)")[:, 0:8 * 124].rearrange("p (h c) -> p h c", h=8)
        self.vector_phase(
            [lambda v, h=h, s=s: v.scalar_tensor_tensor(bias[:, h, :], self.c("dist", T), -8.0 * s, self.c("causal", T), ALU.mult, ALU.add)
             for h, s in enumerate(NSA_SLOPES)]
            + [lambda v, h=h, s=s: v.scalar_tensor_tensor(cmp_bias[:, h, :], self.c("cmp_dist", NT * NCMP), -8.0 * s,
                                                          self.c("cmp_mask", NT * NCMP), ALU.mult, ALU.add)
               for h, s in enumerate(NSA_SLOPES)])
        queries = self.units("arena", 22, 8)
        self.by_head([self.pj(c) for c in range(4)], queries)
        tiles = []
        for h in range(8):
            g = h // 4
            for i in range(NT):
                q, o = queries[:, 2 * (h % 4) + g, i * P:(i + 1) * P], out[:, i, h * HD:(h + 1) * HD]
                n = len(tiles)
                tiles.append(dict(q=q, k=k_cmp, bias=cmp_bias[:, h, i * NCMP:(i + 1) * NCMP], v=[v_cmp], at=HD * g,
                                  out=o, gate=gate(i, h, 0), may_be_empty=True))
                for b, kk, vv in ((1, kv[:, 2, :], vs), (2, kv[:, 4, :], vw)):
                    tiles.append(dict(q=q, k=kk[:, 0:(i + 1) * P], bias=bias[:, h, T - (i + 1) * P:T],
                                      v=[vv[:, j, :] for j in range(i + 1)], at=HD * g, out=o, gate=gate(i, h, b),
                                      add=True, after=n + b - 1))
        self.attention(tiles, HD ** -0.5)
        self.transposes(self.to_features(out, [self.mix[:, c, :] for c in range(4)]))
        self.memory_attention(4, out, [self.mix[:, 4 + c, :] for c in range(4)])
        self.add_to_residual(("b_out", 0, KD), 1, self.mixed_source(), 1.0, split=self.mix, then=("gu3", 2 * KF, KD),
                             next_gain=self.p2("g_ffn", KD, KD))
        self.conv_ffn(1, None)

    def store(self):
        nc = self.nc
        y, logm, rstd = self.units("arena", 0, KD), self.temps[:, 2, :], self.temps[:, 3, :]
        gain = self.p2("g_final", 0, KD)
        with self.phases.phase("summed", "logged", "rstd_ready", "normed", "written") as (
                block, summed, logged, rstd_ready, normed, written):
            @block.tensor
            def _(pe):
                nc.tensor.matmul(self.banks[7][:, :], self.c("ones", P), self.squares, start=True, stop=True).then_inc(summed, 1)

            @block.scalar
            def _(act):
                act.wait_ge(summed, 1)
                nc.scalar.activation(logm, self.banks[7][:, :], ACT.Ln, bias=self.c("eps6"), scale=1.0 / D).then_inc(logged, 1)
                act.wait_ge(logged, 1)
                nc.scalar.activation(rstd, logm, ACT.Exp, scale=-0.5).then_inc(rstd_ready, 1)

            @block.vector
            def _(dve):
                dve.wait_ge(rstd_ready, 1)
                for k in range(KD):
                    nc.vector.scalar_tensor_tensor(y[:, k, :], self.x[:, k, :], gain[:, k:k + 1], rstd,
                                                   ALU.mult, ALU.mult).then_inc(normed, 1)

            @block.sync
            def _(sp):
                for k in range(KD):
                    sp.wait_ge(normed, k + 1)
                    sp.dma_start(self.dram["out"][:, k, :], y[:, k, :]).then_inc(written, 16)
                sp.wait_ge(written, 16 * KD)


def build(nc, dram, parts=3):
    with ExitStack() as ctx:
        core = Core(nc, ctx, dram)
        core.load_start()
        with nc.Fori(0, 2) as layer:
            core.first_layer(layer)
            if core.phases.n % 2:
                core.pause()
        core.gla_layer()
        core.nsa_layer()
        core.store()


def feature_columns(v):
    return np.ascontiguousarray(v.reshape(-1, P).T)


def tiles_of(w, kc):
    n, k, m = w.shape
    t = w.reshape(n, k // (kc * P), kc, P, m // P, P).transpose(0, 4, 1, 3, 2, 5)
    return t.reshape(-1, P, kc * P)


def in_turn(a, b):
    return np.stack([tiles_of(a, KD), tiles_of(b, KD)], axis=1).reshape(-1, P, KD * P)


def layouts(i):
    two = lambda v: np.concatenate([v, v]).reshape(P, 1)
    par1 = []
    for l in range(2):
        cols = [feature_columns(i[n][l]) for n in ("norm_ffn1", "norm_mix", "norm_ffn2", "shift_mu", "rwkv_w0", "rwkv_a0",
                                                    "rwkv_k_k", "rwkv_k_a", "rwkv_r_k", "rwkv_ln_w", "rwkv_ln_b")]
        cols += [two(i["attn_q_norm"][l]), two(i["attn_k_norm"][l])]
        cols += [feature_columns(i[n][l]) for n in ("conv_dw_w", "conv_dw_b", "conv_ln_w", "conv_ln_b")]
        cols += [np.concatenate([i["rwkv_w2"][l], i["rwkv_a2"][l], i["rwkv_g2"][l]])]
        par1.append(np.concatenate(cols, axis=1))
    cols = [feature_columns(i[n]) for n in ("g_mix_2", "g_ffn_2", "g_mem_2", "conv_w_2", "conv_b_2", "a_b_alpha_2",
                                             "a_g_head_2", "g_kv_2", "g_final_2")]
    cols += [np.concatenate([i[n].T, i[n].T]) for n in ("pe_k_2", "pe_v_2")]
    a = i["a_w_in_2"]
    q, mq = i["b_w_in_2"][:, :, 0:512], i["b_w_in_2"][:, :, 536:1048]
    q = q.reshape(1, D, 2, 4, HD).transpose(0, 1, 3, 2, 4).reshape(1, D, 512)
    alr = a[0, :, 1536:1552].reshape(KD, P, 16).transpose(1, 0, 2).reshape(P, P)
    w_alpha = np.concatenate([i["a_w_alpha_2"][0]] * 8)
    halves = lambda w: w.reshape(2, P, HD).transpose(1, 0, 2).reshape(P, P)
    return {
        "consts": constants()[0],
        "masks": constants()[1],
        "x": i["x"][0].T.reshape(KD, P, T).transpose(1, 0, 2),
        "mem": i["mem_2"][0].T.reshape(KD, P, MEM_T).transpose(1, 0, 2),
        "par1": np.stack(par1),
        "par2": np.concatenate(cols, axis=1),
        "gu1": in_turn(i["ffn1_w_gate"], i["ffn1_w_up"]),
        "down1": tiles_of(i["ffn1_w_down"], KF // 2),
        "w_in": tiles_of(i["w_in"], KD),
        "w_out": tiles_of(i["w_out"], KD),
        "gu2": in_turn(i["ffn2_w_gate"], i["ffn2_w_up"]),
        "down2": tiles_of(i["ffn2_w_down"], KF // 2),
        "w_mem": tiles_of(i["w_mem_kv_2"], KD),
        "gu3": in_turn(i["w_up_2"][:, :, 0:FF], i["w_up_2"][:, :, FF:]),
        "down3": tiles_of(i["w_down_2"], KF // 2),
        "a_in": tiles_of(np.concatenate([a[:, :, 0:1536], a[:, :, 1552:]], axis=2), KD),
        "a_out": tiles_of(i["a_w_out_2"], KD),
        "gla_small": np.concatenate([alr, w_alpha], axis=1),
        "w_kv": tiles_of(i["w_kv_2"][None], KD),
        "w_ck1": i["w_ck1_2"].reshape(2, 16, HD, 256).transpose(0, 2, 1, 3).reshape(P, 16, 256),
        "w_ck2": halves(i["w_ck2_2"]),
        "w_cv1": i["w_cv1_2"].reshape(2, 16, HD, 256).transpose(0, 2, 1, 3).reshape(P, 16, 256),
        "w_cv2": halves(i["w_cv2_2"]),
        "w_gates": i["b_w_in_2"][0, :, 512:536].reshape(KD, P, 24).transpose(1, 0, 2),
        "b_in": tiles_of(np.concatenate([q, mq], axis=2), KD),
        "b_out": tiles_of(i["b_w_out_2"], KD),
    }


def kernel(**inputs):
    import concourse.bacc as bacc
    from concourse.bass_utils import run_bass_kernel_spmd

    nc = bacc.Bacc("TRN2", target_bir_lowering=False, num_devices=1)
    arrays = {n: np.ascontiguousarray(a) for n, a in layouts({n: np.asarray(v) for n, v in inputs.items()}).items()}
    dram = {n: nc.dram_tensor(f"in_{n}", a.shape, F32, kind="ExternalInput").ap() for n, a in arrays.items()}
    dram["out"] = nc.dram_tensor("out_x", (P, KD, T), F32, kind="ExternalOutput").ap()
    build(nc, dram)
    r = run_bass_kernel_spmd(nc, [{f"in_{n}": a for n, a in arrays.items()}], core_ids=[0])
    out = np.asarray(r.results[0]["out_x"])
    return out.transpose(2, 1, 0).reshape(1, T, D)
```
